# Optimizing a Trainium2 kernel written in Bass

```python
import jax, jax.numpy as jnp
from jax import lax
import numpy as np
import math

D_MODEL = 1024
BATCH = 1
SEQ = 256
DEPTH = 1

CHUNK = 64
N_MOD = 6
EPS = 1e-6

M_HEADS = 4
M_QK_DIM = 128
M_V_DIM = 256
M_QK_WIDTH = M_HEADS * M_QK_DIM
M_V_WIDTH = M_HEADS * M_V_DIM
CONV_WIDTH = 4

A_HEADS = 8
Q_LORA = 384
KV_LORA = 256
QK_NOPE = 128
QK_ROPE = 64
V_HEAD = 128
A_V_WIDTH = A_HEADS * V_HEAD
ROPE_THETA = 10000.0
Q_BLOCK = 128

N_BRANCHES = 2
IN_SIZES = (M_QK_WIDTH, M_QK_WIDTH, M_V_WIDTH, M_V_WIDTH, M_HEADS, M_HEADS,
            Q_LORA, KV_LORA, QK_ROPE, N_BRANCHES * D_MODEL)
D_IN = sum(IN_SIZES)
IN_SPLIT_POINTS = tuple(sum(IN_SIZES[:i + 1]) for i in range(len(IN_SIZES) - 1))

N_GROUPS = 4
EXPERTS_PER_GROUP = 8
N_EXPERTS = N_GROUPS * EXPERTS_PER_GROUP
TOP_K = 2
D_EXPERT = 256
MOE_BLOCK = 128


def rms_norm(x, g):
    xf = x.astype(jnp.float32)
    y = xf * lax.rsqrt(jnp.mean(xf * xf, axis=-1, keepdims=True) + EPS)
    return (y * g.astype(jnp.float32)).astype(x.dtype)

def modulate(h, shift, scale):
    return h * (1.0 + scale[:, None, :]) + shift[:, None, :]

def apply_rope(x, cos, sin):
    x1, x2 = jnp.split(x, 2, axis=-1)
    return jnp.concatenate([x1 * cos - x2 * sin, x1 * sin + x2 * cos], axis=-1)

def causal_depthwise_conv(x, w, b):
    C = x.shape[-1]
    y = lax.conv_general_dilated(x, w[:, None, :], window_strides=(1,),
                                 padding=((CONV_WIDTH - 1, 0),),
                                 dimension_numbers=('NWC', 'WIO', 'NWC'),
                                 feature_group_count=C)
    return y + b

def mlstm_chunkwise(q, k, v, log_i, log_f):
    B, S, NH, DQK = q.shape
    DV = v.shape[-1]
    nc = S // CHUNK

    def to_chunks(t):
        t = t.reshape(B, nc, CHUNK, NH, *t.shape[3:])
        return jnp.moveaxis(t, (1, 3), (0, 2))

    causal = jnp.tril(jnp.ones((CHUNK, CHUNK), dtype=bool))

    def step(carry, xs):
        C, n, m = carry
        qc, kc, vc, lic, lfc = xs
        b = jnp.cumsum(lfc, axis=-1)
        dmat = b[..., :, None] - b[..., None, :] + lic[..., None, :]
        dmat = jnp.where(causal, dmat, -jnp.inf)
        m_inter = b + m[..., None]
        m_t = jnp.maximum(jnp.max(dmat, axis=-1), m_inter)
        s = jnp.einsum('bhtd,bhsd->bhts', qc, kc) * jnp.exp(dmat - m_t[..., None])
        w_inter = jnp.exp(m_inter - m_t)
        num = (jnp.einsum('bhts,bhsv->bhtv', s, vc)
               + w_inter[..., None] * jnp.einsum('bhtd,bhvd->bhtv', qc, C))
        den = jnp.sum(s, axis=-1) + w_inter * jnp.einsum('bhtd,bhd->bht', qc, n)
        h = num / jnp.maximum(jnp.abs(den), jnp.exp(-m_t))[..., None]
        b_last = b[..., -1]
        a = b_last[..., None] - b + lic
        m_new = jnp.maximum(b_last + m, jnp.max(a, axis=-1))
        decay = jnp.exp(b_last + m - m_new)
        wk = jnp.exp(a - m_new[..., None])
        C_new = decay[..., None, None] * C + jnp.einsum('bhs,bhsv,bhsd->bhvd', wk, vc, kc)
        n_new = decay[..., None] * n + jnp.einsum('bhs,bhsd->bhd', wk, kc)
        return (C_new, n_new, m_new), h

    init = (jnp.zeros((B, NH, DV, DQK), jnp.float32),
            jnp.zeros((B, NH, DQK), jnp.float32),
            jnp.zeros((B, NH), jnp.float32))
    _, h = lax.scan(step, init, (to_chunks(q), to_chunks(k), to_chunks(v),
                                 to_chunks(log_i), to_chunks(log_f)))
    return jnp.moveaxis(h, (0, 2), (1, 3)).reshape(B, S, NH, DV)

def chunk_causal_mla_attention(q_nope, q_rope, k_nope, k_rope, v):
    B, S, H, _ = q_nope.shape
    nqb = S // Q_BLOCK
    key_chunk = jnp.arange(S) // CHUNK
    scale = (QK_NOPE + QK_ROPE) ** -0.5

    def to_blocks(t):
        return t.reshape(B, nqb, Q_BLOCK, *t.shape[2:]).swapaxes(0, 1)

    def one_block(args):
        qn, qr, blk = args
        s = (jnp.einsum('bqhd,bkhd->bhqk', qn, k_nope)
             + jnp.einsum('bqhr,bkr->bhqk', qr, k_rope)).astype(jnp.float32) * scale
        q_chunk = (blk * Q_BLOCK + jnp.arange(Q_BLOCK)) // CHUNK
        mask = key_chunk[None, :] <= q_chunk[:, None]
        s = jnp.where(mask, s, -jnp.inf)
        p = jax.nn.softmax(s, axis=-1).astype(v.dtype)
        return jnp.einsum('bhqk,bkhd->bqhd', p, v)

    out = lax.map(one_block, (to_blocks(q_nope), to_blocks(q_rope), jnp.arange(nqb)))
    return out.swapaxes(0, 1).reshape(B, S, H * V_HEAD)

def mixer_sublayer(h, cos, sin, w_in, conv_w, conv_b, igate_b, fgate_b, q_norm_g,
                   kv_norm_g, w_uq, w_ukv, w_branch_m, w_branch_a, w_out):
    B, S, _ = h.shape
    proj = h @ w_in
    (q_m, k_m, v_m, o_m, i_m, f_m, c_q, c_kv, k_r, gate_pre) = jnp.split(
        proj, IN_SPLIT_POINTS, axis=-1)

    qk = jax.nn.silu(causal_depthwise_conv(jnp.concatenate([q_m, k_m], axis=-1), conv_w, conv_b))
    q_m, k_m = jnp.split(qk.astype(jnp.float32), 2, axis=-1)
    q_m = q_m.reshape(B, S, M_HEADS, M_QK_DIM) * (M_QK_DIM ** -0.5)
    k_m = k_m.reshape(B, S, M_HEADS, M_QK_DIM)
    v_m = v_m.astype(jnp.float32).reshape(B, S, M_HEADS, M_V_DIM)
    log_i = (i_m + igate_b).astype(jnp.float32)
    log_f = jax.nn.log_sigmoid((f_m + fgate_b).astype(jnp.float32))
    y_m = mlstm_chunkwise(q_m, k_m, v_m, log_i, log_f).reshape(B, S, M_V_WIDTH).astype(h.dtype)
    y_m = jax.nn.sigmoid(o_m) * y_m

    q_a = (rms_norm(c_q, q_norm_g) @ w_uq).reshape(B, S, A_HEADS, QK_NOPE + QK_ROPE)
    q_nope = q_a[..., :QK_NOPE]
    q_rope = apply_rope(q_a[..., QK_NOPE:], cos[:, None, :], sin[:, None, :])
    kv = (rms_norm(c_kv, kv_norm_g) @ w_ukv).reshape(B, S, A_HEADS, QK_NOPE + V_HEAD)
    k_nope, v_a = kv[..., :QK_NOPE], kv[..., QK_NOPE:]
    k_rope = apply_rope(k_r, cos, sin)
    y_a = chunk_causal_mla_attention(q_nope, q_rope, k_nope, k_rope, v_a)

    g_m, g_a = jnp.split(jax.nn.sigmoid(gate_pre), 2, axis=-1)
    merged = g_m * (y_m @ w_branch_m) + g_a * (y_a @ w_branch_a)
    return merged @ w_out

def hierarchical_moe(h, w_group, b_group, w_router, b_router, w_gate, w_up, w_down):
    B, S, D = h.shape
    T = B * S
    ht = h.reshape(T, D)
    hf = ht.astype(jnp.float32)
    grp_probs = jax.nn.softmax(hf @ w_group.astype(jnp.float32) + b_group.astype(jnp.float32), axis=-1)
    grp = jnp.argmax(grp_probs, axis=-1)
    p_grp = jnp.take_along_axis(grp_probs, grp[:, None], axis=-1)[:, 0]
    e_logits = (hf @ w_router.astype(jnp.float32) + b_router.astype(jnp.float32)).reshape(
        T, N_GROUPS, EXPERTS_PER_GROUP)
    in_grp = jnp.take_along_axis(e_logits, grp[:, None, None], axis=1)[:, 0]
    top_p, top_e = lax.top_k(jax.nn.softmax(in_grp, axis=-1), TOP_K)
    weights = p_grp[:, None] * top_p / jnp.sum(top_p, axis=-1, keepdims=True)
    expert_id = grp[:, None] * EXPERTS_PER_GROUP + top_e

    n_assign = T * TOP_K
    flat_e = expert_id.reshape(-1).astype(jnp.int32)
    flat_t = jnp.repeat(jnp.arange(T, dtype=jnp.int32), TOP_K)
    flat_w = weights.reshape(-1)
    order = jnp.argsort(flat_e)
    se, st, sw = flat_e[order], flat_t[order], flat_w[order]
    counts = jnp.bincount(flat_e, length=N_EXPERTS)
    padded = (counts + MOE_BLOCK - 1) // MOE_BLOCK * MOE_BLOCK
    starts = jnp.cumsum(counts) - counts
    p_ends = jnp.cumsum(padded)
    p_starts = p_ends - padded
    dest = p_starts[se] + jnp.arange(n_assign, dtype=jnp.int32) - starts[se]
    cap = n_assign + N_EXPERTS * MOE_BLOCK
    n_blocks = cap // MOE_BLOCK
    slot_tok = jnp.zeros((cap,), jnp.int32).at[dest].set(st)
    slot_w = jnp.zeros((cap,), jnp.float32).at[dest].set(sw)
    blk_start = jnp.arange(n_blocks) * MOE_BLOCK
    blk_expert = jnp.minimum(jnp.sum(p_ends[None, :] <= blk_start[:, None], axis=1), N_EXPERTS - 1)
    xg = ht[slot_tok].reshape(n_blocks, MOE_BLOCK, D)

    def run_block(args):
        xb, e, wb = args
        a = jax.nn.silu(xb @ w_gate[e]) * (xb @ w_up[e])
        return (a @ w_down[e]) * wb[:, None].astype(xb.dtype)

    out = lax.map(run_block, (xg, blk_expert, slot_w.reshape(n_blocks, MOE_BLOCK)))
    y = jnp.zeros((T, D), h.dtype).at[slot_tok].add(out.reshape(cap, D))
    return y.reshape(B, S, D)

def first_inputs(seed: int = 0) -> dict:
    key = jax.random.key(seed)
    ks = jax.random.split(key, 26)
    f32 = jnp.float32

    def nrm(k, shape, scale):
        return jax.random.normal(k, shape, f32) * scale

    def gain(k, shape):
        return 1.0 + 0.02 * jax.random.normal(k, shape, f32)

    L, D = DEPTH, D_MODEL
    return {
        "x": nrm(ks[0], (BATCH, SEQ, D), 1.0),
        "c": nrm(ks[1], (BATCH, D), 1.0),
        "mod_w": nrm(ks[2], (L, D, N_MOD * D), 0.5 * D ** -0.5),
        "mod_b": nrm(ks[3], (L, N_MOD * D), 0.02),
        "norm1_g": gain(ks[4], (L, D)),
        "w_in": nrm(ks[5], (L, D, D_IN), D ** -0.5),
        "conv_w": nrm(ks[6], (L, CONV_WIDTH, 2 * M_QK_WIDTH), CONV_WIDTH ** -0.5),
        "conv_b": nrm(ks[7], (L, 2 * M_QK_WIDTH), 0.02),
        "igate_b": nrm(ks[8], (L, M_HEADS), 0.1),
        "fgate_b": 3.0 + nrm(ks[9], (L, M_HEADS), 0.5),
        "q_norm_g": gain(ks[10], (L, Q_LORA)),
        "kv_norm_g": gain(ks[11], (L, KV_LORA)),
        "w_uq": nrm(ks[12], (L, Q_LORA, A_HEADS * (QK_NOPE + QK_ROPE)), Q_LORA ** -0.5),
        "w_ukv": nrm(ks[13], (L, KV_LORA, A_HEADS * (QK_NOPE + V_HEAD)), KV_LORA ** -0.5),
        "w_branch_m": nrm(ks[14], (L, M_V_WIDTH, D), M_V_WIDTH ** -0.5),
        "w_branch_a": nrm(ks[15], (L, A_V_WIDTH, D), A_V_WIDTH ** -0.5),
        "w_out": nrm(ks[16], (L, D, D), D ** -0.5),
        "norm2_g": gain(ks[17], (L, D)),
        "w_group": nrm(ks[18], (L, D, N_GROUPS), D ** -0.5),
        "b_group": nrm(ks[19], (L, N_GROUPS), 0.01),
        "w_router": nrm(ks[20], (L, D, N_EXPERTS), D ** -0.5),
        "b_router": nrm(ks[21], (L, N_EXPERTS), 0.01),
        "w_expert_gate": nrm(ks[22], (L, N_EXPERTS, D, D_EXPERT), D ** -0.5),
        "w_expert_up": nrm(ks[23], (L, N_EXPERTS, D, D_EXPERT), D ** -0.5),
        "w_expert_down": nrm(ks[24], (L, N_EXPERTS, D_EXPERT, D), D_EXPERT ** -0.5),
        "final_norm_g": gain(ks[25], (D,)),
    }

def first_block(x, c, mod_w, mod_b, norm1_g, w_in, conv_w, conv_b, igate_b, fgate_b,
              q_norm_g, kv_norm_g, w_uq, w_ukv, w_branch_m, w_branch_a, w_out, norm2_g,
              w_group, b_group, w_router, b_router, w_expert_gate, w_expert_up,
              w_expert_down, final_norm_g):
    B, S, D = x.shape
    pos = jnp.arange(S, dtype=jnp.float32)
    inv_freq = 1.0 / (ROPE_THETA ** (jnp.arange(0, QK_ROPE, 2, dtype=jnp.float32) / QK_ROPE))
    ang = pos[:, None] * inv_freq[None, :]
    cos = jnp.cos(ang).astype(x.dtype)
    sin = jnp.sin(ang).astype(x.dtype)
    cond = jax.nn.silu(c)
    for l in range(DEPTH):
        mod = cond @ mod_w[l] + mod_b[l]
        shift1, scale1, gate1, shift2, scale2, gate2 = jnp.split(mod, N_MOD, axis=-1)
        h = modulate(rms_norm(x, norm1_g[l]), shift1, scale1)
        x = x + gate1[:, None, :] * mixer_sublayer(
            h, cos, sin, w_in[l], conv_w[l], conv_b[l], igate_b[l], fgate_b[l],
            q_norm_g[l], kv_norm_g[l], w_uq[l], w_ukv[l], w_branch_m[l], w_branch_a[l], w_out[l])
        h = modulate(rms_norm(x, norm2_g[l]), shift2, scale2)
        x = x + gate2[:, None, :] * hierarchical_moe(
            h, w_group[l], b_group[l], w_router[l], b_router[l],
            w_expert_gate[l], w_expert_up[l], w_expert_down[l])
    return rms_norm(x, final_norm_g)


HEAD_DIM = 64
BLOCK_Q = 128
RMS_EPS = 1e-6
NEG_INF = -1e30
TINY = 1e-30

FOX_HEADS = 4
FORGET_BIAS_INIT = 3.0
DIL_WINDOWS = (128, 512, 2048)
DIL_RATES = (1, 4, 16)
DIL_HEADS_PER_GROUP = 2
DIL_HEADS = DIL_HEADS_PER_GROUP * len(DIL_WINDOWS)
NSA_HEADS = 6
NSA_KV_GROUPS = 2
NSA_CMP_BLOCK = 32
NSA_CMP_STRIDE = 16
NSA_CMP_HIDDEN = 256
NSA_SEL_BLOCK = 64
NSA_SEL_TOPK = 8
NSA_WINDOW = 512
FORCE_SCORE = 1e6
ALIBI_HEADS = DIL_HEADS + NSA_HEADS
D_FF = 2816
CONV_WIDTH_2 = 3

FOX_W = FOX_HEADS * HEAD_DIM
DIL_W = DIL_HEADS * HEAD_DIM
NSA_W = NSA_HEADS * HEAD_DIM
NSA_KV_W = NSA_KV_GROUPS * HEAD_DIM
IN_SPLITS = (FOX_W, FOX_W, FOX_W, FOX_HEADS,
             DIL_W, DIL_W, DIL_W,
             NSA_W, NSA_KV_W, NSA_KV_W, NSA_KV_W, NSA_KV_W, NSA_KV_W, NSA_KV_W, NSA_HEADS * 3,
             3 * D_MODEL)
D_IN_2 = sum(IN_SPLITS)


def rms_norm_2(x, g):
    xf = x.astype(jnp.float32)
    y = xf * lax.rsqrt(jnp.mean(xf * xf, axis=-1, keepdims=True) + RMS_EPS)
    return (y * g.astype(jnp.float32)).astype(x.dtype)

def alibi_slopes(n):
    return jnp.exp2(-8.0 * jnp.arange(1, n + 1, dtype=jnp.float32) / n)

def masked_softmax(s, mask):
    s = jnp.where(mask, s, NEG_INF)
    m = jnp.max(s, axis=-1, keepdims=True)
    e = jnp.where(mask, jnp.exp(s - m), 0.0)
    l = jnp.maximum(jnp.sum(e, axis=-1, keepdims=True), TINY)
    return e / l, (m + jnp.log(l))[..., 0]

def fox_attention(q, k, v, f_logit):
    B_, S, H, dh = q.shape
    nb = S // BLOCK_Q
    scale = dh ** -0.5
    c = jnp.cumsum(jax.nn.log_sigmoid(f_logit.astype(jnp.float32)), axis=1)
    c = jnp.transpose(c, (0, 2, 1))
    q_blocks = q.reshape(B_, nb, BLOCK_Q, H, dh).transpose(1, 0, 2, 3, 4)
    c_blocks = c.reshape(B_, H, nb, BLOCK_Q).transpose(2, 0, 1, 3)
    kpos = jnp.arange(S)

    def body(args):
        qb, cb, i = args
        qpos = i * BLOCK_Q + jnp.arange(BLOCK_Q)
        s = jnp.einsum('bqhd,bkhd->bhqk', qb, k).astype(jnp.float32) * scale
        s = s + cb[..., :, None] - c[:, :, None, :]
        p, _ = masked_softmax(s, kpos[None, :] <= qpos[:, None])
        return jnp.einsum('bhqk,bkhd->bqhd', p.astype(v.dtype), v)

    out = lax.map(body, (q_blocks, c_blocks, jnp.arange(nb)))
    return out.transpose(1, 0, 2, 3, 4).reshape(B_, S, H * dh)

def dilated_attention(q, k, v, slopes):
    B_, S, H, dh = q.shape
    P = DIL_HEADS_PER_GROUP
    nb = S // BLOCK_Q
    scale = dh ** -0.5
    q_blocks = q.reshape(B_, nb, BLOCK_Q, H, dh).transpose(1, 0, 2, 3, 4)

    def body(args):
        qb, i = args
        qpos = i * BLOCK_Q + jnp.arange(BLOCK_Q)
        outs, lses = [], []
        for g, (w, r) in enumerate(zip(DIL_WINDOWS, DIL_RATES)):
            hs = slice(g * P, (g + 1) * P)
            offs = r * jnp.arange(w // r + 1)
            kidx = qpos[:, None] - offs[None, :]
            valid = kidx >= 0
            kidx = jnp.maximum(kidx, 0)
            kg = k[:, :, hs][:, kidx]
            vg = v[:, :, hs][:, kidx]
            s = jnp.einsum('bqhd,bqkhd->bhqk', qb[:, :, hs], kg).astype(jnp.float32) * scale
            s = s - slopes[hs][None, :, None, None] * offs.astype(jnp.float32)[None, None, None, :]
            p, lse = masked_softmax(s, valid[None, None])
            outs.append(jnp.einsum('bhqk,bqkhd->bqhd', p.astype(vg.dtype), vg))
            lses.append(lse)
        alpha = jax.nn.softmax(jnp.stack(lses, 0), axis=0)
        o = jnp.stack(outs, 0) * alpha.transpose(0, 1, 3, 2)[..., None].astype(qb.dtype)
        return o.transpose(1, 2, 0, 3, 4).reshape(B_, BLOCK_Q, H * dh)

    out = lax.map(body, (q_blocks, jnp.arange(nb)))
    return out.transpose(1, 0, 2, 3).reshape(B_, S, H * dh)

def compress_blocks(kv, pe, w1, w2):
    B_, S, G, dh = kv.shape
    n_cmp = (S - NSA_CMP_BLOCK) // NSA_CMP_STRIDE + 1
    idx = jnp.arange(n_cmp)[:, None] * NSA_CMP_STRIDE + jnp.arange(NSA_CMP_BLOCK)[None, :]
    blocks = kv[:, idx] + pe[None, None, :, None, :]
    flat = blocks.transpose(0, 1, 3, 2, 4).reshape(B_, n_cmp, G, NSA_CMP_BLOCK * dh)
    return jax.nn.gelu(flat @ w1) @ w2

def nsa_attention(q, k_cmp, v_cmp, k_sel, v_sel, k_win, v_win, gate_logits, slopes,
                  cmp_pe, k_w1, k_w2, v_w1, v_w2):
    B_, S, H, dh = q.shape
    G = NSA_KV_GROUPS
    R = H // G
    nb = S // BLOCK_Q
    scale = dh ** -0.5
    kc = compress_blocks(k_cmp, cmp_pe, k_w1, k_w2)
    vc = compress_blocks(v_cmp, cmp_pe, v_w1, v_w2)
    n_cmp = kc.shape[1]
    cmp_end = jnp.arange(n_cmp) * NSA_CMP_STRIDE + NSA_CMP_BLOCK - 1
    cmp_start = cmp_end - (NSA_CMP_BLOCK - 1)
    n_sel = S // NSA_SEL_BLOCK
    sel_idx = jnp.arange(n_sel)
    sel_start = sel_idx * NSA_SEL_BLOCK
    overlap = ((cmp_start[:, None] < sel_start[None, :] + NSA_SEL_BLOCK)
               & (cmp_end[:, None] >= sel_start[None, :])).astype(jnp.float32)
    top_k = min(NSA_SEL_TOPK, n_sel)
    n_tok = top_k * NSA_SEL_BLOCK
    slope = slopes.reshape(G, R)[None, :, :, None, None]
    ks_t = k_sel.transpose(0, 2, 1, 3)
    vs_t = v_sel.transpose(0, 2, 1, 3)
    pad = ((0, 0), (NSA_WINDOW, 0), (0, 0), (0, 0))
    kw_pad = jnp.pad(k_win, pad)
    vw_pad = jnp.pad(v_win, pad)
    gather = jax.vmap(jax.vmap(lambda t, ii: t[ii]))
    q_blocks = q.reshape(B_, nb, BLOCK_Q, G, R, dh).transpose(1, 0, 2, 3, 4, 5)
    g_blocks = jax.nn.sigmoid(gate_logits).reshape(B_, nb, BLOCK_Q, G, R, 3).transpose(1, 0, 2, 3, 4, 5)

    def body(args):
        qb, gb, i = args
        q0 = i * BLOCK_Q
        qpos = q0 + jnp.arange(BLOCK_Q)
        s = jnp.einsum('bqgrd,bcgd->bgrqc', qb, kc).astype(jnp.float32) * scale
        s = s - slope * (qpos[:, None] - cmp_end[None, :]).astype(jnp.float32)
        p_c, _ = masked_softmax(s, cmp_end[None, :] <= qpos[:, None])
        o_c = jnp.einsum('bgrqc,bcgd->bqgrd', p_c.astype(vc.dtype), vc)
        imp = jnp.einsum('bgrqc,cj->bgqj', p_c, overlap)
        qblk = qpos // NSA_SEL_BLOCK
        causal = sel_start[None, :] <= qpos[:, None]
        forced = ((sel_idx[None, :] == 0) | (sel_idx[None, :] == qblk[:, None])
                  | (sel_idx[None, :] == qblk[:, None] - 1))
        score = jnp.where(causal & forced, FORCE_SCORE, jnp.where(causal, imp, -1.0))
        _, blk = lax.top_k(score, top_k)
        blk_ok = blk * NSA_SEL_BLOCK <= qpos[None, None, :, None]
        tok = (blk[..., None] * NSA_SEL_BLOCK + jnp.arange(NSA_SEL_BLOCK)).reshape(B_, G, BLOCK_Q, n_tok)
        tok_ok = jnp.repeat(blk_ok, NSA_SEL_BLOCK, axis=-1) & (tok <= qpos[None, None, :, None])
        kg = gather(ks_t, tok)
        vg = gather(vs_t, tok)
        s = jnp.einsum('bqgrd,bgqtd->bgrqt', qb, kg).astype(jnp.float32) * scale
        s = s - slope * (qpos[None, None, :, None] - tok)[:, :, None].astype(jnp.float32)
        p_s, _ = masked_softmax(s, tok_ok[:, :, None])
        o_s = jnp.einsum('bgrqt,bgqtd->bqgrd', p_s.astype(vg.dtype), vg)
        kw = lax.dynamic_slice_in_dim(kw_pad, q0, NSA_WINDOW + BLOCK_Q, axis=1)
        vw = lax.dynamic_slice_in_dim(vw_pad, q0, NSA_WINDOW + BLOCK_Q, axis=1)
        kpos = q0 - NSA_WINDOW + jnp.arange(NSA_WINDOW + BLOCK_Q)
        diff = qpos[:, None] - kpos[None, :]
        mask_w = (kpos[None, :] >= 0) & (diff >= 0) & (diff < NSA_WINDOW)
        s = jnp.einsum('bqgrd,bkgd->bgrqk', qb, kw).astype(jnp.float32) * scale
        s = s - slope * diff.astype(jnp.float32)
        p_w, _ = masked_softmax(s, mask_w)
        o_w = jnp.einsum('bgrqk,bkgd->bqgrd', p_w.astype(vw.dtype), vw)
        gb = gb.astype(qb.dtype)
        o = gb[..., 0:1] * o_c + gb[..., 1:2] * o_s + gb[..., 2:3] * o_w
        return o.reshape(B_, BLOCK_Q, H * dh)

    out = lax.map(body, (q_blocks, g_blocks, jnp.arange(nb)))
    return out.transpose(1, 0, 2, 3).reshape(B_, S, H * dh)

def conv_ffn(h, w_up, conv_w, conv_b, w_down):
    a, b = jnp.split(h @ w_up, 2, axis=-1)
    a = lax.conv_general_dilated(a, conv_w.reshape(CONV_WIDTH_2, 1, D_FF), window_strides=(1,),
                                 padding=[(CONV_WIDTH_2 - 1, 0)],
                                 dimension_numbers=('NWC', 'WIO', 'NWC'),
                                 feature_group_count=D_FF) + conv_b
    return (jax.nn.gelu(a) * b) @ w_down

def second_inputs(seed: int = 0) -> dict:
    key = jax.random.key(seed)
    ks = jax.random.split(key, 20)
    f32 = jnp.float32

    def nrm(k, shape, scale):
        return jax.random.normal(k, shape, f32) * scale

    L = DEPTH
    fo = 3 * FOX_W
    b_in = nrm(ks[3], (L, D_IN_2), 0.02).at[:, fo:fo + FOX_HEADS].add(FORGET_BIAS_INIT)
    return {
        "x": nrm(ks[0], (BATCH, SEQ, D_MODEL), 1.0),
        "norm1_g": 1.0 + nrm(ks[1], (L, D_MODEL), 0.02),
        "w_in": nrm(ks[2], (L, D_MODEL, D_IN_2), D_MODEL ** -0.5),
        "b_in": b_in,
        "cmp_pe": nrm(ks[4], (L, NSA_CMP_BLOCK, HEAD_DIM), 0.02),
        "cmp_k_w1": nrm(ks[5], (L, NSA_CMP_BLOCK * HEAD_DIM, NSA_CMP_HIDDEN), (NSA_CMP_BLOCK * HEAD_DIM) ** -0.5),
        "cmp_k_w2": nrm(ks[6], (L, NSA_CMP_HIDDEN, HEAD_DIM), NSA_CMP_HIDDEN ** -0.5),
        "cmp_v_w1": nrm(ks[7], (L, NSA_CMP_BLOCK * HEAD_DIM, NSA_CMP_HIDDEN), (NSA_CMP_BLOCK * HEAD_DIM) ** -0.5),
        "cmp_v_w2": nrm(ks[8], (L, NSA_CMP_HIDDEN, HEAD_DIM), NSA_CMP_HIDDEN ** -0.5),
        "w_pa": nrm(ks[9], (L, FOX_W, D_MODEL), FOX_W ** -0.5),
        "w_pb": nrm(ks[10], (L, DIL_W, D_MODEL), DIL_W ** -0.5),
        "w_pc": nrm(ks[11], (L, NSA_W, D_MODEL), NSA_W ** -0.5),
        "w_o": nrm(ks[12], (L, D_MODEL, D_MODEL), D_MODEL ** -0.5),
        "norm2_g": 1.0 + nrm(ks[13], (L, D_MODEL), 0.02),
        "w_up": nrm(ks[14], (L, D_MODEL, 2 * D_FF), D_MODEL ** -0.5),
        "conv_w": nrm(ks[15], (L, CONV_WIDTH_2, D_FF), CONV_WIDTH_2 ** -0.5),
        "conv_b": nrm(ks[16], (L, D_FF), 0.02),
        "w_down": nrm(ks[17], (L, D_FF, D_MODEL), D_FF ** -0.5),
        "final_g": 1.0 + nrm(ks[18], (D_MODEL,), 0.02),
    }

def second_block(x, norm1_g, w_in, b_in, cmp_pe, cmp_k_w1, cmp_k_w2, cmp_v_w1, cmp_v_w2,
              w_pa, w_pb, w_pc, w_o, norm2_g, w_up, conv_w, conv_b, w_down, final_g):
    B_, S, D = x.shape
    dh = HEAD_DIM
    G = NSA_KV_GROUPS
    slopes = alibi_slopes(ALIBI_HEADS)
    dil_slopes = slopes[0::2]
    nsa_slopes = slopes[1::2]
    split_at = np.cumsum(IN_SPLITS)[:-1].tolist()
    for l in range(DEPTH):
        h = rms_norm_2(x, norm1_g[l])
        proj = h @ w_in[l] + b_in[l]
        (qa, ka, va, fa, qb, kb, vb, qc, kc_, vc_, ksl, vsl, kwn, vwn, gc, gates) = jnp.split(proj, split_at, axis=-1)
        y_a = fox_attention(qa.reshape(B_, S, FOX_HEADS, dh), ka.reshape(B_, S, FOX_HEADS, dh),
                            va.reshape(B_, S, FOX_HEADS, dh), fa)
        y_b = dilated_attention(qb.reshape(B_, S, DIL_HEADS, dh), kb.reshape(B_, S, DIL_HEADS, dh),
                                vb.reshape(B_, S, DIL_HEADS, dh), dil_slopes)
        y_c = nsa_attention(qc.reshape(B_, S, NSA_HEADS, dh),
                            kc_.reshape(B_, S, G, dh), vc_.reshape(B_, S, G, dh),
                            ksl.reshape(B_, S, G, dh), vsl.reshape(B_, S, G, dh),
                            kwn.reshape(B_, S, G, dh), vwn.reshape(B_, S, G, dh),
                            gc.reshape(B_, S, NSA_HEADS, 3), nsa_slopes,
                            cmp_pe[l], cmp_k_w1[l], cmp_k_w2[l], cmp_v_w1[l], cmp_v_w2[l])
        g = jax.nn.sigmoid(gates).reshape(B_, S, 3, D)
        merged = (g[:, :, 0] * (y_a @ w_pa[l]) + g[:, :, 1] * (y_b @ w_pb[l])
                  + g[:, :, 2] * (y_c @ w_pc[l]))
        x = x + merged @ w_o[l]
        x = x + conv_ffn(rms_norm_2(x, norm2_g[l]), w_up[l], conv_w[l], conv_b[l], w_down[l])
    return rms_norm_2(x, final_g)


def setup_inputs(seed=0):
    out = dict(first_inputs(seed))
    for name, value in second_inputs(seed + 1).items():
        if name != "x":
            out[name + "_2"] = value
    return out


def reference(
    x, c, mod_w, mod_b, norm1_g, w_in, conv_w, conv_b, igate_b, fgate_b, q_norm_g, kv_norm_g,
    w_uq, w_ukv, w_branch_m, w_branch_a, w_out, norm2_g, w_group, b_group, w_router, b_router,
    w_expert_gate, w_expert_up, w_expert_down, final_norm_g, norm1_g_2, w_in_2, b_in_2,
    cmp_pe_2, cmp_k_w1_2, cmp_k_w2_2, cmp_v_w1_2, cmp_v_w2_2, w_pa_2, w_pb_2, w_pc_2, w_o_2,
    norm2_g_2, w_up_2, conv_w_2, conv_b_2, w_down_2, final_g_2,
):
    x = first_block(
        x, c, mod_w, mod_b, norm1_g, w_in, conv_w, conv_b, igate_b, fgate_b, q_norm_g,
        kv_norm_g, w_uq, w_ukv, w_branch_m, w_branch_a, w_out, norm2_g, w_group, b_group,
        w_router, b_router, w_expert_gate, w_expert_up, w_expert_down, final_norm_g,
    )
    return second_block(
        x, norm1_g_2, w_in_2, b_in_2, cmp_pe_2, cmp_k_w1_2, cmp_k_w2_2, cmp_v_w1_2, cmp_v_w2_2,
        w_pa_2, w_pb_2, w_pc_2, w_o_2, norm2_g_2, w_up_2, conv_w_2, conv_b_2, w_down_2,
        final_g_2,
    )


_drawn_inputs = setup_inputs


def setup_inputs(seed=0):
    import zlib

    import numpy as np

    out = dict(_drawn_inputs(seed))
    spreads = {}
    factors = {'mod_b': 3.111,
     'norm1_g': 8.0,
     'conv_b': 8.0,
     'igate_b': 8.0,
     'fgate_b': 6.259,
     'q_norm_g': 8.0,
     'kv_norm_g': 8.0,
     'norm2_g': 5.02,
     'b_group': 8.0,
     'b_router': 8.0,
     'norm1_g_2': 6.038,
     'cmp_pe_2': 8.0,
     'norm2_g_2': 3.609,
     'conv_b_2': 5.184,
     'final_g_2': 2.786}
    for name, (base, spread) in spreads.items():
        noise = np.random.default_rng([zlib.crc32(name.encode()), seed]).standard_normal(out[name].shape)
        drawn = base * np.exp(spread * noise) if base else spread * noise
        out[name] = __import__('jax').numpy.asarray(drawn.astype(out[name].dtype))
    for name, factor in factors.items():
        out[name] = (out[name] * factor).astype(out[name].dtype)
    return out
```

```python
from contextlib import ExitStack

import numpy as np

import concourse.bass as bass
from concourse import mybir

F32 = mybir.dt.float32
BF16 = mybir.dt.bfloat16
ALU = mybir.AluOpType
ACT = mybir.ActivationFunctionType
AX = mybir.AxisListType

GELU = 0.7978845608028654
P = 128
RAW = 648
T, D = 256, 1024
NT, KD = T // P, D // P
EPS = 1e-6
NEG = -1e30
TINY = 1e-30
MH, MQK, MV = 4, 128, 256
AH, QL, KVL, NOPE, ROPE, VH = 8, 384, 256, 128, 64, 128
CONV = 4
NG, EG, NE, DE = 4, 8, 32, 256
HD = 64
FOXH, DILH, NSAH, KVG = 4, 6, 6, 2
DILW, DILR = (128, 512, 2048), (1, 4, 16)
CB, CS, CH = 32, 16, 256
NC = (T - CB) // CS + 1
DFF, FB = 2816, 2816 // 128
FP = FB // 2

SPAN = P + T


def columns(sizes):
    at, out = 0, {}
    for name, n in sizes:
        out[name] = (at, at + n)
        at += n
    return out, at


CONST, NCONST = columns([
    ("ident", P), ("ones", P), ("tri", P), ("cos", T), ("sin", T), ("chunk", SPAN), ("causal", SPAN),
    ("dist", SPAN), ("dil", 3 * SPAN), ("cbias", NT * NSAH * NC), ("cmask", NT * NSAH * NC), ("rank4", NG), ("rank8", EG)])
VEC, NVEC = columns([
    ("c", KD), ("mod1", 16), ("mod2", 16), ("g1", KD), ("g2", KD), ("g3", KD), ("g4", KD), ("convw", 8 * CONV),
    ("convb", 8), ("qg", 3), ("kvg", 2), ("ib", 1), ("fb", 1), ("b2f", 17), ("fab", 1), ("conv2", FB * 4),
    ("pe", CB // 2), ("w2k", 2 * HD), ("w2v", 2 * HD), ("router", KD * (NG + NE))])
ROW, NROW = columns([("gate1", D), ("gate2", D), ("final1", D), ("final2", D), ("brouter", NG + NE),
                     ("b2v", 512), ("b2vb", 384), ("b2gc", 3 * NSAH), ("b2g", 3 * D)])

LOADS = [("cq", KD, QL + 2 * MH), ("ckr", KD, KVL + P), ("qk0", KD, 512), ("qk1", KD, 512), ("v0", KD, 512),
         ("v1", KD, 512), ("uqn", 3, 1024), ("uqr", 3, 512), ("ukv", 2, 2048), ("o0", KD, 512), ("o1", KD, 512),
         ("g0", KD, 512), ("g1", KD, 512), ("g2", KD, 512), ("g3", KD, 512),
         ("bm0", KD, 512), ("bm1", KD, 512), ("ba0", KD, 512), ("ba1", KD, 512), ("out0", KD, 512), ("out1", KD, 512)]
LOADS2 = [("fox", KD, 512), ("dilq", KD, 384), ("dilk", KD, 384), ("nsaq", KD, 384), ("kcvw", KD, 256),
          ("kk", KD, 256 + 3 * NSAH + FOXH), ("vv", KD, 512), ("vb", KD, 384), ("ck", 16, CH), ("cv", 16, CH),
          ("h0", KD, 512), ("h1", KD, 512), ("h2", KD, 512), ("h3", KD, 512), ("h4", KD, 512), ("h5", KD, 512),
          ("pa0", 2, 512), ("pa1", 2, 512), ("pb0", 3, 512), ("pb1", 3, 512), ("pc0", 3, 512), ("pc1", 3, 512),
          ("wo0", KD, 512), ("wo1", KD, 512)]
SLOT = max(c * n for _, c, n in LOADS + LOADS2)
BIG = 19300
GU, DN = 2 * KD * DE, 2 * D


class Chain:

    def __init__(self, eng, sem):
        self.eng, self.sem, self.n, self.loop = eng, sem, 0, None

    def __call__(self, ins):
        self.n += 1
        ins.then_inc(self.sem, 1)
        self.eng.wait_ge(self.sem, self.n if self.loop is None else self.loop + self.n)

    def start(self, i, per):
        self.loop, self.per = i * per, per

    def end(self, trips):
        self.n += self.per * (trips - 1)
        self.loop = None


def units():
    out = [("fox", (h,)) for h in range(FOXH)]
    out += [("dil", tuple(2 * g + p for g in range(3))) for p in range(2)]
    for h in range(NSAH):
        out += [("sel", (h,)), ("win", (h,))]
    return out


UNITS1 = [("mla", (h,)) for h in range(AH)]
UNITS2 = units()
DIL_SLOPE = [2.0 ** (-8.0 * (2 * h + 1) / 12) for h in range(DILH)]
NSA_SLOPE = [2.0 ** (-8.0 * (2 * h + 2) / 12) for h in range(NSAH)]


def build(nc, x, consts, vecs, rows, mod, wa, experts, wb, ffn, out):
    with ExitStack() as ctx:
        def sb(name, *shape, dt=F32):
            return ctx.enter_context(nc.sbuf_tensor(name, [P, *shape], dt))

        def sem(name):
            return ctx.enter_context(nc.semaphore(name))

        ring = sb("ring", 2, SLOT)
        dring = sb("dring", 2, DN)
        cst = sb("cst", NCONST)
        vec = sb("vec", NVEC)
        xs = sb("xs", NT, D)
        hn = sb("hn", NT, D)
        hT = sb("hT", KD, T)
        gateb = sb("gateb", 2, D)
        modT = sb("modT", 48)
        finalb = sb("finalb", D)
        small = sb("small", 512)
        att = sb("att", 2, 3, SPAN)
        pT = sb("pT", 3, SPAN)
        zero = sb("zero", 512, dt=BF16)
        big = sb("big", BIG)

        def const(name, a=0, b=None):
            lo, hi = CONST[name]
            return cst[:, lo + a:(hi if b is None else lo + b)]

        def v(name, a=0, b=None):
            lo, hi = VEC[name]
            return vec[:, lo + a:(hi if b is None else lo + b)]

        def row(name, a=0, b=None):
            lo, hi = ROW[name]
            return rows[0:1, lo + a:(hi if b is None else lo + b)].partition_broadcast(P)

        ident = const("ident")
        ones = const("ones")

        place = {}

        def part(name, at, *shape):
            n = int(np.prod(shape))
            place[name] = (at, at + n)
            assert at + n <= BIG, name
            ap = big[:, at:at + n]
            if len(shape) == 2:
                return ap.rearrange("p (a b) -> p a b", a=shape[0])
            if len(shape) == 3:
                return ap.rearrange("p (a b c) -> p a b c", a=shape[0], b=shape[1])
            return ap

        def after(name):
            return place[name][1]

        qkT = part("qkT", 0, 8, T)
        vaug = part("vaug", after("qkT"), NT, MH, MV + 1)
        og = part("og", after("vaug"), NT, D)
        qnT = part("qnT", after("og"), AH, T)
        qrT = part("qrT", after("qnT"), AH // 2, T)
        knT = part("knT", after("qrT"), AH, T)
        krT = part("krT", after("knT"), T)
        va = part("va", after("krT"), NT, D)
        ya = part("ya", after("va"), KD, T)
        wmem = part("wmem", after("ya"), 2 * SPAN)
        mpart = part("mpart", after("wmem"), 2, 512)
        lst = part("lst", after("wmem"), 8, T)
        ym = part("ym", place["qkT"][0], KD, T)
        merged = part("merged", place["va"][0], NT, D)
        mtile = [part("mtile0", place["qnT"][0], KD, 512), part("mtile1", place["qnT"][0] + KD * 512, KD, 512)]
        assert after("mtile1") <= after("ya")
        gates = dring[:, :, :].rearrange("p a b -> p (a b)").rearrange("p (t n) -> p t n", t=NT)
        dflat = dring[:, :, :].rearrange("p a b -> p (a b)")
        raw = dflat[:, 0:NT * RAW].rearrange("p (t n) -> p t n", t=NT)
        cT = dflat[:, NT * RAW:NT * RAW + 5 * T].rearrange("p (c n) -> p c n", c=5)
        mergedT = hT
        wb_bc = part("wb_bc", 0, NE, T)
        aT = part("aT", after("wb_bc"), 2, 2, T)
        tmp = part("tmp", after("aT"), 2, 2 * T)
        rt = part("rt", after("tmp"), 1024)
        fmT = part("fmT", 0, 17, T)
        kvc = part("kvc", after("fmT"), 2, CB // 2, KVG * NC)
        tv = part("tv", after("kvc"), NT, 512)
        tvb = part("tvb", after("tv"), NT, 384)
        gc = part("gc", after("tvb"), NT, 3 * NSAH)
        g2 = part("g2", after("gc"), NT, 3 * D)
        hidT = part("hidT", after("g2"), 2, 2, KVG * NC)
        kcT = part("kcT", after("hidT"), KVG * NC)
        vc = part("vc", after("kcT"), KVG, HD)
        pcm = part("pcm", after("vc"), NT * NSAH, NC)
        fox = part("fox", after("pcm"), 4, T)
        gel = part("gel", after("fox"), 4, 2, 2 * KVG * NC)
        bias2 = part("bias2", after("gel"), NROW - ROW["b2v"][0])
        yT2 = part("yT2", place["bias2"][0], 8, T)
        pcT = part("pcT", after("yT2"), NSAH, T)
        merged2 = part("merged2", place["fmT"][0], NT, D)
        faT = part("faT", 0, 2, 2, T)
        ft = part("ft", after("faT"), 5, 2 * T)

        ps = ctx.enter_context(nc.psum_tensor("ps", [P, 8, 512], F32))

        s_const, s_x, s_brow, s_final1, s_final2, s_bias2, s_out = (
            sem(n) for n in ("s_const", "s_x", "s_brow", "s_final1", "s_final2", "s_bias2", "s_out"))
        s_ring = [sem("s_ring0"), sem("s_ring1")]
        s_gu = [sem("s_gu0"), sem("s_gu1")]
        s_dn = [sem("s_dn0"), sem("s_dn1")]
        s_mt = [sem("s_mt0"), sem("s_mt1")]
        s_dnp = sem("s_dnp")
        c_dve, c_act, c_pool = sem("c_dve"), sem("c_act"), sem("c_pool")
        s_cond, s_condt, s_mpart, s_msum, s_mev = (
            sem(n) for n in ("s_cond", "s_condt", "s_mpart", "s_msum", "s_mev"))
        s_ss, s_ms, s_rstd, s_hn, s_tr, s_hTv, s_hTa = (
            sem(n) for n in ("s_ss", "s_ms", "s_rstd", "s_hn", "s_tr", "s_hTv", "s_hTa"))
        s_grp, s_gv, s_ga = sem("s_grp"), sem("s_gv"), sem("s_ga")
        s_conv, s_convt = sem("s_conv"), sem("s_convt")
        s_css, s_cms, s_crs, s_cn, s_ctr, s_cT = (sem(n) for n in ("s_css", "s_cms", "s_crs", "s_cn", "s_ctr", "s_cT"))
        s_lf, s_le, s_scan, s_em, s_gt, s_gte = (sem(n) for n in ("s_lf", "s_le", "s_scan", "s_em", "s_gt", "s_gte"))
        s_mS, s_mw, s_mexp, s_mst, s_mnum, s_mr, s_mh, s_my = (
            sem(n) for n in ("s_mS", "s_mw", "s_mexp", "s_mst", "s_mnum", "s_mr", "s_mh", "s_my"))
        s_sc, s_sfree, s_nm, s_exp, s_p, s_pt, s_pTc, s_pv, s_y = (
            sem(n) for n in ("s_sc", "s_sfree", "s_nm", "s_exp", "s_p", "s_pt", "s_pTc", "s_pv", "s_y"))
        s_yt, s_ymT = sem("s_yt"), sem("s_ymT")
        s_br, s_mrg, s_mt2, s_mT, s_pr, s_x1 = (sem(n) for n in ("s_br", "s_mrg", "s_mt2", "s_mT", "s_pr", "s_x1"))
        s_lg, s_re, s_rx, s_w32, s_wt, s_wtc, s_wbp, s_wba, s_wbv = (
            sem(n) for n in ("s_lg", "s_re", "s_rx", "s_w32", "s_wt", "s_wtc", "s_wbp", "s_wba", "s_wbv"))
        s_gup, s_th, s_aT, s_a2 = (sem(n) for n in ("s_gup", "s_th", "s_aT", "s_a2"))
        s_xf, s_fss, s_fms, s_frs = (sem(n) for n in ("s_xf", "s_fss", "s_fms", "s_frs"))
        s_F, s_hid, s_hz, s_hu, s_hth, s_hg, s_kc, s_kce = (
            sem(n) for n in ("s_F", "s_hid", "s_hz", "s_hu", "s_hth", "s_hg", "s_kc", "s_kce"))
        s_cs, s_ce, s_cx, s_cp, s_cpt, s_cpc = (sem(n) for n in ("s_cs", "s_ce", "s_cx", "s_cp", "s_cpt", "s_cpc"))
        s_fl, s_fsc, s_zero = sem("s_fl"), sem("s_fsc"), sem("s_zero")
        s_ggu, s_fsq, s_fz, s_fth, s_ffn = (sem(n) for n in ("s_ggu", "s_fsq", "s_fz", "s_fth", "s_ffn"))
        s_fe, s_gct = sem("s_fe"), sem("s_gct")

        ALL = LOADS + LOADS2
        NL = {name: n for n, (name, _, _) in enumerate(ALL)}
        offs = {}
        for stream in (LOADS, LOADS2):
            at = 0
            for name, c, n in stream:
                offs[name] = (at, c * n)
                at += c * n

        def wtile(name):
            n = NL[name]
            _, c, m = ALL[n]
            return ring[:, n % 2, 0:c * m].rearrange("p (c n) -> p c n", c=c)

        def landed(eng, name):
            n = NL[name]
            eng.wait_ge(s_ring[n % 2], 16 * (n // 2 + 1))

        GROUPS = [("misc0", "a"), ("misc1", "a"), ("ckv", "a"), ("kr", "v"), ("qk0", "v"), ("qk1", "v"), ("qk2", "v"),
                  ("qk3", "v"), ("v0", "a"), ("v1", "a"), ("v2", "a"), ("v3", "a")]
        GROUPS += [(f"qn{i}", "a") for i in range(4)] + [("qr0", "v"), ("qr1", "v")]
        GROUPS += [(f"kn{i}", "a") for i in range(4)] + [(f"va{i}", "v") for i in range(4)]
        GROUPS += [(f"o{i}", "a") for i in range(4)] + [(f"g{i}", "a") for i in range(8)]
        NG1 = len(GROUPS)
        GROUPS += [("fox0", "v"), ("fox1", "a"), ("dil0", "v"), ("dil1", "v"), ("dil2", "a"), ("dil3", "a"),
                   ("nsa0", "v"), ("nsa1", "v"), ("kcv", "v"), ("kk", "a"), ("gf", "v"), ("vv0", "v"), ("vv1", "v"),
                   ("vb0", "v"), ("vb1", "v")]
        GROUPS += [(f"h{i}", "v") for i in range(12)]
        VGROUPS = sum(1 for g in GROUPS if g[1] == "v")
        GI = {name: n for n, (name, _) in enumerate(GROUPS)}

        def bank(name):
            return ps[:, GI[name] % 4, :]

        def emptied(eng, n):
            who = GROUPS[n][1]
            count = sum(1 for g in GROUPS[:n + 1] if g[1] == who)
            eng.wait_ge(s_ga if who == "a" else s_gv, count)

        def grouped(eng, name):
            eng.wait_ge(s_grp, GI[name] + 1)

        USED = {"cq": "misc1", "ckr": "kr", "qk0": "qk1", "qk1": "qk3", "v0": "v1", "v1": "v3", "uqn": "qn3",
                "uqr": "qr1", "ukv": "va3", "o0": "o1", "o1": "o3", "fox": "fox1", "dilq": "dil1", "dilk": "dil3",
                "nsaq": "nsa1", "kcvw": "kcv", "kk": "gf", "vv": "vv1", "vb": "vb1"}
        USED.update({f"g{q}": f"g{2 * q + 1}" for q in range(4)})
        USED.update({f"h{q}": f"h{2 * q + 1}" for q in range(6)})
        USED = {name: (s_grp, GI[g] + 1) for name, g in USED.items()}
        for n, name in enumerate(("bm0", "bm1", "ba0", "ba1", "pa0", "pa1", "pb0", "pb1", "pc0", "pc1")):
            USED[name] = (s_br, 2 * (n + 1))
        for n, name in enumerate(("out0", "out1", "wo0", "wo1")):
            USED[name] = (s_pr, 2 * (n + 1))
        USED["ck"], USED["cv"] = (s_hid, 1), (s_hid, 2)

        def used(eng, n):
            eng.wait_ge(*USED[ALL[n][0]])

        DN2 = NE + 2

        NMOD = 12
        block = ctx.enter_context(nc.Block())

        @block.sync
        def _(sp):
            sp.dma_start(vec[:, :], vecs).then_inc(s_const, 16)
            sp.dma_start(cst[:, :], consts).then_inc(s_const, 16)

            def mod_tile(j):
                if j >= 2:
                    sp.wait_ge(s_mpart, j - 1)
                sp.dma_start(mtile[j % 2], mod[j].rearrange("p (c n) -> p c n", c=KD)).then_inc(s_mt[j % 2], 16)

            def load(name, stream):
                n = NL[name]
                if n >= 2:
                    used(sp, n - 2)
                at, size = offs[name]
                sp.dma_start(ring[:, n % 2, 0:size], stream[:, at:at + size]).then_inc(s_ring[n % 2], 16)

            mod_tile(0)
            mod_tile(1)
            sp.dma_start(xs[:, :, :], x.rearrange("b (t p) d -> p (b t) d", p=P)).then_inc(s_x, 16)
            sp.dma_start(gateb[:, 0, :], row("gate1")).then_inc(s_brow, 16)
            sp.dma_start(gateb[:, 1, :], row("gate2")).then_inc(s_brow, 16)
            mod_tile(2)
            mod_tile(3)
            load("cq", wa)
            load("ckr", wa)
            mod_tile(4)
            mod_tile(5)
            load("qk0", wa)
            mod_tile(6)
            load("qk1", wa)
            mod_tile(7)
            mod_tile(8)
            load("v0", wa)
            mod_tile(9)
            load("v1", wa)
            mod_tile(10)
            mod_tile(11)
            for name, _, _ in LOADS[6:]:
                load(name, wa)
            sp.dma_start(finalb[:, :], row("final1")).then_inc(s_final1, 16)
            sp.dma_start(small[:, 448:448 + 36], row("brouter")).then_inc(s_final1, 16)

            n0 = len(LOADS)
            for e in range(2):
                used(sp, n0 - 2 + e)
                sp.dma_start(ring[:, (n0 + e) % 2, 0:GU], experts[e, :, 0:GU]).then_inc(s_gu[e], 16)
                sp.dma_start(dring[:, e, :], experts[e, :, GU:GU + DN]).then_inc(s_dn[e], 16)
            with sp.Fori(0, NE // 2 - 1) as i:
                for b in range(2):
                    sp.wait_ge(s_gup, 2 * i + b + 1)
                    sp.dma_start(ring[:, (n0 + b) % 2, 0:GU],
                                 experts[bass.ds(2 * i + b + 2, 1), :, 0:GU].rearrange("a p n -> p (a n)")
                                 ).then_inc(s_gu[b], 16)
                    sp.wait_ge(s_dnp, 2 * i + b + 2)
                    sp.dma_start(dring[:, b, :],
                                 experts[bass.ds(2 * i + b + 2, 1), :, GU:GU + DN].rearrange("a p n -> p (a n)")
                                 ).then_inc(s_dn[b], 16)

            sp.wait_ge(s_gup, NE - 1)
            first = True
            for name, _, _ in LOADS2:
                n = NL[name]
                if n - n0 < 2:
                    sp.wait_ge(s_gup, NE - 1 + (n - n0))
                else:
                    used(sp, n - 2)
                at, size = offs[name]
                sp.dma_start(ring[:, n % 2, 0:size], wb[:, at:at + size]).then_inc(s_ring[n % 2], 16)
                if first:
                    sp.wait_ge(s_aT, NE)
                    sp.dma_start(bias2, rows[0:1, ROW["b2v"][0]:NROW].partition_broadcast(P)
                                 ).then_inc(s_bias2, 16)
                    first = False

            n1 = len(ALL)
            for f in range(2):
                used(sp, n1 - 2 + f)
                sp.dma_start(ring[:, (n1 + f) % 2, 0:GU], ffn[f, :, 0:GU]).then_inc(s_gu[f], 16)
                sp.dma_start(dring[:, f, :], ffn[f, :, GU:GU + DN]).then_inc(s_dn[f], 16)
            sp.wait_ge(s_xf, 2)
            sp.dma_start(finalb[:, :], row("final2")).then_inc(s_final2, 16)
            with sp.Fori(0, FP // 2 - 1) as i:
                for b in range(2):
                    sp.wait_ge(s_gup, NE + 2 * i + b + 1)
                    sp.dma_start(ring[:, (n1 + b) % 2, 0:GU],
                                 ffn[bass.ds(2 * i + b + 2, 1), :, 0:GU].rearrange("a p n -> p (a n)")
                                 ).then_inc(s_gu[b], 16)
                    sp.wait_ge(s_dnp, DN2 + 2 * i + b + 1)
                    sp.dma_start(dring[:, b, :],
                                 ffn[bass.ds(2 * i + b + 2, 1), :, GU:GU + DN].rearrange("a p n -> p (a n)")
                                 ).then_inc(s_dn[b], 16)
            sp.wait_ge(s_gup, NE + FP - 2)
            sp.dma_start(ring[:, n1 % 2, 0:GU], ffn[FP - 1, :, 0:GU]).then_inc(s_gu[0], 16)
            sp.wait_ge(s_dnp, DN2 + FP - 2)
            sp.dma_start(dring[:, 0, :], ffn[FP - 1, :, GU:GU + DN]).then_inc(s_dn[0], 16)

            sp.wait_ge(s_xf, 4)
            sp.dma_start(out.rearrange("b (t p) d -> p (b t) d", p=P), hn[:, :, :]).then_inc(s_out, 16)
            sp.wait_ge(s_out, 16)

        @block.tensor
        def _(pe):
            def group_start(name):
                n = GI[name]
                if n >= 4:
                    emptied(pe, n - 4)

            def mod_sum(j):
                pe.wait_ge(s_mpart, j + 1)
                if j in (4, 5, 6, 10, 11):
                    pe.wait_ge(s_mev, {4: 1, 5: 2, 6: 3, 10: 4, 11: 5}[j])
                pp = mpart[:, j % 2, :]
                if j in (4, 5, 10, 11):
                    mm = pe.matmul(ps[:, 7, :], ones, pp, start=True, stop=True)
                else:
                    col = 4 * j if j < 4 else 4 * (j - 6)
                    for i in range(4):
                        mm = pe.matmul(ps[:, 7, col + i:col + i + 1], pp[:, i * P:(i + 1) * P], ones[:, 0:1],
                                       start=True, stop=True)
                mm.then_inc(s_msum, 1)

            def turn_rows(k):
                pe.wait_ge(s_hn, 2 * (k + 1))
                for c in range(KD):
                    for t in range(NT):
                        mm = pe.transpose(ps[:, c // 2, (c % 2) * T + t * P:(c % 2) * T + (t + 1) * P],
                                          hn[:, t, c * P:(c + 1) * P], ident)
                    if c % 2:
                        mm.then_inc(s_tr, 1)

            def hT_ready(k):
                pe.wait_ge(s_hTv, 4 * (k + 1))
                pe.wait_ge(s_hTa, 4 * (k + 1))

            def feature(name, w, cols, src, nk, out0=0, m=P):
                b = bank(name)
                for j, c0 in enumerate(cols):
                    for c in range(nk):
                        mm = pe.matmul(b[0:m, out0 + j * T:out0 + (j + 1) * T], w[:, c, c0:c0 + m], src[:, c, :],
                                       start=(c == 0), stop=(c == nk - 1))
                return mm

            def token(b, t, w, c0, c1, src, nk, at=0):
                for c in range(nk):
                    mm = pe.matmul(b[:, at:at + c1 - c0], src[:, c, t * P:(t + 1) * P], w[:, c, c0:c1],
                                   start=(c == 0), stop=(c == nk - 1))
                return mm

            pe.wait_ge(s_const, 32)
            for j in range(4):
                mod_sum(j)
            turn_rows(0)
            hT_ready(0)
            landed(pe, "cq")
            w = wtile("cq")
            for t in range(NT):
                mm = token(bank(f"misc{t}"), t, w, 0, QL + 2 * MH, hT, KD).then_inc(s_grp, 1)
            landed(pe, "ckr")
            w = wtile("ckr")
            b = bank("ckv")
            for t in range(NT):
                mm = token(b, t, w, 0, KVL, hT, KD, at=t * KVL)
            mm.then_inc(s_grp, 1)
            feature("kr", w, [KVL], hT, KD).then_inc(s_grp, 1)
            for half in range(2):
                landed(pe, f"qk{half}")
                w = wtile(f"qk{half}")
                for i in range(2):
                    name = f"qk{2 * half + i}"
                    group_start(name)
                    mm = feature(name, w, [i * 256, i * 256 + P], hT, KD).then_inc(s_grp, 1)
                mod_sum(4 + 2 * half)
                mod_sum(5 + 2 * half)
            for half in range(2):
                landed(pe, f"v{half}")
                w = wtile(f"v{half}")
                for t in range(NT):
                    group_start(f"v{2 * half + t}")
                    mm = token(bank(f"v{2 * half + t}"), t, w, 0, 512, hT, KD).then_inc(s_grp, 1)
                mod_sum(8 + 2 * half)
                mod_sum(9 + 2 * half)
            pe.wait_ge(s_cn, 2)
            for c in range(5):
                for t in range(NT):
                    at = (c % 2) * T + t * P
                    src = raw[:, t, c * P:(c + 1) * P] if c < 3 else raw[:, t, 392 + (c - 3) * P:392 + (c - 2) * P]
                    pe.transpose(ps[:, 4 + c // 2, at:at + P], src, ident)
            for t in range(NT):
                pe.transpose(ps[0:MH, 6, T + t * P:T + (t + 1) * P], raw[:, t, QL:QL + MH], ident)
            pe.wait_ge(s_mev, 6)
            for t in range(NT):
                mm = pe.transpose(ps[0:MH, 7, t * P:(t + 1) * P], raw[:, t, QL + MH:QL + 2 * MH], ident)
            mm.then_inc(s_ctr, 1)
            pe.wait_ge(s_cT, 1)
            landed(pe, "uqn")
            w = wtile("uqn")
            for i in range(4):
                group_start(f"qn{i}")
                mm = feature(f"qn{i}", w, [2 * i * P, (2 * i + 1) * P], cT, 3).then_inc(s_grp, 1)
            landed(pe, "uqr")
            w = wtile("uqr")
            for i in range(2):
                group_start(f"qr{i}")
                mm = feature(f"qr{i}", w, [2 * i * P, (2 * i + 1) * P], cT, 3).then_inc(s_grp, 1)
            landed(pe, "ukv")
            w = wtile("ukv")
            for i in range(4):
                group_start(f"kn{i}")
                feature(f"kn{i}", w, [2 * i * P, (2 * i + 1) * P], cT[:, 3:5, :], 2).then_inc(s_grp, 1)
            for i in range(4):
                group_start(f"va{i}")
                mm = token(bank(f"va{i}"), i % 2, w, 1024 + 512 * (i // 2), 1536 + 512 * (i // 2), cT[:, 3:5, :], 2)
                mm.then_inc(s_grp, 1)
            for half in range(2):
                landed(pe, f"o{half}")
                w = wtile(f"o{half}")
                for t in range(NT):
                    group_start(f"o{2 * half + t}")
                    mm = token(bank(f"o{2 * half + t}"), t, w, 0, 512, hT, KD).then_inc(s_grp, 1)
            for q in range(4):
                landed(pe, f"g{q}")
                w = wtile(f"g{q}")
                for t in range(NT):
                    group_start(f"g{2 * q + t}")
                    mm = token(bank(f"g{2 * q + t}"), t, w, 0, 512, hT, KD).then_inc(s_grp, 1)
            pe.wait_ge(s_scan, 1)
            pe.wait_ge(s_em, 1)
            for t in range(NT):
                pe.transpose(ps[:, 4, t * MH:(t + 1) * MH], lst[0:MH, 2, t * P:(t + 1) * P], ident[0:MH, 0:MH])
                mm = pe.transpose(ps[:, 4, (2 + t) * MH:(3 + t) * MH], lst[0:MH, 5, t * P:(t + 1) * P],
                                  ident[0:MH, 0:MH])
            mm.then_inc(s_gt, 1)
            emptied(pe, NG1 - 1)
            emptied(pe, GI["va3"])

            def m_scores(h):
                if h >= 2:
                    pe.wait_ge(s_mst, h - 1)
                pe.matmul(ps[:, h % 2, 0:T], ident[0:MH, h:h + 1].to_broadcast([MH, P]), lst[0:MH, 4, :],
                          start=True, stop=True)
                pe.matmul(ps[:, 2 + h % 2, 0:T], qkT[:, 4 + h, 0:P], qkT[:, h, :], start=True, stop=True)
                pe.matmul(ps[:, 2 + h % 2, T:SPAN], qkT[:, 4 + h, P:T], qkT[:, h, P:T], start=True, stop=True
                          ).then_inc(s_mS, 1)

            def m_values(h):
                pe.wait_ge(s_mst, h + 1)
                if h >= 1:
                    pe.wait_ge(s_mh, 2 * h)
                w = wmem[:, (h % 2) * SPAN:(h % 2 + 1) * SPAN]
                pe.matmul(ps[:, 5, 0:MV + 1], w[:, 0:P], vaug[:, 0, h, :], start=True, stop=True)
                pe.matmul(ps[:, 6, 0:MV + 1], w[:, P:T], vaug[:, 0, h, :], start=True, stop=False)
                pe.matmul(ps[:, 6, 0:MV + 1], w[:, T:SPAN], vaug[:, 1, h, :], start=False, stop=True
                          ).then_inc(s_mnum, 1)

            pe.wait_ge(s_gte, 1)
            for h in range(MH + 1):
                if h < MH:
                    m_scores(h)
                if h >= 1:
                    m_values(h - 1)

            def attention(todo, set0, unit0, out0, scores, value, outputs, finished):
                at = []
                n = set0
                for _, heads in todo:
                    at.append(n)
                    n += len(heads)
                o = out0
                for u in range(len(todo) + 1):
                    if u < len(todo):
                        kind, heads = todo[u]
                        for g, h in enumerate(heads):
                            s = at[u] + g
                            if s - set0 >= 3:
                                pe.wait_ge(s_sfree, s - 2)
                            scores(ps[:, s % 3, 0:SPAN], kind, h).then_inc(s_sc, 1)
                    if u >= 1:
                        kind, heads = todo[u - 1]
                        pe.wait_ge(s_p, unit0 + u)
                        for g, h in enumerate(heads):
                            s = at[u - 1] + g
                            if s - set0 >= 3:
                                pe.wait_ge(s_pTc, s - 2)
                            src = att[:, (unit0 + u - 1) % 2, g, :]
                            b = ps[:, 3 + s % 3, :]
                            pe.transpose(b[:, 0:P], src[:, 0:P], ident)
                            pe.transpose(b[:, P:T], src[:, P:T], ident)
                            pe.transpose(b[:, T:SPAN], src[:, T:SPAN], ident).then_inc(s_pt, 1)
                        for g, h in enumerate(heads):
                            s = at[u - 1] + g
                            pe.wait_ge(s_pTc, s + 1)
                            lo, hi = outputs(kind, h)
                            first, last = finished(kind)
                            if first and o - out0 >= 2:
                                pe.wait_ge(s_y, o - 1)
                            dst = ps[lo:hi, 6 + o % 2, :]
                            if first and kind == "sel":
                                pe.matmul(dst[:, 0:T], vc[0:NC, h // 3, :], pcT[0:NC, h, :], start=True, stop=False,
                                          skip_group_check=True)
                            v0, v1 = value(kind, h)
                            pe.matmul(dst[:, 0:T], v0, pT[:, s % 3, 0:T], start=first and kind != "sel", stop=False,
                                      skip_group_check=True)
                            pe.matmul(dst[:, P:T], v1, pT[:, s % 3, T:SPAN], start=False, stop=last,
                                      skip_group_check=True).then_inc(s_pv, 1)
                            if last:
                                o += 1

            def scores1(b, kind, h):
                r = (h % 2) * ROPE
                for lo, q0, n in ((0, 0, P), (P, P, T)):
                    pe.matmul(b[:, lo:lo + n], qnT[:, h, q0:q0 + P], knT[:, h, 0:n], start=True, stop=False)
                    mm = pe.matmul(b[:, lo:lo + n], qrT[r:r + ROPE, h // 2, q0:q0 + P], krT[r:r + ROPE, 0:n],
                                   start=False, stop=True)
                return mm

            pe.wait_ge(s_mw, 2 * MH)
            pe.wait_ge(s_mh, 2 * MH)
            attention(UNITS1, 0, 0, 0, scores1,
                      lambda kind, h: (va[:, 0, h * VH:(h + 1) * VH], va[:, 1, h * VH:(h + 1) * VH]),
                      lambda kind, h: (0, P), lambda kind: (True, True))
            pe.wait_ge(s_my, 2 * MH)
            pe.wait_ge(s_sfree, AH)
            pe.wait_ge(s_pTc, AH)
            for c in range(KD):
                for t in range(NT):
                    mm = pe.transpose(ps[:, c // 2, (c % 2) * T + t * P:(c % 2) * T + (t + 1) * P],
                                      og[:, t, c * P:(c + 1) * P], ident)
                if c % 2:
                    mm.then_inc(s_yt, 1)
            pe.wait_ge(s_ymT, 4)
            pe.wait_ge(s_y, AH)
            for br, src in (("bm", ym), ("ba", ya)):
                for half in range(2):
                    landed(pe, f"{br}{half}")
                    w = wtile(f"{br}{half}")
                    for t in range(NT):
                        mm = token(ps[:, (4 if br == "ba" else 0) + 2 * half + t, :], t, w, 0, 512, src, KD
                                   ).then_inc(s_br, 1)

            def turn_merged(k):
                pe.wait_ge(s_mrg, 4 * (k + 1))
                for c in range(KD):
                    for t in range(NT):
                        mm = pe.transpose(ps[:, c // 2, (c % 2) * T + t * P:(c % 2) * T + (t + 1) * P],
                                          (merged if k == 0 else merged2)[:, t, c * P:(c + 1) * P], ident)
                    if c % 2:
                        mm.then_inc(s_mt2, 1)
                pe.wait_ge(s_mT, 4 * (k + 1))

            def project_out(k, name):
                for half in range(2):
                    landed(pe, f"{name}{half}")
                    w = wtile(f"{name}{half}")
                    for t in range(NT):
                        mm = token(ps[:, 4 + 2 * half + t, :], t, w, 0, 512, mergedT, KD).then_inc(s_pr, 1)

            turn_merged(0)
            project_out(0, "out")
            turn_rows(1)
            hT_ready(1)
            wr = v("router").rearrange("p (c n) -> p c n", c=KD)
            for t in range(NT):
                mm = token(ps[:, 0, :], t, wr, 0, NG + NE, hT, KD, at=t * (NG + NE))
            mm.then_inc(s_lg, 1)
            pe.wait_ge(s_w32, 1)
            for t in range(NT):
                mm = pe.transpose(ps[0:NE, 1, t * P:(t + 1) * P], rt[:, 256 + t * NE:256 + (t + 1) * NE], ident)
            mm.then_inc(s_wt, 1)
            pe.wait_ge(s_wtc, 1)
            wT = rt[0:NE, 384:384 + T]
            for i in range(NE // 2):
                if i >= 4:
                    pe.wait_ge(s_wbv if i % 2 else s_wba, i // 2 - 1)
                for j in range(2):
                    e = 2 * i + j
                    mm = pe.matmul(ps[:, 4 + i % 4, j * T:(j + 1) * T], ident[0:NE, e:e + 1].to_broadcast([NE, P]), wT,
                                   start=True, stop=True)
                mm.then_inc(s_wbp, 1)

            def open_sums():
                for b in range(4):
                    mm = pe.matmul(ps[:, b, :], zero[:, 0:P], zero[:, :], start=True, stop=False,
                                   skip_group_check=True)
                mm.then_inc(s_dnp, 1)

            def gate_up(slot, pb):
                w = ring[:, slot, 0:GU].rearrange("p (m c n) -> p m c n", m=2, c=KD)
                for m in range(2):
                    for f in range(2):
                        for c in range(KD):
                            mm = pe.matmul(ps[:, pb + m, f * T:(f + 1) * T], w[:, m, c, f * P:(f + 1) * P], hT[:, c, :],
                                           start=(c == 0), stop=(c == KD - 1))
                mm.then_inc(s_gup, 1)

            def down(slot, a):
                w = dring[:, slot, :].rearrange("p (f n) -> p f n", f=2)
                for f in range(2):
                    for t in range(NT):
                        for n in range(2):
                            mm = pe.matmul(ps[:, 2 * t + n, :], a[:, slot, f, t * P:(t + 1) * P],
                                           w[:, f, n * 512:(n + 1) * 512], start=False, stop=False,
                                           skip_group_check=True)
                mm.then_inc(s_dnp, 1)

            n0 = len(LOADS)
            pe.wait_ge(s_zero, 1)
            open_sums()
            pe.wait_ge(s_wba, NE // 4)
            pe.wait_ge(s_wbv, NE // 4)

            def stream(count0, total, slot0, a, s_read, read0):
                pairs = (total - 1) // 2
                pe.wait_ge(s_gu[0], 16 * (count0 // 2 + 1))
                gate_up(slot0, 4)

                def step(b, i):
                    nxt = 1 - b
                    pe.wait_ge(s_gu[nxt], (i + (count0 // 2 + 1 + b)) * 16)
                    if b == 0:
                        pe.wait_ge(s_read, 2 * i + read0)
                    else:
                        pe.wait_ge(s_read, 2 * i + read0 + 1)
                    gate_up((slot0 + nxt) % 2, 4 + 2 * nxt)
                    pe.wait_ge(s_aT, 2 * i + count0 + b + 1)
                    pe.wait_ge(s_dn[b], (i + (count0 // 2 + 1)) * 16)
                    down(b, a)

                with pe.Fori(0, pairs) as i:
                    step(0, i)
                    step(1, i)
                done = 2 * pairs
                if done < total - 1:
                    step(0, pairs)
                    done += 1
                b = done % 2
                pe.wait_ge(s_aT, count0 + total)
                pe.wait_ge(s_dn[b], (done // 2 + count0 // 2 + 1) * 16)
                down(b, a)

            stream(0, NE, n0 % 2, aT, s_a2, 1)

            turn_rows(2)
            hT_ready(2)

            def fm(name, load, cols):
                group_start(name)
                feature(name, wtile(load), cols, hT, KD).then_inc(s_grp, 1)

            for load, names in (("fox", ("fox0", "fox1")), ("dilq", ("dil0", "dil1")), ("dilk", ("dil2", "dil3")),
                                ("nsaq", ("nsa0", "nsa1")), ("kcvw", ("kcv",))):
                landed(pe, load)
                width = ALL[NL[load]][2]
                for j, name in enumerate(names):
                    fm(name, load, range(2 * P * j, min(2 * P * (j + 1), width), P))
            landed(pe, "kk")
            fm("kk", "kk", [0, P])
            group_start("gf")
            for t in range(NT):
                token(bank("gf"), t, wtile("kk"), 256, 256 + 3 * NSAH, hT, KD, at=t * 3 * NSAH)
            at = 256 + 3 * NSAH
            for c in range(KD):
                mm = pe.matmul(bank("gf")[0:FOXH, T:2 * T], wtile("kk")[:, c, at:at + FOXH], hT[:, c, :], start=(c == 0),
                               stop=(c == KD - 1))
            mm.then_inc(s_grp, 1)
            landed(pe, "vv")
            for t in range(NT):
                group_start(f"vv{t}")
                mm = token(bank(f"vv{t}"), t, wtile("vv"), 0, 512, hT, KD).then_inc(s_grp, 1)
            landed(pe, "vb")
            for t in range(NT):
                group_start(f"vb{t}")
                mm = token(bank(f"vb{t}"), t, wtile("vb"), 0, 384, hT, KD).then_inc(s_grp, 1)
            pe.wait_ge(s_F, 1)
            for i, name in enumerate(("ck", "cv")):
                landed(pe, name)
                w = wtile(name)
                for m in range(2):
                    for j in range(CB // 2):
                        mm = pe.matmul(ps[:, 4 + i, m * 30:(m + 1) * 30], w[:, j, m * P:(m + 1) * P], kvc[:, i, j, :],
                                       start=(j == 0), stop=(j == CB // 2 - 1))
                mm.then_inc(s_hid, 1)
            for q in range(6):
                landed(pe, f"h{q}")
                w = wtile(f"h{q}")
                for t in range(NT):
                    group_start(f"h{2 * q + t}")
                    mm = token(bank(f"h{2 * q + t}"), t, w, 0, 512, hT, KD).then_inc(s_grp, 1)
            pe.wait_ge(s_hg, 1)
            w2k = v("w2k").rearrange("p (c n) -> p c n", c=2)
            w2v = v("w2v").rearrange("p (c n) -> p c n", c=2)
            for g in range(KVG):
                for c in range(2):
                    pe.matmul(ps[g * HD:(g + 1) * HD, 6, 0:NC], w2k[:, c, :], hidT[:, 0, c, g * NC:(g + 1) * NC],
                              start=(c == 0), stop=(c == 1))
                for c in range(2):
                    mm = pe.matmul(ps[0:NC, 7, g * HD:(g + 1) * HD], hidT[:, 1, c, g * NC:(g + 1) * NC], w2v[:, c, :],
                                   start=(c == 0), stop=(c == 1))
            mm.then_inc(s_kc, 1)
            pe.wait_ge(s_kce, 1)
            for t in range(NT):
                for h in range(NSAH):
                    g, r = h // 3, h % 3
                    q = fmT[g * HD:(g + 1) * HD, 10 + r, t * P:(t + 1) * P]
                    at = (3 * t + r) * NC
                    mm = pe.matmul(ps[:, 3 + g, at:at + NC], q, kcT[g * HD:(g + 1) * HD, 0:NC], start=True, stop=True)
            mm.then_inc(s_cs, 1)
            pe.wait_ge(s_cp, 1)
            for h in range(NSAH):
                for t in range(NT):
                    at = (h % 2) * T + t * P
                    mm = pe.transpose(ps[0:NC, 5 + h // 2, at:at + P], pcm[:, t * NSAH + h, :], ident)
            mm.then_inc(s_cpt, 1)
            pe.wait_ge(s_cpc, 3)
            pe.wait_ge(s_fsc, 1)
            emptied(pe, len(GROUPS) - 1)

            def scores2(b, kind, h):
                if kind == "fox":
                    r, q, k = h % 2, fmT[:, h // 2, :], fmT[:, 2 + h // 2, :]
                elif kind == "dil":
                    r, q, k = h % 2, fmT[:, 4 + h // 2, :], fmT[:, 7 + h // 2, :]
                else:
                    r, q, k = h // 3, fmT[:, 10 + h % 3, :], fmT[:, 15 if kind == "sel" else 16, :]
                r = r * HD
                for lo, q0, n in ((0, 0, P), (P, P, T)):
                    mm = pe.matmul(b[:, lo:lo + n], q[r:r + HD, q0:q0 + P], k[r:r + HD, 0:n], start=True,
                                   stop=kind != "fox")
                    if kind == "fox":
                        mm = pe.matmul(b[:, lo:lo + n], ident[0:FOXH, h:h + 1].to_broadcast([FOXH, P]),
                                       fox[0:FOXH, 3, 0:n], start=False, stop=True)
                return mm

            def value2(kind, h):
                if kind == "fox":
                    return tv[:, 0, h * HD:(h + 1) * HD], tv[:, 1, h * HD:(h + 1) * HD]
                if kind == "dil":
                    return tvb[:, 0, h * HD:(h + 1) * HD], tvb[:, 1, h * HD:(h + 1) * HD]
                at = (256 if kind == "sel" else 384) + (h // 3) * HD
                return tv[:, 0, at:at + HD], tv[:, 1, at:at + HD]

            def outputs2(kind, h):
                r = h // 3 if kind in ("sel", "win") else h % 2
                return r * HD, (r + 1) * HD

            attention(UNITS2, AH, AH, AH, scores2, value2, outputs2,
                      lambda kind: (kind != "win", kind != "sel"))
            pe.wait_ge(s_y, AH + FOXH + DILH + NSAH)
            for i, (br, c0, nk) in enumerate((("pa", 0, 2), ("pb", 2, 3), ("pc", 5, 3))):
                for half in range(2):
                    landed(pe, f"{br}{half}")
                    w = wtile(f"{br}{half}")
                    for t in range(NT):
                        if i == 2:
                            pe.wait_ge(s_gv, VGROUPS + 2 * half + t + 1)
                        mm = token(ps[:, 4 * (i % 2) + 2 * half + t, :], t, w, 0, 512, yT2[:, c0:c0 + nk, :], nk
                                   ).then_inc(s_br, 1)
            turn_merged(1)
            project_out(1, "wo")
            turn_rows(3)
            hT_ready(3)
            open_sums()
            stream(NE, FP, len(ALL) % 2, faT, s_aT, NE)

        @block.scalar
        def _(act):
            link = Chain(act, c_act)
            act.wait_ge(s_const, 32)
            nc.scalar.activation(small[:, 0:KD], v("c"), ACT.Tanh, scale=0.5).then_inc(s_condt, 1)

            def row_squares(k):
                for t in range(NT):
                    link(nc.scalar.activation(hn[:, t, :], xs[:, t, :], ACT.Square,
                                              accum_out=small[:, 16 + t:17 + t]))
                act.nop().then_inc(s_ss, 1)

            def hT_half(k, scale, shift):
                for c in range(4):
                    if c % 2 == 0:
                        act.wait_ge(s_tr, 4 * k + c // 2 + 1)
                    src = ps[:, c // 2, (c % 2) * T:(c % 2 + 1) * T]
                    if shift is None:
                        nc.scalar.activation(hT[:, c, :], src, ACT.Copy, scale=scale[:, c:c + 1]).then_inc(s_hTa, 1)
                    else:
                        nc.scalar.activation(hT[:, c, :], src, ACT.Identity, scale=scale[:, c:c + 1],
                                             bias=shift[:, c:c + 1]).then_inc(s_hTa, 1)

            act.wait_ge(s_x, 16)
            row_squares(0)
            act.wait_ge(s_mev, 1)
            hT_half(0, modT[:, 32:40], modT[:, 0:8])
            for t in range(NT):
                grouped(act, f"misc{t}")
                nc.scalar.copy(raw[:, t, 0:392], bank(f"misc{t}")[:, 0:392]).then_inc(s_ga, 1)
            grouped(act, "ckv")
            for t in range(NT):
                ins = nc.scalar.copy(raw[:, t, 392:RAW], bank("ckv")[:, t * KVL:(t + 1) * KVL])
            ins.then_inc(s_ga, 1)
            act.wait_ge(s_ga, 3)
            for t in range(NT):
                link(nc.scalar.activation(att[:, 0, 0, :], raw[:, t, 0:QL], ACT.Square,
                                          accum_out=small[:, 20 + t:21 + t]))
                link(nc.scalar.activation(att[:, 0, 0, 0:KVL], raw[:, t, 392:RAW], ACT.Square,
                                          accum_out=small[:, 22 + t:23 + t]))
            act.nop().then_inc(s_css, 1)
            for i in range(4):
                act.wait_ge(s_conv, i + 1)
                nc.scalar.activation(att[:, 1, 0:2, 0:T], hn[:, i % 2, 0:512].rearrange("p (a b) -> p a b", a=2), ACT.Tanh,
                                     scale=0.5).then_inc(s_convt, 1)
                if i < 3:
                    act.wait_ge(s_gv, i + 2)

            for i in range(4):
                grouped(act, f"v{i}")
                src = bank(f"v{i}").rearrange("p (h d) -> p h d", h=2)
                nc.scalar.copy(vaug[:, i % 2, 2 * (i // 2):2 * (i // 2) + 2, 0:MV], src).then_inc(s_ga, 1)
            for i in range(4):
                grouped(act, f"qn{i}")
                if i == 0:
                    act.wait_ge(s_mpart, NMOD)
                nc.scalar.copy(qnT[:, 2 * i:2 * i + 2, :], bank(f"qn{i}").rearrange("p (a b) -> p a b", a=2)
                               ).then_inc(s_ga, 1)
            act.wait_ge(s_lf, 1)
            link(nc.scalar.activation(lst[0:MH, 6, :], lst[0:MH, 5, :], ACT.Exp, scale=-1.0))
            nc.scalar.activation(lst[0:MH, 7, :], lst[0:MH, 6, :], ACT.Ln, bias=1.0).then_inc(s_le, 1)
            for i in range(4):
                grouped(act, f"kn{i}")
                nc.scalar.copy(knT[:, 2 * i:2 * i + 2, :], bank(f"kn{i}").rearrange("p (a b) -> p a b", a=2)
                               ).then_inc(s_ga, 1)
            act.wait_ge(s_scan, 1)
            nc.scalar.activation(lst[0:MH, 5, :], lst[0:MH, 3, :], ACT.Exp, scale=-1.0).then_inc(s_em, 1)
            for i in range(4):
                grouped(act, f"o{i}")
                nc.scalar.activation(og[:, i % 2, 512 * (i // 2):512 * (i // 2 + 1)], bank(f"o{i}"), ACT.Tanh,
                                     scale=0.5).then_inc(s_ga, 1)
            act.wait_ge(s_cn, 2)
            act.wait_ge(s_grp, GI["va3"] + 1)
            for i in range(8):
                grouped(act, f"g{i}")
                nc.scalar.activation(gates[:, i % 2, 512 * (i // 2):512 * (i // 2 + 1)], bank(f"g{i}"), ACT.Tanh,
                                     scale=0.5).then_inc(s_ga, 1)

            def m_out(h):
                for t in range(NT):
                    act.wait_ge(s_mr, 2 * h + t + 1)
                    nc.scalar.activation(hn[:, t, h * MV:(h + 1) * MV], ps[:, 5 + t, 0:MV], ACT.Copy,
                                         scale=small[:, 82 + 2 * (h % 2) + t:83 + 2 * (h % 2) + t]).then_inc(s_mh, 1)

            for h in range(MH):
                act.wait_ge(s_mw, 2 * (h + 1))
                w = att[:, h % 2, 0, :]
                nc.scalar.activation(w, w, ACT.Exp).then_inc(s_mexp, 1)
                if h >= 1:
                    m_out(h - 1)
            m_out(MH - 1)

            def attention(todo, set0, unit0, out0, scale, dest, last_of):
                n, at = set0, []
                for _, heads in todo:
                    at.append(n)
                    n += len(heads)
                o = out0
                for u in range(len(todo) + 1):
                    if u < len(todo):
                        kind, heads = todo[u]
                        ui = unit0 + u
                        g = len(heads)
                        act.wait_ge(s_nm, ui + 1)
                        a = att[:, ui % 2, 0:g, :]
                        sm = small[:, 32 + 8 * (ui % 2):40 + 8 * (ui % 2)]
                        nc.scalar.activation(a[:, :, 0:P], a[:, :, 0:P], ACT.Exp, scale=scale, bias=sm[:, 0:1],
                                             accum_out=sm[:, 2:3])
                        nc.scalar.activation(a[:, :, P:SPAN], a[:, :, P:SPAN], ACT.Exp, scale=scale, bias=sm[:, 1:2],
                                             accum_out=sm[:, 3:4]).then_inc(s_exp, 1)
                    if u >= 1:
                        kind, heads = todo[u - 1]
                        for g, h in enumerate(heads):
                            s = at[u - 1] + g
                            act.wait_ge(s_pt, s + 1)
                            if s >= 3:
                                act.wait_ge(s_pv, s - 2)
                            nc.scalar.copy(pT[:, s % 3, :], ps[:, 3 + s % 3, 0:SPAN]).then_inc(s_pTc, 1)
                        if last_of(kind):
                            for g, h in enumerate(heads):
                                act.wait_ge(s_pv, at[u - 1] + g + 1)
                                d, lo, hi = dest(kind, h)
                                nc.scalar.copy(d, ps[lo:hi, 6 + o % 2, 0:T]).then_inc(s_y, 1)
                                o += 1

            attention(UNITS1, 0, 0, 0, float((NOPE + ROPE) ** -0.5), lambda kind, h: (ya[:, h, :], 0, P),
                      lambda kind: True)
            for b in range(4):
                act.wait_ge(s_yt, b + 1)
                nc.scalar.copy(ym[:, 2 * b:2 * b + 2, :], ps[:, b, :].rearrange("p (a b) -> p a b", a=2)
                               ).then_inc(s_ymT, 1)

            def merged_half(k):
                for b in range(4):
                    act.wait_ge(s_mt2, 4 * k + b + 1)
                    nc.scalar.copy(mergedT[:, 2 * b:2 * b + 2, :], ps[:, b, :].rearrange("p (a b) -> p a b", a=2)
                                   ).then_inc(s_mT, 1)

            merged_half(0)
            act.wait_ge(s_x1, 4)
            row_squares(1)
            hT_half(1, modT[:, 40:48], modT[:, 16:24])
            act.wait_ge(s_re, 1)
            nc.scalar.activation(rt[:, 80:88], rt[:, 72:80], ACT.Exp).then_inc(s_rx, 1)
            act.wait_ge(s_re, 2)
            nc.scalar.activation(rt[:, 190:192], rt[:, 188:190], ACT.Exp).then_inc(s_rx, 1)
            for i in range(0, NE // 2, 2):
                act.wait_ge(s_wbp, i + 1)
                nc.scalar.copy(wb_bc[:, 2 * i:2 * i + 2, :], ps[:, 4 + i % 4, :].rearrange("p (a b) -> p a b", a=2)
                               ).then_inc(s_wba, 1)

            def half_tanh(i, b):
                act.wait_ge(s_gup, 2 * i + b + 1)
                act.wait_ge(s_a2, 2 * i + b + 1)
                nc.scalar.activation(tmp[:, b, :], ps[:, 4 + 2 * b, :], ACT.Tanh, scale=0.5).then_inc(s_th, 1)

            with act.Fori(0, NE // 2) as i:
                half_tanh(i, 0)
                half_tanh(i, 1)

            def final_norm(k):
                act.wait_ge(s_x1, 8 * (k + 1))
                for t in range(NT):
                    link(nc.scalar.activation(hn[:, t, :], xs[:, t, :], ACT.Square, accum_out=small[:, 16 + t:17 + t]))
                act.nop().then_inc(s_fss, 1)

            final_norm(0)
            act.wait_ge(s_xf, 2)
            row_squares(2)
            hT_half(2, v("g3"), None)
            for name, c0, n in (("fox1", 2, 2), ("dil2", 7, 2), ("dil3", 9, 1), ("kk", 15, 2)):
                grouped(act, name)
                for j in range(n):
                    ins = nc.scalar.activation(fmT[:, c0 + j, :], bank(name)[:, j * T:(j + 1) * T], ACT.Identity,
                                               bias=v("b2f", c0 + j, c0 + j + 1))
                ins.then_inc(s_ga, 1)
            act.wait_ge(s_fl, 1)
            link(nc.scalar.activation(fox[0:FOXH, 1, :], fox[0:FOXH, 1, :], ACT.Exp, scale=-1.0))
            nc.scalar.activation(fox[0:FOXH, 2, :], fox[0:FOXH, 1, :], ACT.Ln, bias=1.0).then_inc(s_fe, 1)
            nc.scalar.activation(gc, gc, ACT.Tanh, scale=0.5).then_inc(s_gct, 1)
            act.wait_ge(s_hu, 1)
            nc.scalar.activation(gel[:, 3], gel[:, 2], ACT.Tanh, scale=GELU).then_inc(s_hth, 1)
            for i in range(12):
                act.wait_ge(s_gv, VGROUPS - 12 + i + 1)
                sl = g2[:, i % 2, 512 * (i // 2):512 * (i // 2 + 1)]
                nc.scalar.activation(sl, sl, ACT.Tanh, scale=0.5).then_inc(s_ggu, 1)
            act.wait_ge(s_ce, 1)
            nc.scalar.activation(pcm, pcm, ACT.Exp).then_inc(s_cx, 1)
            act.wait_ge(s_cpt, 1)
            for i in range(3):
                nc.scalar.copy(pcT[0:NC, 2 * i:2 * i + 2, :], ps[0:NC, 5 + i, :].rearrange("p (a b) -> p a b", a=2)
                               ).then_inc(s_cpc, 1)

            def dest2(kind, h):
                if kind == "fox":
                    c, r = h // 2, h % 2
                elif kind == "dil":
                    c, r = 2 + h // 2, h % 2
                else:
                    c, r = 5 + h % 3, h // 3
                return yT2[r * HD:(r + 1) * HD, c, :], r * HD, (r + 1) * HD

            attention(UNITS2, AH, AH, AH, 1.0, dest2, lambda kind: kind != "sel")
            merged_half(1)
            act.wait_ge(s_x1, 12)
            row_squares(3)
            hT_half(3, v("g4"), None)

            def ff_act(i, b):
                act.wait_ge(s_fsq, 2 * i + b + 1)
                nc.scalar.activation(ft[:, 2, :], ft[:, b, :], ACT.Square).then_inc(s_fz, 1)
                act.wait_ge(s_fth, 2 * i + b + 1)
                nc.scalar.activation(ft[:, 4, :], ft[:, 3, :], ACT.Tanh, scale=GELU).then_inc(s_ffn, 1)

            with act.Fori(0, FP // 2) as i:
                ff_act(i, 0)
                ff_act(i, 1)
            ff_act(FP // 2, 0)
            final_norm(1)

        @block.gpsimd
        def _(pool):
            link = Chain(pool, c_pool)
            pool.wait_ge(s_zero, 1)

            def power(dst, src, n, ready, count, done):
                pool.wait_ge(ready, count)
                nc.gpsimd.tensor_tensor(dst, src, small[:, 496:496 + n], ALU.pow).then_inc(done, 1)

            power(small[:, 18:20], small[:, 18:20], 2, s_ms, 1, s_rstd)
            power(small[:, 24:28], small[:, 24:28], 4, s_cms, 1, s_crs)
            power(small[:, 18:20], small[:, 18:20], 2, s_ms, 2, s_rstd)
            power(small[:, 18:20], small[:, 18:20], 2, s_fms, 1, s_frs)
            power(small[:, 18:20], small[:, 18:20], 2, s_ms, 3, s_rstd)
            power(small[:, 18:20], small[:, 18:20], 2, s_ms, 4, s_rstd)
            power(small[:, 18:20], small[:, 18:20], 2, s_fms, 2, s_frs)

        @block.vector
        def _(dve):
            link = Chain(dve, c_dve)
            V = nc.vector
            V.memset(small[:, 496:500], -0.5).then_inc(c_dve, 1)
            link.n += 1
            link(V.memset(zero[:, :], 0.0))
            dve.nop().then_inc(s_zero, 1)
            dve.wait_ge(s_condt, 1)
            link(V.scalar_tensor_tensor(small[:, 8:16], small[:, 0:8], 1.0, v("c"), ALU.add, ALU.mult))
            link(V.tensor_scalar(small[:, 8:16], small[:, 8:16], 0.5, None, ALU.mult))

            def mod_part(j):
                dve.wait_ge(s_mt[j % 2], 16 * (j // 2 + 1))
                if j >= 2:
                    dve.wait_ge(s_msum, j - 1)
                d = mpart[:, j % 2, :]
                w = mtile[j % 2]
                link(V.tensor_scalar(d, w[:, 0, :], small[:, 8:9], None, ALU.mult))
                for c in range(1, KD):
                    ins = V.scalar_tensor_tensor(d, w[:, c, :], small[:, 8 + c:9 + c], d, ALU.mult, ALU.add)
                    if c < KD - 1:
                        link(ins)
                ins.then_inc(s_mpart, 1)

            def mod_gate(j):
                dve.wait_ge(s_msum, j + 1)
                if j == 4:
                    dve.wait_ge(s_brow, 32)
                k, half = (0, j - 4) if j < 6 else (1, j - 10)
                g = gateb[:, k, half * 512:(half + 1) * 512]
                V.tensor_tensor(g, ps[:, 7, :], g, ALU.add).then_inc(s_mev, 1)

            def mod_columns(k):
                link(V.tensor_tensor(modT[:, 16 * k:16 * k + 16], ps[:, 7, 0:16], v(f"mod{k + 1}"), ALU.add))
                V.scalar_tensor_tensor(modT[:, 32 + 8 * k:40 + 8 * k], modT[:, 16 * k + 8:16 * k + 16], 1.0,
                                       v(f"g{k + 1}"), ALU.add, ALU.mult).then_inc(s_mev, 1)

            for j in range(4):
                mod_part(j)
            dve.wait_ge(s_msum, 4)
            mod_columns(0)

            def row_scale(k, sem_in, n_in, sem_ms, sem_rs, n):
                dve.wait_ge(sem_in, n_in)
                V.tensor_scalar(small[:, 18:20], small[:, 16:18], 1.0 / D, EPS, ALU.mult, ALU.add).then_inc(sem_ms, 1)
                dve.wait_ge(sem_rs, n)

            def norm_rows(k):
                row_scale(k, s_ss, k + 1, s_ms, s_rstd, k + 1)
                for t in range(NT):
                    V.tensor_scalar(hn[:, t, :], xs[:, t, :], small[:, 18 + t:19 + t], None, ALU.mult).then_inc(s_hn, 1)

            def hT_half(k, scale, shift):
                for c in range(4, KD):
                    if c % 2 == 0:
                        dve.wait_ge(s_tr, 4 * k + c // 2 + 1)
                    src = ps[:, c // 2, (c % 2) * T:(c % 2 + 1) * T]
                    if shift is None:
                        V.tensor_scalar(hT[:, c, :], src, scale[:, c:c + 1], None, ALU.mult).then_inc(s_hTv, 1)
                    else:
                        V.tensor_scalar(hT[:, c, :], src, scale[:, c:c + 1], shift[:, c:c + 1], ALU.mult, ALU.add
                                        ).then_inc(s_hTv, 1)

            norm_rows(0)
            dve.wait_ge(s_mev, 1)
            hT_half(0, modT[:, 32:40], modT[:, 0:8])

            def rope(dst, src, t1, t2):
                link(V.tensor_tensor(t1, src, const("cos"), ALU.mult))
                for q in range(4):
                    o = q ^ 1
                    ins = V.tensor_tensor(t2[q * 32:(q + 1) * 32, :], src[o * 32:(o + 1) * 32, :],
                                          const("sin")[q * 32:(q + 1) * 32, :], ALU.mult)
                    link(ins)
                return V.tensor_tensor(dst, t1, t2, ALU.add)

            sc1, sc2 = pT[:, 0, 0:T], pT[:, 1, 0:T]
            grouped(dve, "kr")
            krope = pT[:, 2, 0:T]
            link(rope(krope, bank("kr")[:, 0:T], sc1, sc2))
            dve.nop().then_inc(s_gv, 1)
            dve.wait_ge(s_css, 1)
            link(V.tensor_scalar(small[:, 24:26], small[:, 20:22], 1.0 / QL, EPS, ALU.mult, ALU.add))
            V.tensor_scalar(small[:, 26:28], small[:, 22:24], 1.0 / KVL, EPS, ALU.mult, ALU.add).then_inc(s_cms, 1)
            dve.wait_ge(s_crs, 1)
            for t in range(NT):
                link(V.tensor_scalar(raw[:, t, 0:QL], raw[:, t, 0:QL], small[:, 24 + t:25 + t], None, ALU.mult))
                V.tensor_scalar(raw[:, t, 392:RAW], raw[:, t, 392:RAW], small[:, 26 + t:27 + t], None, ALU.mult
                                ).then_inc(s_cn, 1)

            def conv(i):
                name = f"qk{i}"
                grouped(dve, name)
                src = bank(name).rearrange("p (a b) -> p a b", a=2)
                acc = hn[:, i % 2, 0:512].rearrange("p (a b) -> p a b", a=2)
                for j in range(2):
                    blk = 2 * i + j
                    wv = v("convw", 4 * blk, 4 * blk + 4)
                    link(V.tensor_scalar(acc[:, j, :], src[:, j, :], wv[:, 3:4], v("convb", blk, blk + 1), ALU.mult,
                                         ALU.add))
                    for d in range(1, CONV):
                        link(V.scalar_tensor_tensor(acc[:, j, d:T], src[:, j, 0:T - d], wv[:, 3 - d:4 - d],
                                                    acc[:, j, d:T], ALU.mult, ALU.add))
                dve.nop().then_inc(s_conv, 1)
                dve.wait_ge(s_convt, i + 1)
                V.scalar_tensor_tensor(qkT[:, 2 * i:2 * i + 2, :], att[:, 1, 0:2, 0:T], 1.0, acc, ALU.add, ALU.mult
                                       ).then_inc(s_gv, 1)

            dve.wait_ge(s_hn, 2)
            dve.wait_ge(s_tr, 4)
            conv(0)
            conv(1)
            mod_part(4)
            mod_gate(4)
            mod_part(5)
            mod_gate(5)
            mod_part(6)
            conv(2)
            conv(3)
            mod_part(7)
            mod_part(8)
            mod_part(9)
            dve.wait_ge(s_msum, 10)
            mod_columns(1)
            mod_part(10)
            mod_gate(10)
            mod_part(11)
            mod_gate(11)
            V.memset(vaug[:, :, :, MV:MV + 1], 1.0).then_inc(c_dve, 1)
            link.n += 1
            dve.wait_ge(s_ctr, 1)
            for c in range(5):
                g = v("qg", c, c + 1) if c < 3 else v("kvg", c - 3, c - 2)
                V.tensor_scalar(cT[:, c, :], ps[:, 4 + c // 2, (c % 2) * T:(c % 2 + 1) * T], g, None, ALU.mult
                                ).then_inc(c_dve, 1)
                link.n += 1
            link(V.tensor_copy(krT, krope))
            dve.nop().then_inc(s_cT, 1)
            L = lst[0:MH, :, :]
            link(V.tensor_scalar(L[:, 1, :], ps[0:MH, 7, 0:T], v("fb")[0:MH, :], None, ALU.add))
            link(V.tensor_scalar(L[:, 2, :], ps[0:MH, 6, T:2 * T], v("ib")[0:MH, :], None, ALU.add))
            V.scalar_tensor_tensor(L[:, 5, :], L[:, 1, :], -1.0, L[:, 1, :], ALU.mult, ALU.max).then_inc(s_lf, 1)
            dve.wait_ge(s_le, 1)
            link(V.scalar_tensor_tensor(L[:, 1, :], L[:, 1, :], 0.0, L[:, 7, :], ALU.min, ALU.subtract))
            link(V.tensor_tensor_scan(L[:, 6, :], const("ones")[0:MH, 0:1].to_broadcast([MH, T]), L[:, 1, :], 0.0,
                                      ALU.mult, ALU.add))
            link(V.tensor_tensor(L[:, 2, :], L[:, 2, :], L[:, 6, :], ALU.subtract))
            link(V.tensor_tensor_scan(L[:, 4, :], const("ones")[0:MH, 0:1].to_broadcast([MH, T]), L[:, 2, :], 0.0,
                                      ALU.mult, ALU.max))
            link(V.tensor_tensor(L[:, 3, :], L[:, 4, :], L[:, 6, :], ALU.add))
            link(V.tensor_scalar(L[:, 4, :], L[:, 4, :], -1.0, None, ALU.mult))
            dve.nop().then_inc(s_scan, 1)
            for i in range(2):
                grouped(dve, f"qr{i}")
                for j in range(2):
                    link(rope(qrT[:, 2 * i + j, :], bank(f"qr{i}")[:, j * T:(j + 1) * T], sc1, sc2))
                dve.nop().then_inc(s_gv, 1)
            for i in range(4):
                grouped(dve, f"va{i}")
                V.tensor_copy(va[:, i % 2, 512 * (i // 2):512 * (i // 2 + 1)], bank(f"va{i}")).then_inc(s_gv, 1)
            dve.wait_ge(s_gt, 1)
            V.tensor_copy(small[:, 64:80], ps[:, 4, 0:16]).then_inc(s_gte, 1)
            dve.wait_ge(s_gte, 1)

            def m_weights(h):
                dve.wait_ge(s_mS, h + 1)
                w = att[:, h % 2, 0, :]
                V.tensor_scalar(w[:, 0:T], ps[:, h % 2, 0:T], small[:, 64 + h:65 + h], 0.0, ALU.add, ALU.min
                                ).then_inc(s_mw, 1)
                V.tensor_scalar(w[:, T:SPAN], ps[:, h % 2, P:T], small[:, 68 + h:69 + h], 0.0, ALU.add, ALU.min
                                ).then_inc(s_mw, 1)
                dve.wait_ge(s_mexp, h + 1)
                if h >= 2:
                    dve.wait_ge(s_mnum, h - 1)
                d = wmem[:, (h % 2) * SPAN:(h % 2 + 1) * SPAN]
                link(V.scalar_tensor_tensor(d, ps[:, 2 + h % 2, 0:SPAN], 0.25 * MQK ** -0.5, w, ALU.mult, ALU.mult))
                link(V.tensor_tensor(d[:, 0:P], d[:, 0:P], const("tri"), ALU.mult))
                V.tensor_tensor(d[:, T:SPAN], d[:, T:SPAN], const("tri"), ALU.mult).then_inc(s_mst, 1)

            def m_den(h):
                dve.wait_ge(s_mnum, h + 1)
                for t in range(NT):
                    r = small[:, 80 + t:81 + t]
                    link(V.tensor_scalar(r, ps[:, 5 + t, MV:MV + 1], -1.0, small[:, 72 + 4 * t + h:73 + 4 * t + h],
                                         ALU.mult, ALU.max))
                    link(V.tensor_tensor(r, ps[:, 5 + t, MV:MV + 1], r, ALU.max))
                    V.reciprocal(small[:, 82 + 2 * (h % 2) + t:83 + 2 * (h % 2) + t], r).then_inc(s_mr, 1)
                dve.wait_ge(s_mh, 2 * (h + 1))
                for t in range(NT):
                    o = og[:, t, h * MV:(h + 1) * MV]
                    V.scalar_tensor_tensor(o, o, 1.0, hn[:, t, h * MV:(h + 1) * MV], ALU.add, ALU.mult
                                           ).then_inc(s_my, 1)

            for h in range(MH):
                m_weights(h)
                if h >= 1:
                    m_den(h - 1)
            m_den(MH - 1)

            def attention(todo, set0, unit0, scale, bias):
                n, at = set0, []
                for _, heads in todo:
                    at.append(n)
                    n += len(heads)
                for u in range(len(todo) + 1):
                    if u < len(todo):
                        kind, heads = todo[u]
                        ui = unit0 + u
                        a = att[:, ui % 2, 0:len(heads), :]
                        sm = small[:, 32 + 8 * (ui % 2):40 + 8 * (ui % 2)]
                        if u >= 2:
                            dve.wait_ge(s_pt, at[u - 1])
                        for g, h in enumerate(heads):
                            s = at[u] + g
                            dve.wait_ge(s_sc, s + 1)
                            tile, slope = bias(kind, g, h)
                            V.scalar_tensor_tensor(a[:, g, :], tile, slope, ps[:, s % 3, 0:SPAN], ALU.mult, ALU.add
                                                   ).then_inc(s_sfree, 1)
                        dve.wait_ge(s_sfree, at[u] + len(heads))
                        V.tensor_reduce(sm[:, 0:1], a[:, :, 0:P], AX.XY, ALU.max, negate=True).then_inc(c_dve, 1)
                        link.n += 1
                        if scale is None:
                            V.tensor_reduce(sm[:, 1:2], a[:, :, P:SPAN], AX.XY, ALU.max, negate=True
                                            ).then_inc(s_nm, 1)
                        else:
                            link(V.tensor_reduce(sm[:, 1:2], a[:, :, P:SPAN], AX.XY, ALU.max, negate=True))
                            V.tensor_scalar(sm[:, 0:2], sm[:, 0:2], scale, None, ALU.mult).then_inc(s_nm, 1)
                    if u >= 1:
                        kind, heads = todo[u - 1]
                        ui = unit0 + u - 1
                        a = att[:, ui % 2, 0:len(heads), :]
                        sm = small[:, 32 + 8 * (ui % 2):40 + 8 * (ui % 2)]
                        dve.wait_ge(s_exp, ui + 1)
                        link(V.tensor_scalar(sm[:, 4:6], sm[:, 2:4], TINY, None, ALU.max))
                        link(V.reciprocal(sm[:, 4:6], sm[:, 4:6]))
                        if kind in ("sel", "win"):
                            j = 3 * heads[0] + (1 if kind == "sel" else 2)
                            link(V.tensor_tensor(sm[:, 4:6], sm[:, 4:6], gc[:, :, j:j + 1].rearrange("p t o -> p (t o)"),
                                                 ALU.mult))
                        V.tensor_scalar(a[:, :, 0:P], a[:, :, 0:P], sm[:, 4:5], None, ALU.mult)
                        V.tensor_scalar(a[:, :, P:SPAN], a[:, :, P:SPAN], sm[:, 5:6], None, ALU.mult).then_inc(s_p, 1)

            attention(UNITS1, 0, 0, float((NOPE + ROPE) ** -0.5), lambda kind, g, h: (const("chunk"), 1.0))

            for half in range(2):
                for t in range(NT):
                    dve.wait_ge(s_br, 2 * half + t + 1)
                    cs = slice(512 * half, 512 * (half + 1))
                    link(V.scalar_tensor_tensor(hn[:, t, cs], gates[:, t, cs], 1.0, ps[:, 2 * half + t, :], ALU.add,
                                                ALU.mult))
            for half in range(2):
                for t in range(NT):
                    dve.wait_ge(s_br, 4 + 2 * half + t + 1)
                    cs = slice(512 * half, 512 * (half + 1))
                    ga = gates[:, t, D + 512 * half:D + 512 * (half + 1)]
                    link(V.scalar_tensor_tensor(ga, ga, 1.0, ps[:, 4 + 2 * half + t, :], ALU.add, ALU.mult))
                    V.scalar_tensor_tensor(merged[:, t, cs], hn[:, t, cs], 0.5, ga, ALU.mult, ALU.add
                                           ).then_inc(s_mrg, 1)
            link(V.tensor_scalar(gateb[:, 0, :], gateb[:, 0, :], 0.5, None, ALU.mult))
            for half in range(2):
                for t in range(NT):
                    dve.wait_ge(s_pr, 2 * half + t + 1)
                    cs = slice(512 * half, 512 * (half + 1))
                    link(V.tensor_tensor(hn[:, t, cs], ps[:, 4 + 2 * half + t, :], gateb[:, 0, cs], ALU.mult))
                    V.tensor_tensor(xs[:, t, cs], xs[:, t, cs], hn[:, t, cs], ALU.add).then_inc(s_x1, 1)
            norm_rows(1)
            hT_half(1, modT[:, 40:48], modT[:, 16:24])

            lg = rt[:, 0:72].rearrange("p (t n) -> p t n", t=NT)
            lgrp = lg[:, :, 0:NG]
            lexp = lg[:, :, NG:NG + NE].rearrange("p t (g e) -> p t g e", g=NG)

            def t2(a, n):
                return rt[:, a:a + NT * n].rearrange("p (t n) -> p t n", t=NT)

            def bc(a, shape):
                return a.to_broadcast(shape)

            dve.wait_ge(s_final1, 32)
            dve.wait_ge(s_lg, 1)
            for t in range(NT):
                link(V.tensor_tensor(lg[:, t, :], ps[:, 0, t * 36:(t + 1) * 36], small[:, 448:484], ALU.add))
            gmax, gdif, gexp = t2(88, 1), t2(72, NG), t2(80, NG)
            link(V.tensor_reduce(gmax, lgrp, AX.X, ALU.max))
            ins = V.tensor_tensor(gdif, lgrp, bc(gmax, [P, NT, NG]), ALU.subtract)
            ins.then_inc(s_re, 1)
            gsum, pg, oh, key, kmax = t2(90, 1), t2(92, 1), t2(96, NG), t2(104, EG), t2(120, 1)
            dve.wait_ge(s_rx, 1)
            link(V.tensor_reduce(gsum, gexp, AX.X, ALU.add))
            link(V.reciprocal(pg, gsum))

            def first_max(dst, src, top, rank, n):
                k = t2(104, n)
                link(V.tensor_tensor(dst, src, bc(top, [P, NT, n]), ALU.is_equal))
                for t in range(NT):
                    link(V.tensor_tensor(k[:, t, :], dst[:, t, :], rank, ALU.mult))
                link(V.tensor_reduce(kmax, k, AX.X, ALU.max))
                link(V.tensor_tensor(dst, k, bc(kmax, [P, NT, n]), ALU.is_equal))

            first_max(oh, lgrp, gmax, const("rank4"), NG)
            prod = rt[:, 512:512 + 64].rearrange("p (t g e) -> p t g e", t=NT, g=NG)
            for t in range(NT):
                link(V.tensor_tensor(prod[:, t], lexp[:, t], bc(oh[:, t, :].rearrange("p (g o) -> p g o", o=1), [P, NG, EG]),
                                     ALU.mult))
            l8, top1, oh1, l8b, top2, oh2 = t2(122, EG), t2(138, 1), t2(140, EG), t2(156, EG), t2(172, 1), t2(194, EG)
            link(V.tensor_reduce(l8, prod.rearrange("p t g e -> p t e g"), AX.X, ALU.add))
            link(V.tensor_reduce(top1, l8, AX.X, ALU.max))
            first_max(oh1, l8, top1, const("rank8"), EG)
            link(V.scalar_tensor_tensor(l8b, oh1, NEG, l8, ALU.mult, ALU.add))
            link(V.tensor_reduce(top2, l8b, AX.X, ALU.max))
            first_max(oh2, l8b, top2, const("rank8"), EG)
            e2, w1, w2 = rt[:, 190:192], rt[:, 174:176], rt[:, 176:178]
            V.tensor_tensor(rt[:, 188:190], rt[:, 172:174], rt[:, 138:140], ALU.subtract).then_inc(s_re, 1)
            dve.wait_ge(s_rx, 2)
            link(V.tensor_scalar(w1, e2, 1.0, None, ALU.add))
            link(V.reciprocal(w1, w1))
            link(V.tensor_tensor(w1, w1, rt[:, 92:94], ALU.mult))
            link(V.tensor_scalar(w1, w1, 0.5, None, ALU.mult))
            link(V.tensor_tensor(w2, w1, e2, ALU.mult))
            w8 = t2(210, EG)
            w32 = rt[:, 256:256 + 64].rearrange("p (t g e) -> p t g e", t=NT, g=NG)
            for t in range(NT):
                link(V.tensor_scalar(w8[:, t, :], oh1[:, t, :], w1[:, t:t + 1], None, ALU.mult))
                link(V.scalar_tensor_tensor(w8[:, t, :], oh2[:, t, :], w2[:, t:t + 1], w8[:, t, :], ALU.mult, ALU.add))
                for g in range(NG):
                    link(V.tensor_scalar(w32[:, t, g, :], w8[:, t, :], oh[:, t, g:g + 1], None, ALU.mult))
            dve.nop().then_inc(s_w32, 1)
            dve.wait_ge(s_wt, 1)
            V.tensor_copy(rt[0:NE, 384:384 + T], ps[0:NE, 1, 0:T]).then_inc(s_wtc, 1)
            for i in range(1, NE // 2, 2):
                dve.wait_ge(s_wbp, i + 1)
                V.tensor_copy(wb_bc[:, 2 * i:2 * i + 2, :], ps[:, 4 + i % 4, :].rearrange("p (a b) -> p a b", a=2)
                              ).then_inc(s_wbv, 1)
            dve.wait_ge(s_wba, NE // 4)

            def expert(i, b):
                dve.wait_ge(s_th, 2 * i + b + 1)
                t0, g, u = tmp[:, b, :], ps[:, 4 + 2 * b, :], ps[:, 5 + 2 * b, :]
                link(V.scalar_tensor_tensor(t0, t0, 1.0, g, ALU.add, ALU.mult))
                V.tensor_tensor(t0, t0, u, ALU.mult).then_inc(s_a2, 1)
                dve.wait_ge(s_a2, 2 * i + b + 2)
                dve.wait_ge(s_dnp, 2 * i + b + 1)
                for f in range(2):
                    ins = V.tensor_tensor(aT[:, b, f, :], t0[:, f * T:(f + 1) * T],
                                          wb_bc[:, bass.ds(2 * i + b, 1), :].rearrange("p a n -> p (a n)"), ALU.mult)
                    link(ins)
                dve.nop().then_inc(s_aT, 1)

            dve.nop().then_inc(s_a2, 1)
            per = 6
            with dve.Fori(0, NE // 2) as i:
                n = link.n
                link.start(i, per)
                expert(i, 0)
                expert(i, 1)
                assert link.n - n == per
            link.end(NE // 2)
            dve.wait_ge(s_dnp, NE + 1)
            for t in range(NT):
                for half in range(2):
                    cs = slice(512 * half, 512 * (half + 1))
                    link(V.tensor_tensor(hn[:, t, cs], ps[:, 2 * t + half, :], gateb[:, 1, cs], ALU.mult))
                    V.tensor_tensor(xs[:, t, cs], xs[:, t, cs], hn[:, t, cs], ALU.add).then_inc(s_x1, 1)

            def final_norm(k, dst):
                row_scale(k, s_fss, k + 1, s_fms, s_frs, k + 1)
                if k == 1:
                    dve.wait_ge(s_final2, 16)
                for t in range(NT):
                    V.scalar_tensor_tensor(dst[:, t, :], xs[:, t, :], small[:, 18 + t:19 + t], finalb[:, :], ALU.mult,
                                           ALU.mult).then_inc(s_xf, 1)

            final_norm(0, xs)
            dve.wait_ge(s_xf, 2)
            norm_rows(2)
            hT_half(2, v("g3"), None)

            def columns_out(name, c0, n, scale):
                grouped(dve, name)
                for j in range(n):
                    src = bank(name)[:, j * T:(j + 1) * T]
                    if scale:
                        ins = V.tensor_scalar(fmT[:, c0 + j, :], src, v("b2f", c0 + j, c0 + j + 1), 0.125, ALU.add,
                                              ALU.mult)
                    else:
                        ins = V.tensor_scalar(fmT[:, c0 + j, :], src, v("b2f", c0 + j, c0 + j + 1), None, ALU.add)
                ins.then_inc(s_gv, 1)

            columns_out("fox0", 0, 2, True)
            columns_out("dil0", 4, 2, True)
            columns_out("dil1", 6, 1, True)
            columns_out("nsa0", 10, 2, True)
            columns_out("nsa1", 12, 1, True)
            columns_out("kcv", 13, 2, False)
            emptied(dve, GI["kcv"])
            for i in range(2):
                for g in range(KVG):
                    for jj in range(2):
                        src = fmT[g * HD:(g + 1) * HD, 13 + i, :]
                        d = kvc[jj * HD:(jj + 1) * HD, i, :, g * NC:(g + 1) * NC]
                        for q in range(2):
                            s3 = src[:, 16 * q:16 * q + 240].rearrange("p (c j two) -> p two j c", j=8, two=2)[:, jj]
                            link(V.tensor_copy(d[:, 8 * q:8 * q + 8, :], s3))
                link(V.tensor_tensor(kvc[:, i], kvc[:, i],
                                     v("pe").rearrange("p (j o) -> p j o", o=1).to_broadcast([P, CB // 2, KVG * NC]),
                                     ALU.add))
            dve.nop().then_inc(s_F, 1)
            dve.wait_ge(s_bias2, 16)
            grouped(dve, "gf")
            f = fox[0:FOXH]
            for t in range(NT):
                V.tensor_tensor(gc[:, t, :], bank("gf")[:, t * 3 * NSAH:(t + 1) * 3 * NSAH], bias2[:, 896:914], ALU.add)
            V.tensor_scalar(f[:, 0, :], bank("gf")[0:FOXH, T:2 * T], v("fab")[0:FOXH, :], None, ALU.add).then_inc(s_gv, 1)
            emptied(dve, GI["gf"])
            V.scalar_tensor_tensor(f[:, 1, :], f[:, 0, :], -1.0, f[:, 0, :], ALU.mult, ALU.max).then_inc(s_fl, 1)
            for t in range(NT):
                grouped(dve, f"vv{t}")
                V.tensor_tensor(tv[:, t, :], bank(f"vv{t}"), bias2[:, 0:512], ALU.add).then_inc(s_gv, 1)
            for t in range(NT):
                grouped(dve, f"vb{t}")
                V.tensor_tensor(tvb[:, t, :], bank(f"vb{t}")[:, 0:384], bias2[:, 512:896], ALU.add).then_inc(s_gv, 1)
            dve.wait_ge(s_fe, 1)
            link(V.scalar_tensor_tensor(f[:, 0, :], f[:, 0, :], 0.0, f[:, 2, :], ALU.min, ALU.subtract))
            link(V.tensor_tensor_scan(f[:, 3, :], const("ones")[0:MH, 0:1].to_broadcast([MH, T]), f[:, 0, :], 0.0,
                                      ALU.mult, ALU.add))
            V.tensor_scalar(f[:, 3, :], f[:, 3, :], -1.0, None, ALU.mult).then_inc(s_fsc, 1)
            dve.wait_ge(s_hid, 2)
            hu, hw, hz, ht = (gel[:, k] for k in range(4))
            link(V.tensor_copy(hu, ps[:, 4:6, 0:60]))
            link(V.tensor_tensor(hw, hu, hu, ALU.mult))
            link(V.tensor_scalar(hw, hw, 0.044715, 1.0, ALU.mult, ALU.add))
            V.tensor_tensor(hz, hw, hu, ALU.mult).then_inc(s_hu, 1)
            dve.wait_ge(s_hth, 1)
            link(V.scalar_tensor_tensor(hw, ht, 1.0, hu, ALU.add, ALU.mult))
            V.tensor_scalar(hidT.rearrange("p a b c -> p a (b c)"), hw, 0.5, None, ALU.mult).then_inc(s_hg, 1)
            for i in range(12):
                grouped(dve, f"h{i}")
                V.tensor_tensor(g2[:, i % 2, 512 * (i // 2):512 * (i // 2 + 1)], bank(f"h{i}"),
                                bias2[:, 914 + 512 * (i // 2):914 + 512 * (i // 2 + 1)], ALU.add).then_inc(s_gv, 1)
            dve.wait_ge(s_kc, 1)
            link(V.tensor_copy(kcT[:, 0:NC], ps[:, 6, 0:NC]))
            V.tensor_copy(vc[0:NC], ps[0:NC, 7, 0:2 * HD].rearrange("p (g d) -> p g d", g=KVG)).then_inc(s_kce, 1)
            dve.wait_ge(s_gct, 1)
            gcf = gc.rearrange("p t n -> p (t n)")
            link(V.tensor_scalar(gcf, gcf, 0.5, 0.5, ALU.mult, ALU.add))
            dve.wait_ge(s_cs, 1)
            pf = pcm.rearrange("p a b -> p (a b)")
            for g in range(KVG):
                link(V.tensor_tensor(pf.rearrange("p (t g n) -> p t g n", t=NT, g=KVG)[:, :, g, :],
                                     ps[:, 3 + g, 0:NT * 3 * NC].rearrange("p (t n) -> p t n", t=NT),
                                     const("cbias").rearrange("p (t g n) -> p t g n", t=NT, g=KVG)[:, :, g, :], ALU.add))
            cm, cl = small[:, 420:432], small[:, 432:444]
            m3 = cm.rearrange("p (a o) -> p a o", o=1)
            link(V.tensor_reduce(m3, pcm, AX.X, ALU.max))
            V.tensor_tensor(pcm, pcm, m3.to_broadcast([P, NT * NSAH, NC]), ALU.subtract).then_inc(s_ce, 1)
            dve.wait_ge(s_cx, 1)
            link(V.tensor_tensor(pf, pf, const("cmask"), ALU.mult))
            link(V.tensor_reduce(cl.rearrange("p (a o) -> p a o", o=1), pcm, AX.X, ALU.add))
            link(V.tensor_scalar(cl, cl, TINY, None, ALU.max))
            link(V.reciprocal(cl, cl))
            link(V.tensor_tensor(cl.rearrange("p (t h) -> p t h", t=NT), cl.rearrange("p (t h) -> p t h", t=NT),
                                 gc[:, :, 0:3 * NSAH:3], ALU.mult))
            V.tensor_tensor(pcm, pcm, cl.rearrange("p (a o) -> p a o", o=1).to_broadcast([P, NT * NSAH, NC]), ALU.mult
                            ).then_inc(s_cp, 1)

            def bias2_tile(kind, g, h):
                if kind == "fox":
                    return const("causal"), 1.0
                if kind == "dil":
                    return const("dil", g * SPAN, (g + 1) * SPAN), DIL_SLOPE[h]
                return const("dist"), NSA_SLOPE[h]

            attention(UNITS2, AH, AH, None, bias2_tile)

            for i in range(3):
                for half in range(2):
                    for t in range(NT):
                        dve.wait_ge(s_br, 8 + 4 * i + 2 * half + t + 1)
                        if i == 0:
                            dve.wait_ge(s_ggu, 12)
                        cs = slice(512 * half, 512 * (half + 1))
                        gsl = g2[:, t, i * D + 512 * half:i * D + 512 * (half + 1)]
                        p = ps[:, 4 * (i % 2) + 2 * half + t, :]
                        if i == 0:
                            V.scalar_tensor_tensor(merged2[:, t, cs], gsl, 1.0, p, ALU.add, ALU.mult
                                                   ).then_inc(s_gv, 1)
                        else:
                            link(V.scalar_tensor_tensor(gsl, gsl, 1.0, p, ALU.add, ALU.mult))
                            ins = V.tensor_tensor(merged2[:, t, cs], merged2[:, t, cs], gsl, ALU.add)
                            if i == 1:
                                link(ins)
                            else:
                                ins.then_inc(s_mrg, 1)
            for half in range(2):
                for t in range(NT):
                    dve.wait_ge(s_pr, 4 + 2 * half + t + 1)
                    cs = slice(512 * half, 512 * (half + 1))
                    V.scalar_tensor_tensor(xs[:, t, cs], ps[:, 4 + 2 * half + t, :], 0.5, xs[:, t, cs], ALU.mult,
                                           ALU.add).then_inc(s_x1, 1)
            norm_rows(3)
            hT_half(3, v("g4"), None)

            cw = v("conv2").rearrange("p (f n) -> p f n", n=4)

            def feed(i, b):
                dve.wait_ge(s_gup, NE + 2 * i + b + 1)
                acc, z, th = ft[:, b, :], ft[:, 3, :], ft[:, 4, :]
                for f in range(2):
                    src = ps[:, 4 + 2 * b, f * T:(f + 1) * T]
                    par = cw[:, bass.ds(4 * i + 2 * b + f, 1), :].rearrange("p a n -> p (a n)")
                    d = acc[:, f * T:(f + 1) * T]
                    link(V.tensor_scalar(d, src, par[:, 2:3], par[:, 3:4], ALU.mult, ALU.add))
                    for k in (1, 2):
                        ins = V.scalar_tensor_tensor(d[:, k:T], src[:, 0:T - k], par[:, 2 - k:3 - k], d[:, k:T],
                                                     ALU.mult, ALU.add)
                        if (f, k) != (1, 2):
                            link(ins)
                ins.then_inc(s_fsq, 1)
                dve.wait_ge(s_fz, 2 * i + b + 1)
                link(V.tensor_scalar(z, ft[:, 2, :], 0.044715, 1.0, ALU.mult, ALU.add))
                V.tensor_tensor(z, z, acc, ALU.mult).then_inc(s_fth, 1)
                dve.wait_ge(s_ffn, 2 * i + b + 1)
                link(V.scalar_tensor_tensor(z, th, 1.0, acc, ALU.add, ALU.mult))
                dve.wait_ge(s_dnp, DN2 + 2 * i + b)
                V.tensor_tensor(faT[:, b].rearrange("p f n -> p (f n)"), z, ps[:, 5 + 2 * b, :], ALU.mult
                                ).then_inc(s_aT, 1)

            per = 14
            with dve.Fori(0, FP // 2) as i:
                n = link.n
                link.start(i, per)
                feed(i, 0)
                feed(i, 1)
                assert link.n - n == per, link.n - n
            link.end(FP // 2)
            feed(FP // 2, 0)
            dve.wait_ge(s_dnp, DN2 + FP)
            for t in range(NT):
                for half in range(2):
                    cs = slice(512 * half, 512 * (half + 1))
                    V.scalar_tensor_tensor(xs[:, t, cs], ps[:, 2 * t + half, :], 0.5, xs[:, t, cs], ALU.mult, ALU.add
                                           ).then_inc(s_x1, 1)
            final_norm(1, hn)


def constants():
    c = np.zeros((P, NCONST), np.float32)

    def put(name, value):
        lo, hi = CONST[name]
        c[:, lo:hi] = np.asarray(value, np.float32).reshape(-1, hi - lo)

    put("ident", np.eye(P))
    put("ones", np.ones((P, P)))
    p = np.arange(P)
    put("tri", p[:, None] <= p[None, :])
    inv = np.float32(1.0) / (np.float32(10000.0) ** (np.arange(0, ROPE, 2, dtype=np.float32) / np.float32(ROPE)))
    ang = (np.arange(T, dtype=np.float32)[:, None] * inv[None, :]).T.astype(np.float32)
    put("cos", np.tile(np.cos(ang), (4, 1)))
    put("sin", np.concatenate([-np.sin(ang), np.sin(ang)] * 2, 0))
    q = np.concatenate([np.repeat(p[:, None], P, 1), np.repeat(P + p[:, None], T, 1)], 1)
    k = np.concatenate([np.repeat(p[None, :], P, 0), np.repeat(np.arange(T)[None, :], P, 0)], 1)
    put("chunk", np.where(k // 64 <= q // 64, 0.0, NEG))
    d = q - k
    put("causal", np.where(d >= 0, 0.0, NEG))
    put("dist", np.where(d >= 0, -d, NEG))
    put("dil", np.concatenate([np.where((d >= 0) & (d <= w) & (d % r == 0), -d, NEG)
                               for w, r in zip(DILW, DILR)], 1))
    end = np.arange(NC) * CS + CB - 1
    tok = (np.arange(NT)[None, :] * P + p[:, None])[:, :, None, None]
    seen = np.broadcast_to(end <= tok, (P, NT, NSAH, NC))
    slope = np.float32(NSA_SLOPE)[None, None, :, None]
    put("cbias", np.where(seen, -slope * (tok - end).astype(np.float32), np.float32(NEG)))
    put("cmask", seen)
    put("rank4", np.arange(NG, 0, -1)[None, :])
    put("rank8", np.arange(EG, 0, -1)[None, :])
    return c


def kernel(**inputs):
    import concourse.bacc as bacc
    from concourse.bass_utils import run_bass_kernel_spmd

    a = {k: np.asarray(x) for k, x in inputs.items()}

    def chunks(w):
        w = np.asarray(w)
        return w.reshape(w.shape[0] // P, P, -1).transpose(1, 0, 2)

    def flat(w):
        return chunks(w).reshape(P, -1)

    w1 = a["w_in"][0]
    o = np.cumsum([0, 512, 512, 1024, 1024, 4, 4, 384, 256, 64, 2048])
    qm, km, vm, om, im, fm, cq, ckv, kr, gp = (w1[:, o[i]:o[i + 1]] for i in range(10))
    uq = a["w_uq"][0].reshape(QL, AH, NOPE + ROPE)
    ukv = a["w_ukv"][0].reshape(KVL, AH, NOPE + VH)
    tiles = {"cq": np.concatenate([cq, im, fm], 1), "ckr": np.concatenate([ckv, kr, kr], 1), "qk0": qm, "qk1": km,
             "uqn": uq[:, :, :NOPE].reshape(QL, -1), "uqr": uq[:, :, NOPE:].reshape(QL, -1),
             "ukv": np.concatenate([ukv[:, :, :NOPE].reshape(KVL, -1), ukv[:, :, NOPE:].reshape(KVL, -1)], 1)}

    def halves(name, w):
        for i in range(w.shape[1] // 512):
            tiles[f"{name}{i}"] = w[:, 512 * i:512 * (i + 1)]

    for name, w in (("v", vm), ("o", om), ("g", gp), ("bm", a["w_branch_m"][0]), ("ba", a["w_branch_a"][0]),
                    ("out", a["w_out"][0])):
        halves(name, w)
    wa = np.ascontiguousarray(np.concatenate([flat(tiles[n]) for n, _, _ in LOADS], 1))

    w2, b2 = a["w_in_2"][0], a["b_in_2"][0]
    o2 = np.cumsum([0, 256, 256, 256, 4, 384, 384, 384, 384, 128, 128, 128, 128, 128, 128, 18, 3072])
    names = ("qa", "ka", "va", "fa", "qb", "kb", "vb", "qc", "kc", "vc", "ksl", "vsl", "kwn", "vwn", "gc", "gates")
    c2 = {n: w2[:, o2[i]:o2[i + 1]] for i, n in enumerate(names)}
    d2 = {n: b2[o2[i]:o2[i + 1]] for i, n in enumerate(names)}

    def pairs(w):
        return w.reshape(*w.shape[:-1], KVG, 3, HD).swapaxes(-3, -2).reshape(*w.shape)

    tiles.update({"fox": np.concatenate([c2["qa"], c2["ka"]], 1), "dilq": c2["qb"], "dilk": c2["kb"],
                  "nsaq": pairs(c2["qc"]), "kcvw": np.concatenate([c2["kc"], c2["vc"]], 1),
                  "kk": np.concatenate([c2["ksl"], c2["kwn"], c2["gc"], c2["fa"]], 1),
                  "vv": np.concatenate([c2["va"], c2["vsl"], c2["vwn"]], 1), "vb": c2["vb"],
                  "ck": a["cmp_k_w1_2"][0], "cv": a["cmp_v_w1_2"][0]})
    pc = a["w_pc_2"][0].reshape(KVG, 3, HD, D).swapaxes(0, 1).reshape(-1, D)
    for name, w in (("h", c2["gates"]), ("pa", a["w_pa_2"][0]), ("pb", a["w_pb_2"][0]), ("pc", pc),
                    ("wo", a["w_o_2"][0])):
        halves(name, w)
    wb = np.ascontiguousarray(np.concatenate([flat(tiles[n]) for n, _, _ in LOADS2], 1))

    def triple(gate, up, dn):
        n = gate.shape[0]
        gu = [w.reshape(n, KD, P, DE).transpose(0, 2, 1, 3).reshape(n, P, -1) for w in (gate, up)]
        dn = dn.reshape(n, 2, P, D).transpose(0, 2, 1, 3).reshape(n, P, -1)
        return np.ascontiguousarray(np.concatenate(gu + [dn], 2))

    experts = triple(a["w_expert_gate"][0], a["w_expert_up"][0], a["w_expert_down"][0])
    up = a["w_up_2"][0]
    ffn = triple(up[:, :DFF].reshape(D, FP, DE).swapaxes(0, 1), up[:, DFF:].reshape(D, FP, DE).swapaxes(0, 1),
                 a["w_down_2"][0].reshape(FP, DE, D))
    mod = np.ascontiguousarray(a["mod_w"][0].reshape(KD, P, 12, 512).transpose(2, 1, 0, 3).reshape(12, P, -1))

    vecs = np.zeros((P, NVEC), np.float32)

    def put(name, value, rows=P):
        lo, hi = VEC[name]
        vecs[:rows, lo:hi] = np.asarray(value).reshape(rows, hi - lo)

    def col(x):
        return np.asarray(x).reshape(-1, P).T

    mb = a["mod_b"][0]
    put("c", col(a["c"][0]))
    put("mod1", col(mb[:2048]))
    put("mod2", col(mb[3072:5120]))
    for name, key in (("g1", "norm1_g"), ("g2", "norm2_g"), ("g3", "norm1_g_2"), ("g4", "norm2_g_2"),
                      ("convb", "conv_b"), ("qg", "q_norm_g"), ("kvg", "kv_norm_g")):
        put(name, col(a[key][0]))
    put("convw", a["conv_w"][0].reshape(CONV, 8, P).transpose(2, 1, 0))
    put("ib", a["igate_b"][0], MH)
    put("fb", a["fgate_b"][0], MH)
    put("b2f", col(np.concatenate([d2["qa"], d2["ka"], d2["qb"], d2["kb"], pairs(d2["qc"]), d2["kc"], d2["vc"],
                                   d2["ksl"], d2["kwn"]])))
    put("fab", d2["fa"], FOXH)
    put("conv2", np.concatenate([a["conv_w_2"][0], a["conv_b_2"]], 0).reshape(4, FB, P).transpose(2, 1, 0))
    put("pe", a["cmp_pe_2"][0].reshape(CB // 2, P).T)
    put("w2k", flat(a["cmp_k_w2_2"][0]))
    put("w2v", flat(a["cmp_v_w2_2"][0]))
    put("router", flat(np.concatenate([a["w_group"][0], a["w_router"][0]], 1)))
    rows = np.concatenate([mb[2048:3072], mb[5120:], a["final_norm_g"], a["final_g_2"], a["b_group"][0],
                           a["b_router"][0], d2["va"], d2["vsl"], d2["vwn"], d2["vb"], d2["gc"], d2["gates"]])[None, :]
    assert rows.shape[1] == NROW

    arrays = {"x": np.ascontiguousarray(a["x"]), "consts": constants(), "vecs": vecs,
              "rows": np.ascontiguousarray(rows), "mod": mod, "wa": wa, "experts": experts, "wb": wb, "ffn": ffn}
    nc = bacc.Bacc("TRN2", target_bir_lowering=False, num_devices=1)
    args = [nc.dram_tensor(f"in_{k}_dram", v.shape, F32, kind="ExternalInput").ap() for k, v in arrays.items()]
    out = nc.dram_tensor("out_dram", (1, T, D), F32, kind="ExternalOutput").ap()
    build(nc, *args, out)
    r = run_bass_kernel_spmd(nc, [{f"in_{k}_dram": v for k, v in arrays.items()}], core_ids=[0])
    return r.results[0]["out_dram"]
```

```python
from contextlib import ExitStack

import numpy as np

import concourse.bass as bass
from concourse import mybir

F32 = mybir.dt.float32
F32R = mybir.dt.float32r
BF16 = mybir.dt.bfloat16
ALU = mybir.AluOpType
ACT = mybir.ActivationFunctionType
AX = mybir.AxisListType

GELU = 0.7978845608028654
P = 128
RAW = 648
T, D = 256, 1024
NT, KD = T // P, D // P
EPS = 1e-6
NEG = -1e30
TINY = 1e-30
MH, MQK, MV = 4, 128, 256
AH, QL, KVL, NOPE, ROPE, VH = 8, 384, 256, 128, 64, 128
CONV = 4
NG, EG, NE, DE = 4, 8, 32, 256
HD = 64
FOXH, DILH, NSAH, KVG = 4, 6, 6, 2
DILW, DILR = (128, 512, 2048), (1, 4, 16)
CB, CS, CH = 32, 16, 256
NC = (T - CB) // CS + 1
DFF, FB = 2816, 2816 // 128
FP = FB // 2

SPAN = P + T


def columns(sizes):
    at, out = 0, {}
    for name, n in sizes:
        out[name] = (at, at + n)
        at += n
    return out, at


CONST, NCONST = columns([
    ("ident", P), ("ones", P), ("tri", P), ("cos", T), ("sin", T), ("chunk", SPAN), ("causal", SPAN),
    ("dist", SPAN), ("dil", 3 * SPAN), ("cbias", NT * NSAH * NC), ("cmask", NT * NSAH * NC), ("rank4", NG), ("rank8", EG)])
VEC, NVEC = columns([
    ("c", KD), ("mod1", 16), ("mod2", 16), ("g1", KD), ("g2", KD), ("g3", KD), ("g4", KD), ("convw", 8 * CONV),
    ("convb", 8), ("qg", 3), ("kvg", 2), ("ib", 1), ("fb", 1), ("b2f", 17), ("fab", 1), ("conv2", FB * 4),
    ("pe", CB // 2), ("w2k", 2 * HD), ("w2v", 2 * HD), ("router", KD * (NG + NE))])
ROW, NROW = columns([("gate1", D), ("gate2", D), ("final1", D), ("final2", D), ("brouter", NG + NE),
                     ("b2v", 512), ("b2vb", 384), ("b2gc", 3 * NSAH), ("b2g", 3 * D)])

LOADS = [("cq", KD, QL + 2 * MH), ("ckr", KD, KVL + P), ("qk0", KD, 512), ("qk1", KD, 512), ("v0", KD, 512),
         ("v1", KD, 512), ("o0", KD, 512), ("o1", KD, 512), ("uqn", 3, 1024), ("uqr", 3, 512), ("ukv", 2, 2048),
         ("g0", KD, 512), ("g1", KD, 512), ("g2", KD, 512), ("g3", KD, 512),
         ("bm0", KD, 512), ("bm1", KD, 512), ("ba0", KD, 512), ("ba1", KD, 512), ("out0", KD, 512), ("out1", KD, 512)]
LOADS2 = [("fox", KD, 512), ("dilq", KD, 384), ("dilk", KD, 384), ("nsaq", KD, 384), ("kcvw", KD, 256),
          ("kk", KD, 256 + 3 * NSAH + FOXH), ("vv", KD, 512), ("vb", KD, 384),
          ("h0", KD, 512), ("h1", KD, 512), ("h2", KD, 512), ("h3", KD, 512), ("h4", KD, 512), ("h5", KD, 512),
          ("pa0", 2, 512), ("pa1", 2, 512), ("pb0", 3, 512), ("pb1", 3, 512), ("pc0", 3, 512), ("pc1", 3, 512),
          ("wo0", KD, 512), ("wo1", KD, 512)]
LOADS3 = [("ck", 16, CH), ("cv", 16, CH)]
SLOT = max(c * n for _, c, n in LOADS + LOADS2)
BIG = 21240
W3 = KD * DE
GU, DN = 2 * KD * DE, 2 * D


class Chain:

    def __init__(self, eng, sem):
        self.eng, self.sem, self.n, self.loop = eng, sem, 0, None

    def __call__(self, ins):
        self.n += 1
        ins.then_inc(self.sem, 1)
        self.eng.wait_ge(self.sem, self.n if self.loop is None else self.loop + self.n)

    def start(self, i, per):
        self.loop, self.per = i * per, per

    def end(self, trips):
        self.n += self.per * (trips - 1)
        self.loop = None


def units():
    out = [("fox", (h,)) for h in range(FOXH)]
    out += [("dil", tuple(2 * g + p for g in range(3))) for p in range(2)]
    for h in range(NSAH):
        out += [("sel", (h,)), ("win", (h,))]
    return out


UNITS1 = [("mla", (h,)) for h in range(AH)]
UNITS2 = units()
DIL_SLOPE = [2.0 ** (-8.0 * (2 * h + 1) / 12) for h in range(DILH)]
NSA_SLOPE = [2.0 ** (-8.0 * (2 * h + 2) / 12) for h in range(NSAH)]


def build(nc, routing, x, consts, vecs, rows, mod, wa, experts, wb, ffn, out):
    with ExitStack() as ctx:
        def sb(name, *shape, dt=F32):
            return ctx.enter_context(nc.sbuf_tensor(name, [P, *shape], dt))

        def here():
            return -(-nc.sbuf_base // 32) * 32

        def sem(name):
            return ctx.enter_context(nc.semaphore(name))

        ring_at = here()
        ring = sb("ring", 2, SLOT)
        dring_at = here()
        dring = sb("dring", 2, DN)
        cst = sb("cst", NCONST)
        vec = sb("vec", NVEC)
        xs = sb("xs", NT, D)
        hn = sb("hn", NT, D)
        hT_at = here()
        hT = sb("hT", KD, T)
        gateb_at = here()
        gateb = sb("gateb", 2, D)
        modT = sb("modT", 48)
        finalb = sb("finalb", D)
        small = sb("small", 512)
        att = sb("att", 2, 3, SPAN)
        pT = sb("pT", 3, SPAN)
        zero = sb("zero", 512, dt=BF16)
        big_at = here()
        big = sb("big", BIG)

        def const(name, a=0, b=None):
            lo, hi = CONST[name]
            return cst[:, lo + a:(hi if b is None else lo + b)]

        def v(name, a=0, b=None):
            lo, hi = VEC[name]
            return vec[:, lo + a:(hi if b is None else lo + b)]

        def row(name, a=0, b=None):
            lo, hi = ROW[name]
            return rows[0:1, lo + a:(hi if b is None else lo + b)].partition_broadcast(P)

        ident = const("ident")
        ones = const("ones")

        place = {}

        def part(name, at, *shape):
            n = int(np.prod(shape))
            place[name] = (at, at + n)
            assert at + n <= BIG, name
            ap = big[:, at:at + n]
            if len(shape) == 2:
                return ap.rearrange("p (a b) -> p a b", a=shape[0])
            if len(shape) == 3:
                return ap.rearrange("p (a b c) -> p a b c", a=shape[0], b=shape[1])
            return ap

        def after(name):
            return place[name][1]

        qkT = part("qkT", 0, 8, T)
        vaug = part("vaug", after("qkT"), NT, MH, MV + 1)
        og = part("og", after("vaug"), NT, D)
        qnT = part("qnT", after("og"), AH, T)
        qrT = part("qrT", after("qnT"), AH // 2, T)
        knT = part("knT", after("qrT"), AH, T)
        krT = part("krT", after("knT"), T)
        va = part("va", after("krT"), NT, D)
        ya = part("ya", after("va"), KD, T)
        wmem = part("wmem", after("ya"), 2 * SPAN)
        mpart = part("mpart", after("wmem"), 2, 512)
        lst = part("lst", after("wmem"), 8, T)
        ym = part("ym", place["qkT"][0], KD, T)
        merged = part("merged", place["va"][0], NT, D)
        mtile = [part("mtile0", place["qnT"][0], KD, 512), part("mtile1", place["qnT"][0] + KD * 512, KD, 512)]
        assert after("mtile1") <= after("ya")
        gates = dring[:, :, :].rearrange("p a b -> p (a b)").rearrange("p (t n) -> p t n", t=NT)
        dflat = dring[:, :, :].rearrange("p a b -> p (a b)")
        raw = dflat[:, 0:NT * RAW].rearrange("p (t n) -> p t n", t=NT)
        cT = dflat[:, NT * RAW:NT * RAW + 5 * T].rearrange("p (c n) -> p c n", c=5)
        mergedT = hT
        hflat = hn[:, :, :].rearrange("p t n -> p (t n)")
        aflat = att[:, :, :, :].rearrange("p a b c -> p (a b c)")
        rt = aflat[:, 0:1024]
        tmp = pT[:, :, :].rearrange("p a b -> p (a b)")[:, 0:2 * 2 * T].rearrange("p (b n) -> p b n", b=2)
        act32 = hflat[:, 0:2 * T]
        wbe = hflat[:, 2 * T:4 * T].rearrange("p (b n) -> p b n", b=2)

        def split(name, at, *shape):
            assert at + int(np.prod(shape)) <= BIG
            return nc.alloc_sbuf_tensor_at(name, [P, *shape], F32R, offset=big_at + 4 * at)

        wsp = split("wsp", 0, 3, 2, W3)
        hTs = split("hTs", 6 * W3, 2, KD, T)
        aTs = split("aTs", 6 * W3 + 2 * KD * T, 2, 2, 2, T)
        fmT = part("fmT", 0, 17, T)
        kvc = part("kvc", after("fmT"), 2, CB // 2, KVG * NC)
        tv = part("tv", after("kvc"), NT, 512)
        tvb = part("tvb", after("tv"), NT, 384)
        gc = part("gc", after("tvb"), NT, 3 * NSAH)
        g2 = part("g2", after("gc"), NT, 3 * D)
        hidT = part("hidT", after("g2"), 2, 2, KVG * NC)
        kcT = part("kcT", after("hidT"), KVG * NC)
        vc = part("vc", after("kcT"), KVG, HD)
        pcm = part("pcm", after("vc"), NT * NSAH, NC)
        fox = part("fox", after("pcm"), 4, T)
        gel = part("gel", after("fox"), 4, 2, 2 * KVG * NC)
        bias2 = part("bias2", after("gel"), NROW - ROW["b2v"][0])
        yT2 = hflat.rearrange("p (c n) -> p c n", c=8)
        pcT = part("pcT", after("bias2"), NSAH, T)
        merged2 = part("merged2", place["fmT"][0], NT, D)
        ckw = big[:, place["g2"][0]:place["g2"][0] + 4096].rearrange("p (c n) -> p c n", c=16)
        cvw = [big[:, place["g2"][0] + 4096:after("g2")].rearrange("p (c n) -> p c n", c=8),
               aflat[:, 0:2048].rearrange("p (c n) -> p c n", c=8)]
        hTh = nc.alloc_sbuf_tensor_at("hTh", [P, KD, T], F32R, offset=gateb_at)
        hTl = nc.alloc_sbuf_tensor_at("hTl", [P, KD, T], F32R, offset=hT_at)
        wh = nc.alloc_sbuf_tensor_at("wh", [P, 4, 1024], F32R, offset=dring_at)
        wl = nc.alloc_sbuf_tensor_at("wl", [P, 2, SLOT], F32R, offset=ring_at)
        ft = hflat.rearrange("p (a n) -> p a n", a=4)

        ps = ctx.enter_context(nc.psum_tensor("ps", [P, 8, 512], F32))

        s_const, s_x, s_brow, s_final1, s_final2, s_bias2, s_out = (
            sem(n) for n in ("s_const", "s_x", "s_brow", "s_final1", "s_final2", "s_bias2", "s_out"))
        s_ring = [sem("s_ring0"), sem("s_ring1")]
        s_gu = [sem("s_gu0"), sem("s_gu1")]
        s_dn = [sem("s_dn0"), sem("s_dn1")]
        s_mt = [sem("s_mt0"), sem("s_mt1")]
        s_dnp = sem("s_dnp")
        c_dve, c_act, c_pool = sem("c_dve"), sem("c_act"), sem("c_pool")
        s_cond, s_condt, s_mpart, s_msum, s_mev = (
            sem(n) for n in ("s_cond", "s_condt", "s_mpart", "s_msum", "s_mev"))
        s_ss, s_ms, s_rstd, s_hn, s_tr, s_hTv, s_hTa = (
            sem(n) for n in ("s_ss", "s_ms", "s_rstd", "s_hn", "s_tr", "s_hTv", "s_hTa"))
        s_grp, s_gv, s_ga = sem("s_grp"), sem("s_gv"), sem("s_ga")
        s_conv, s_convt = sem("s_conv"), sem("s_convt")
        s_css, s_cms, s_crs, s_cn, s_ctr, s_cT = (sem(n) for n in ("s_css", "s_cms", "s_crs", "s_cn", "s_ctr", "s_cT"))
        s_lf, s_le, s_scan, s_em, s_gt, s_gte = (sem(n) for n in ("s_lf", "s_le", "s_scan", "s_em", "s_gt", "s_gte"))
        s_mS, s_mw, s_mexp, s_mst, s_mnum, s_mr, s_mh, s_my = (
            sem(n) for n in ("s_mS", "s_mw", "s_mexp", "s_mst", "s_mnum", "s_mr", "s_mh", "s_my"))
        s_sc, s_sfree, s_nm, s_exp, s_p, s_pt, s_pTc, s_pv, s_y = (
            sem(n) for n in ("s_sc", "s_sfree", "s_nm", "s_exp", "s_p", "s_pt", "s_pTc", "s_pv", "s_y"))
        s_yt, s_ymT = sem("s_yt"), sem("s_ymT")
        s_br, s_mrg, s_mt2, s_mT, s_pr, s_x1 = (sem(n) for n in ("s_br", "s_mrg", "s_mt2", "s_mT", "s_pr", "s_x1"))
        s_lg, s_re, s_rx, s_w32, s_wt, s_wtc, s_wst = (
            sem(n) for n in ("s_lg", "s_re", "s_rx", "s_w32", "s_wt", "s_wtc", "s_wst"))
        s_wb = [sem("s_wb0"), sem("s_wb1")]
        s_hi = [sem("s_hi_gate"), sem("s_hi_up"), sem("s_hi_down")]
        s_lo = [sem("s_lo_gate"), sem("s_lo_up"), sem("s_lo_down")]
        s_gate = sem("s_gate")
        s_hs = sem("s_hs")
        s_hsh = sem("s_hsh")
        s_qh, s_ql, s_qu = sem("s_qh"), sem("s_ql"), sem("s_qu")
        s_cw = [sem("s_cw0"), sem("s_cw1")]
        s_gup, s_th, s_aT, s_a2 = (sem(n) for n in ("s_gup", "s_th", "s_aT", "s_a2"))
        s_xf, s_fss, s_fms, s_frs = (sem(n) for n in ("s_xf", "s_fss", "s_fms", "s_frs"))
        s_F, s_hid, s_hz, s_hu, s_hth, s_hg, s_kc, s_kce = (
            sem(n) for n in ("s_F", "s_hid", "s_hz", "s_hu", "s_hth", "s_hg", "s_kc", "s_kce"))
        s_cs, s_ce, s_cx, s_cp, s_cpt, s_cpc = (sem(n) for n in ("s_cs", "s_ce", "s_cx", "s_cp", "s_cpt", "s_cpc"))
        s_fl, s_fsc, s_zero = sem("s_fl"), sem("s_fsc"), sem("s_zero")
        s_ggu, s_fsq, s_fz, s_fth, s_ffn = (sem(n) for n in ("s_ggu", "s_fsq", "s_fz", "s_fth", "s_ffn"))
        s_fe, s_gct = sem("s_fe"), sem("s_gct")

        ALL = LOADS + LOADS2
        NL = {name: n for n, (name, _, _) in enumerate(ALL)}
        offs = {}
        for stream in (LOADS, LOADS2 + LOADS3):
            at = 0
            for name, c, n in stream:
                offs[name] = (at, c * n)
                at += c * n

        def wtile(name):
            n = NL[name]
            _, c, m = ALL[n]
            return ring[:, n % 2, 0:c * m].rearrange("p (c n) -> p c n", c=c)

        def landed(eng, name):
            n = NL[name]
            eng.wait_ge(s_ring[n % 2], 16 * (n // 2 + 1))

        GROUPS = [("misc0", "a"), ("misc1", "a"), ("ckv", "a"), ("kr", "v"), ("qk0", "v"), ("qk1", "v"), ("qk2", "v"),
                  ("qk3", "v")] + [(f"v{i}", "a") for i in range(4)] + [(f"o{i}", "a") for i in range(4)]
        GROUPS += [(f"qn{i}", "a") for i in range(4)] + [("qr0", "v"), ("qr1", "v")]
        GROUPS += [(f"kn{i}", "a") for i in range(4)] + [(f"va{i}", "v") for i in range(4)]
        GROUPS += [(f"g{i}", "a") for i in range(8)]
        NG1 = len(GROUPS)
        GROUPS += [("fox0", "v"), ("fox1", "a"), ("dil0", "v"), ("dil1", "v"), ("dil2", "a"), ("dil3", "a"),
                   ("nsa0", "v"), ("nsa1", "v"), ("kcv", "v"), ("kk", "a"), ("gf", "v"), ("vv0", "v"), ("vv1", "v"),
                   ("vb0", "v"), ("vb1", "v")]
        GROUPS += [(f"h{i}", "v") for i in range(12)]
        VGROUPS = sum(1 for g in GROUPS if g[1] == "v")
        GI = {name: n for n, (name, _) in enumerate(GROUPS)}

        SPLIT = [("fox", ("fox0", "fox1")), ("dilq", ("dil0", "dil1")), ("dilk", ("dil2", "dil3")),
                 ("nsaq", ("nsa0", "nsa1")), ("kcvw", ("kcv",)), ("kk", ("kk", "gf")), ("vv", ("vv0", "vv1")),
                 ("vb", ("vb0", "vb1"))] + [(f"h{q}", (f"h{2 * q}", f"h{2 * q + 1}")) for q in range(6)]
        LH = 8

        def quarter(name, q, buf):
            _, c, n = ALL[NL[name]]
            if buf is wh:
                return wh[:, q, 0:2 * n]
            return buf[:, NL[name] % 2, 2 * q * n:2 * (q + 1) * n]

        GM = 2
        HM = 4
        BANK = {name: n % 4 for n, (name, _) in enumerate(GROUPS)}
        BANK.update({f"g{i}": 7 - 3 * i if i < GM else 5 - 3 * (i % 2) for i in range(8)})
        BANK.update({f"h{i}": (0, 1, 2, 0)[i] if i < HM else 5 - 3 * (i % 2) for i in range(12)})

        def bank(name):
            return ps[:, BANK[name], :]

        def emptied(eng, n):
            who = GROUPS[n][1]
            count = sum(1 for g in GROUPS[:n + 1] if g[1] == who)
            eng.wait_ge(s_ga if who == "a" else s_gv, count)

        def grouped(eng, name):
            eng.wait_ge(s_grp, GI[name] + 1)

        USED = {"cq": "misc1", "ckr": "kr", "qk0": "qk1", "qk1": "qk3", "v0": "v1", "v1": "v3", "uqn": "qn3",
                "uqr": "qr1", "ukv": "va3", "o0": "o1", "o1": "o3", "fox": "fox1", "dilq": "dil1", "dilk": "dil3",
                "nsaq": "nsa1", "kcvw": "kcv", "kk": "gf", "vv": "vv1", "vb": "vb1"}
        USED.update({f"g{q}": f"g{2 * q + 1}" for q in range(4)})
        USED.update({f"h{q}": f"h{2 * q + 1}" for q in range(6)})
        USED = {name: (s_grp, GI[g] + 1) for name, g in USED.items()}
        for n, name in enumerate(("bm0", "bm1", "ba0", "ba1", "pa0", "pa1", "pb0", "pb1", "pc0", "pc1")):
            USED[name] = (s_br, 2 * (n + 1))
        for n, name in enumerate(("out0", "out1", "wo0", "wo1")):
            USED[name] = (s_pr, 2 * (n + 1))

        def used(eng, n):
            eng.wait_ge(*USED[ALL[n][0]])

        DN2 = NE + 2

        NMOD = 12
        block = ctx.enter_context(nc.Block())

        @block.sync
        def _(sp):
            sp.dma_start(vec[:, :], vecs).then_inc(s_const, 16)
            sp.dma_start(cst[:, :], consts).then_inc(s_const, 16)

            def mod_tile(j):
                if j >= 2:
                    sp.wait_ge(s_mpart, j - 1)
                sp.dma_start(mtile[j % 2], mod[j].rearrange("p (c n) -> p c n", c=KD)).then_inc(s_mt[j % 2], 16)

            def load(name, stream):
                n = NL[name]
                if n >= 2:
                    used(sp, n - 2)
                at, size = offs[name]
                sp.dma_start(ring[:, n % 2, 0:size], stream[:, at:at + size]).then_inc(s_ring[n % 2], 16)

            mod_tile(0)
            mod_tile(1)
            sp.dma_start(xs[:, :, :], x.rearrange("b (t p) d -> p (b t) d", p=P)).then_inc(s_x, 16)
            sp.dma_start(gateb[:, 0, :], row("gate1")).then_inc(s_brow, 16)
            sp.dma_start(gateb[:, 1, :], row("gate2")).then_inc(s_brow, 16)
            mod_tile(2)
            mod_tile(3)
            load("cq", wa)
            load("ckr", wa)
            mod_tile(4)
            mod_tile(5)
            load("qk0", wa)
            mod_tile(6)
            load("qk1", wa)
            mod_tile(7)
            mod_tile(8)
            load("v0", wa)
            mod_tile(9)
            load("v1", wa)
            mod_tile(10)
            mod_tile(11)
            for name, _, _ in LOADS[6:]:
                load(name, wa)
            sp.dma_start(finalb[:, :], row("final1")).then_inc(s_final1, 16)
            sp.dma_start(small[:, 448:448 + 36], row("brouter")).then_inc(s_final1, 16)

            n0 = len(LOADS)
            for e in range(2):
                used(sp, n0 - 2 + e)
                sp.dma_start(ring[:, (n0 + e) % 2, 0:GU], experts[e, :, 0:GU]).then_inc(s_gu[e], 16)
                if e == 0:
                    sp.wait_ge(s_mrg, 4)
                sp.dma_start(dring[:, e, :], experts[e, :, GU:GU + DN]).then_inc(s_dn[e], 16)
            sp.wait_ge(s_wtc, 1)
            sp.dma_start(routing, rt[0:NE, 384:384 + T]).then_inc(s_wst, 16)
            sp.wait_ge(s_wst, 16)
            for e in range(2):
                sp.dma_start(wbe[:, e, :], routing[e:e + 1, :].partition_broadcast(P)).then_inc(s_wb[e], 16)

            def element(i, b, src, slot0, count0):
                for m in (0, 1):
                    sp.wait_ge(s_lo[m], 2 * i + b + 1 + count0)
                row = src[bass.ds(2 * i + b + 2, 1)]
                sp.dma_start(ring[:, (slot0 + b) % 2, 0:GU], row[:, :, 0:GU].rearrange("a p n -> p (a n)")
                             ).then_inc(s_gu[b], 16)
                sp.wait_ge(s_lo[2], 2 * i + b + 1 + count0)
                sp.dma_start(dring[:, b, :], row[:, :, GU:GU + DN].rearrange("a p n -> p (a n)")
                             ).then_inc(s_dn[b], 16)

            with sp.Fori(0, NE // 2 - 1) as i:
                for b in range(2):
                    element(i, b, experts, n0, 0)
                    sp.wait_ge(s_aT, 2 * i + b + 1)
                    sp.dma_start(wbe[:, b, :], routing[bass.ds(2 * i + b + 2, 1), :].partition_broadcast(P)
                                 ).then_inc(s_wb[b], 16)

            first = True
            for name, _, _ in LOADS2:
                n = NL[name]
                if n - n0 < 2:
                    for m in (0, 1):
                        sp.wait_ge(s_lo[m], NE - 1 + (n - n0))
                else:
                    used(sp, n - 2)
                at, size = offs[name]
                sp.dma_start(ring[:, n % 2, 0:size], wb[:, at:at + size]).then_inc(s_ring[n % 2], 16)
                if first:
                    sp.wait_ge(s_dnp, NE + 1)
                    sp.dma_start(bias2, rows[0:1, ROW["b2v"][0]:NROW].partition_broadcast(P)
                                 ).then_inc(s_bias2, 16)
                    for i, name in enumerate(("ck", "cv")):
                        at, size = offs[name]
                        parts = ((ckw, size),) if i == 0 else ((cvw[0], size // 2), (cvw[1], size // 2))
                        for dst, size in parts:
                            sp.dma_start(dst, wb[:, at:at + size].rearrange("p (c n) -> p c n", n=CH)
                                         ).then_inc(s_cw[i], 16)
                            at += size
                    first = False

            n1 = len(ALL)
            for f in range(2):
                used(sp, n1 - 2 + f)
                sp.dma_start(ring[:, (n1 + f) % 2, 0:GU], ffn[f, :, 0:GU]).then_inc(s_gu[f], 16)
                sp.dma_start(dring[:, f, :], ffn[f, :, GU:GU + DN]).then_inc(s_dn[f], 16)
            sp.wait_ge(s_xf, 2)
            sp.dma_start(finalb[:, :], row("final2")).then_inc(s_final2, 16)
            with sp.Fori(0, FP // 2 - 1) as i:
                for b in range(2):
                    element(i, b, ffn, n1, NE)
            element(FP // 2 - 1, 0, ffn, n1, NE)

            sp.wait_ge(s_xf, 4)
            sp.dma_start(out.rearrange("b (t p) d -> p (b t) d", p=P), hn[:, :, :]).then_inc(s_out, 16)
            sp.wait_ge(s_out, 16)

        @block.tensor
        def _(pe):
            def group_start(name):
                last = [m for m in range(GI[name]) if BANK[GROUPS[m][0]] == BANK[name]]
                if last:
                    emptied(pe, last[-1])

            def mod_sum(j):
                pe.wait_ge(s_mpart, j + 1)
                if j in (4, 5, 6, 10, 11):
                    pe.wait_ge(s_mev, {4: 1, 5: 2, 6: 3, 10: 4, 11: 5}[j])
                pp = mpart[:, j % 2, :]
                if j in (4, 5, 10, 11):
                    mm = pe.matmul(ps[:, 7, :], ones, pp, start=True, stop=True)
                else:
                    col = 4 * j if j < 4 else 4 * (j - 6)
                    for i in range(4):
                        mm = pe.matmul(ps[:, 7, col + i:col + i + 1], pp[:, i * P:(i + 1) * P], ones[:, 0:1],
                                       start=True, stop=True)
                mm.then_inc(s_msum, 1)

            def turn_rows(k):
                pe.wait_ge(s_hn, 2 * (k + 1))
                for c in range(KD):
                    for t in range(NT):
                        mm = pe.transpose(ps[:, c // 2, (c % 2) * T + t * P:(c % 2) * T + (t + 1) * P],
                                          hn[:, t, c * P:(c + 1) * P], ident)
                    if c % 2:
                        mm.then_inc(s_tr, 1)

            def hT_ready(k):
                pe.wait_ge(s_hTv, 4 * (k + 1))
                pe.wait_ge(s_hTa, 4 * (k + 1))

            def feature(name, w, cols, src, nk, out0=0, m=P):
                b = bank(name)
                for j, c0 in enumerate(cols):
                    for c in range(nk):
                        mm = pe.matmul(b[0:m, out0 + j * T:out0 + (j + 1) * T], w[:, c, c0:c0 + m], src[:, c, :],
                                       start=(c == 0), stop=(c == nk - 1))
                return mm

            def token(b, t, w, c0, c1, src, nk, at=0):
                for c in range(nk):
                    mm = pe.matmul(b[:, at:at + c1 - c0], src[:, c, t * P:(t + 1) * P], w[:, c, c0:c1],
                                   start=(c == 0), stop=(c == nk - 1))
                return mm

            pe.wait_ge(s_const, 32)
            for j in range(4):
                mod_sum(j)
            turn_rows(0)
            hT_ready(0)
            landed(pe, "cq")
            w = wtile("cq")
            for t in range(NT):
                mm = token(bank(f"misc{t}"), t, w, 0, QL + 2 * MH, hT, KD).then_inc(s_grp, 1)
            mod_sum(4)
            landed(pe, "ckr")
            w = wtile("ckr")
            b = bank("ckv")
            for t in range(NT):
                mm = token(b, t, w, 0, KVL, hT, KD, at=t * KVL)
            mm.then_inc(s_grp, 1)
            feature("kr", w, [KVL], hT, KD).then_inc(s_grp, 1)
            mod_sum(5)
            for half in range(2):
                landed(pe, f"qk{half}")
                w = wtile(f"qk{half}")
                for i in range(2):
                    name = f"qk{2 * half + i}"
                    group_start(name)
                    mm = feature(name, w, [i * 256, i * 256 + P], hT, KD).then_inc(s_grp, 1)
                    mod_sum(6 + 2 * half + i)

            def token_groups(name, half):
                landed(pe, f"{name}{half}")
                for t in range(NT):
                    group_start(f"{name}{2 * half + t}")
                    token(bank(f"{name}{2 * half + t}"), t, wtile(f"{name}{half}"), 0, 512, hT, KD
                          ).then_inc(s_grp, 1)

            token_groups("v", 0)
            mod_sum(10)
            token_groups("v", 1)
            mod_sum(11)
            token_groups("o", 0)
            token_groups("o", 1)
            pe.wait_ge(s_cn, 2)
            for c in range(5):
                for t in range(NT):
                    at = (c % 2) * T + t * P
                    src = raw[:, t, c * P:(c + 1) * P] if c < 3 else raw[:, t, 392 + (c - 3) * P:392 + (c - 2) * P]
                    pe.transpose(ps[:, 4 + c // 2, at:at + P], src, ident)
            for t in range(NT):
                pe.transpose(ps[0:MH, 6, T + t * P:T + (t + 1) * P], raw[:, t, QL:QL + MH], ident)
            pe.wait_ge(s_mev, 6)
            for t in range(NT):
                mm = pe.transpose(ps[0:MH, 7, t * P:(t + 1) * P], raw[:, t, QL + MH:QL + 2 * MH], ident)
            mm.then_inc(s_ctr, 1)
            pe.wait_ge(s_cT, 1)
            landed(pe, "uqn")
            w = wtile("uqn")
            for i in range(4):
                group_start(f"qn{i}")
                mm = feature(f"qn{i}", w, [2 * i * P, (2 * i + 1) * P], cT, 3).then_inc(s_grp, 1)
            landed(pe, "uqr")
            w = wtile("uqr")
            for i in range(2):
                group_start(f"qr{i}")
                mm = feature(f"qr{i}", w, [2 * i * P, (2 * i + 1) * P], cT, 3).then_inc(s_grp, 1)
            landed(pe, "ukv")
            w = wtile("ukv")
            for i in range(4):
                group_start(f"kn{i}")
                feature(f"kn{i}", w, [2 * i * P, (2 * i + 1) * P], cT[:, 3:5, :], 2).then_inc(s_grp, 1)
            for i in range(4):
                group_start(f"va{i}")
                mm = token(bank(f"va{i}"), i % 2, w, 1024 + 512 * (i // 2), 1536 + 512 * (i // 2), cT[:, 3:5, :], 2)
                mm.then_inc(s_grp, 1)

            def gate_group(i):
                q, t = i // 2, i % 2
                if t == 0:
                    landed(pe, f"g{q}")
                group_start(f"g{i}")
                token(bank(f"g{i}"), t, wtile(f"g{q}"), 0, 512, hT, KD).then_inc(s_grp, 1)

            pe.wait_ge(s_scan, 1)
            pe.wait_ge(s_em, 1)
            for t in range(NT):
                pe.transpose(ps[:, 4, t * MH:(t + 1) * MH], lst[0:MH, 2, t * P:(t + 1) * P], ident[0:MH, 0:MH])
                mm = pe.transpose(ps[:, 4, (2 + t) * MH:(3 + t) * MH], lst[0:MH, 5, t * P:(t + 1) * P],
                                  ident[0:MH, 0:MH])
            mm.then_inc(s_gt, 1)
            emptied(pe, GI["kn3"])
            emptied(pe, GI["va3"])

            def m_scores(h):
                if h >= 2:
                    pe.wait_ge(s_mst, h - 1)
                pe.matmul(ps[:, h % 2, 0:T], ident[0:MH, h:h + 1].to_broadcast([MH, P]), lst[0:MH, 4, :],
                          start=True, stop=True)
                pe.matmul(ps[:, 2 + h % 2, 0:T], qkT[:, 4 + h, 0:P], qkT[:, h, :], start=True, stop=True)
                pe.matmul(ps[:, 2 + h % 2, T:SPAN], qkT[:, 4 + h, P:T], qkT[:, h, P:T], start=True, stop=True
                          ).then_inc(s_mS, 1)

            def m_values(h):
                pe.wait_ge(s_mst, h + 1)
                if h >= 1:
                    pe.wait_ge(s_mh, 2 * h)
                w = wmem[:, (h % 2) * SPAN:(h % 2 + 1) * SPAN]
                pe.matmul(ps[:, 5, 0:MV + 1], w[:, 0:P], vaug[:, 0, h, :], start=True, stop=True)
                pe.matmul(ps[:, 6, 0:MV + 1], w[:, P:T], vaug[:, 0, h, :], start=True, stop=False)
                pe.matmul(ps[:, 6, 0:MV + 1], w[:, T:SPAN], vaug[:, 1, h, :], start=False, stop=True
                          ).then_inc(s_mnum, 1)

            pe.wait_ge(s_gte, 1)
            for h in range(MH + 1):
                if h < MH:
                    m_scores(h)
                if h in (1, 3):
                    gate_group(h // 2)
                if h >= 1:
                    m_values(h - 1)

            def attention(todo, set0, unit0, out0, scores, value, outputs, finished, fill):
                at = []
                n = set0
                for _, heads in todo:
                    at.append(n)
                    n += len(heads)
                o = out0
                for u in range(len(todo) + 1):
                    if u < len(todo):
                        kind, heads = todo[u]
                        for g, h in enumerate(heads):
                            s = at[u] + g
                            if s - set0 >= 2:
                                pe.wait_ge(s_sfree, s - 1)
                            scores(ps[:, s % 2, 0:SPAN], kind, h).then_inc(s_sc, 1)
                        fill(u)
                    if u >= 1:
                        kind, heads = todo[u - 1]
                        pe.wait_ge(s_p, unit0 + u)
                        for g, h in enumerate(heads):
                            s = at[u - 1] + g
                            if s - set0 >= 2:
                                pe.wait_ge(s_pTc, s - 1)
                            src = att[:, (unit0 + u - 1) % 2, g, :]
                            b = ps[:, 3 + s % 2, :]
                            pe.transpose(b[:, 0:P], src[:, 0:P], ident)
                            pe.transpose(b[:, P:T], src[:, P:T], ident)
                            pe.transpose(b[:, T:SPAN], src[:, T:SPAN], ident).then_inc(s_pt, 1)
                        for g, h in enumerate(heads):
                            s = at[u - 1] + g
                            pe.wait_ge(s_pTc, s + 1)
                            lo, hi = outputs(kind, h)
                            first, last = finished(kind)
                            if first and o - out0 >= 2:
                                pe.wait_ge(s_y, o - 1)
                            dst = ps[lo:hi, 6 + o % 2, :]
                            if first and kind == "sel":
                                pe.matmul(dst[:, 0:T], vc[0:NC, h // 3, :], pcT[0:NC, h, :], start=True, stop=False,
                                          skip_group_check=True)
                            v0, v1 = value(kind, h)
                            pe.matmul(dst[:, 0:T], v0, pT[:, s % 3, 0:T], start=first and kind != "sel", stop=False,
                                      skip_group_check=True)
                            pe.matmul(dst[:, P:T], v1, pT[:, s % 3, T:SPAN], start=False, stop=last,
                                      skip_group_check=True).then_inc(s_pv, 1)
                            if last:
                                o += 1

            def scores1(b, kind, h):
                r = (h % 2) * ROPE
                for lo, q0, n in ((0, 0, P), (P, P, T)):
                    pe.matmul(b[:, lo:lo + n], qnT[:, h, q0:q0 + P], knT[:, h, 0:n], start=True, stop=False)
                    mm = pe.matmul(b[:, lo:lo + n], qrT[r:r + ROPE, h // 2, q0:q0 + P], krT[r:r + ROPE, 0:n],
                                   start=False, stop=True)
                return mm

            pe.wait_ge(s_mw, 2 * MH)
            pe.wait_ge(s_mh, 2 * MH)
            emptied(pe, GI["g1"])
            attention(UNITS1, 0, 0, 0, scores1,
                      lambda kind, h: (va[:, 0, h * VH:(h + 1) * VH], va[:, 1, h * VH:(h + 1) * VH]),
                      lambda kind, h: (0, P), lambda kind: (True, True),
                      lambda u: gate_group(GM + u) if GM + u < 8 else None)
            pe.wait_ge(s_my, 2 * MH)
            pe.wait_ge(s_sfree, AH)
            pe.wait_ge(s_pTc, AH)
            emptied(pe, GI["g7"])
            for c in range(KD):
                for t in range(NT):
                    mm = pe.transpose(ps[:, c // 2, (c % 2) * T + t * P:(c % 2) * T + (t + 1) * P],
                                      og[:, t, c * P:(c + 1) * P], ident)
                if c % 2:
                    mm.then_inc(s_yt, 1)
            pe.wait_ge(s_ymT, 4)
            pe.wait_ge(s_y, AH)
            for br, src in (("bm", ym), ("ba", ya)):
                for half in range(2):
                    landed(pe, f"{br}{half}")
                    w = wtile(f"{br}{half}")
                    for t in range(NT):
                        mm = token(ps[:, (4 if br == "ba" else 0) + 2 * half + t, :], t, w, 0, 512, src, KD
                                   ).then_inc(s_br, 1)

            def turn_merged(k):
                pe.wait_ge(s_mrg, 4 * (k + 1))
                for c in range(KD):
                    for t in range(NT):
                        mm = pe.transpose(ps[:, c // 2, (c % 2) * T + t * P:(c % 2) * T + (t + 1) * P],
                                          (merged if k == 0 else merged2)[:, t, c * P:(c + 1) * P], ident)
                    if c % 2:
                        mm.then_inc(s_mt2, 1)
                pe.wait_ge(s_mT, 4 * (k + 1))

            def project_out(k, name):
                for half in range(2):
                    landed(pe, f"{name}{half}")
                    w = wtile(f"{name}{half}")
                    for t in range(NT):
                        mm = token(ps[:, 4 + 2 * half + t, :], t, w, 0, 512, mergedT, KD).then_inc(s_pr, 1)

            turn_merged(0)
            project_out(0, "out")
            turn_rows(1)
            hT_ready(1)
            wr = v("router").rearrange("p (c n) -> p c n", c=KD)
            for t in range(NT):
                mm = token(ps[:, 0, :], t, wr, 0, NG + NE, hT, KD, at=t * (NG + NE))
            mm.then_inc(s_lg, 1)

            def prod(out, w, x, start, stop, skip=False):
                for n, (a, b) in enumerate(((0, 0), (0, 1), (1, 0))):
                    mm = pe.matmul(out, w[a], x[b], start=start and n == 0, stop=stop and n == 2,
                                   skip_group_check=skip)
                return mm

            def gate_or_up(m, pb, count):
                pe.wait_ge(s_lo[m], count)
                w = wsp[:, m, :, :].rearrange("p s (c n) -> p s c n", c=KD)
                for f in range(2):
                    for c in range(KD):
                        mm = prod(ps[:, pb + m, f * T:(f + 1) * T], [w[:, s, c, f * P:(f + 1) * P] for s in range(2)],
                                  [hTs[:, s, c, :] for s in range(2)], c == 0, c == KD - 1)
                mm.then_inc(s_gup if m else s_gate, 1)

            def down(b, count):
                pe.wait_ge(s_lo[2], count)
                w = wsp[:, 2, :, :].rearrange("p s (f n) -> p s f n", f=2)
                for f in range(2):
                    for t in range(NT):
                        for n in range(2):
                            mm = prod(ps[:, 2 * t + n, :], [aTs[:, b, s, f, t * P:(t + 1) * P] for s in range(2)],
                                      [w[:, s, f, n * 512:(n + 1) * 512] for s in range(2)], False, False, True)
                mm.then_inc(s_dnp, 1)

            pe.wait_ge(s_hs, 2)
            gate_or_up(0, 4, 1)
            gate_or_up(1, 4, 1)
            pe.wait_ge(s_w32, 1)
            for t in range(NT):
                mm = pe.transpose(ps[0:NE, 1, t * P:(t + 1) * P], rt[:, 256 + t * NE:256 + (t + 1) * NE], ident)
            mm.then_inc(s_wt, 1)
            pe.wait_ge(s_wtc, 1)

            def open_sums():
                for b in range(4):
                    mm = pe.matmul(ps[:, b, :], zero[:, 0:P], zero[:, :], start=True, stop=False,
                                   skip_group_check=True)
                mm.then_inc(s_dnp, 1)

            pe.wait_ge(s_zero, 1)
            open_sums()

            def stream(count0, total):
                read0 = count0 + 1

                def step(i, b):
                    e = 2 * i + b
                    pb = 6 - 2 * b
                    pe.wait_ge(s_a2, e + read0)
                    gate_or_up(0, pb, e + count0 + 2)
                    gate_or_up(1, pb, e + count0 + 2)
                    pe.wait_ge(s_aT, e + count0 + 1)
                    down(b, e + count0 + 1)

                pairs = (total - 1) // 2
                with pe.Fori(0, pairs) as i:
                    step(i, 0)
                    step(i, 1)
                if 2 * pairs < total - 1:
                    step(pairs, 0)
                pe.wait_ge(s_aT, count0 + total)
                down((total - 1) % 2, count0 + total)

            stream(0, NE)

            turn_rows(2)
            hT_ready(2)

            pe.wait_ge(s_hs, 4)

            def outputs_of(name):
                load = next(n for n, groups in SPLIT if name in groups)
                width = ALL[NL[load]][2]
                hl = (hTh, hTl)

                def weights(c, a, b):
                    return [w.rearrange("p (c n) -> p c n", c=2)[:, c % 2, a:b] for w in
                            (quarter(load, c // 2, wh), quarter(load, c // 2, wl))]

                def tokens_by(t, a, b):
                    return lambda c: ([h[:, c, t * P:(t + 1) * P] for h in hl], weights(c, a, b))

                def features(a, m):
                    return lambda c: (weights(c, a, a + m), [h[:, c, :] for h in hl])

                b = bank(name)
                if load in ("vv", "vb") or load in [f"h{q}" for q in range(6)]:
                    return [(b[:, 0:width], tokens_by(int(name[len(load.rstrip("012345")):]) % 2, 0, width))]
                if name == "gf":
                    out = [(b[:, t * 3 * NSAH:(t + 1) * 3 * NSAH], tokens_by(t, 2 * P, 2 * P + 3 * NSAH))
                           for t in range(NT)]
                    return out + [(b[0:FOXH, T:2 * T], features(2 * P + 3 * NSAH, FOXH))]
                j = dict(SPLIT)[load].index(name)
                last = 2 * P if load == "kk" else width
                return [(b[:, n * T:(n + 1) * T], features(a, P))
                        for n, a in enumerate(range(2 * P * j, min(2 * P * (j + 1), last), P))]

            def split_quarter(n, q):
                load, groups = SPLIT[n]
                pe.wait_ge(s_ql, 4 * n + q + 1)
                for name in groups:
                    if q == 0:
                        group_start(name)
                    for p, (out, operands) in enumerate(outputs_of(name)):
                        for c in (2 * q, 2 * q + 1):
                            for k, (i, j) in enumerate(((0, 0), (0, 1), (1, 0))):
                                x, y = operands(c)
                                mm = pe.matmul(out, x[i], y[j], start=(p, c, k) == (0, 0, 0),
                                               stop=(c, k) == (KD - 1, 2), skip_group_check=True)
                    if q == 3:
                        mm.then_inc(s_grp, 1)
                if q < 3:
                    mm.then_inc(s_qu, 1)

            for n in range(LH):
                for q in range(4):
                    split_quarter(n, q)
            pe.wait_ge(s_F, 1)
            for i in range(2):
                pe.wait_ge(s_cw[i], 16 * (i + 1))
                for m in range(2):
                    for j in range(CB // 2):
                        w = ckw[:, j] if i == 0 else cvw[j // 8][:, j % 8]
                        mm = pe.matmul(ps[:, 4 + i, m * 30:(m + 1) * 30], w[:, m * P:(m + 1) * P], kvc[:, i, j, :],
                                       start=(j == 0), stop=(j == CB // 2 - 1))
                mm.then_inc(s_hid, 1)
            for q in range(4):
                split_quarter(LH, q)
            pe.wait_ge(s_hg, 1)
            w2k = v("w2k").rearrange("p (c n) -> p c n", c=2)
            w2v = v("w2v").rearrange("p (c n) -> p c n", c=2)
            for g in range(KVG):
                for c in range(2):
                    pe.matmul(ps[g * HD:(g + 1) * HD, 6, 0:NC], w2k[:, c, :], hidT[:, 0, c, g * NC:(g + 1) * NC],
                              start=(c == 0), stop=(c == 1))
                for c in range(2):
                    mm = pe.matmul(ps[0:NC, 7, g * HD:(g + 1) * HD], hidT[:, 1, c, g * NC:(g + 1) * NC], w2v[:, c, :],
                                   start=(c == 0), stop=(c == 1))
            mm.then_inc(s_kc, 1)
            split_quarter(LH + 1, 0)
            split_quarter(LH + 1, 1)
            pe.wait_ge(s_kce, 1)
            emptied(pe, GI["vb1"])
            for t in range(NT):
                for h in range(NSAH):
                    g, r = h // 3, h % 3
                    q = fmT[g * HD:(g + 1) * HD, 10 + r, t * P:(t + 1) * P]
                    at = (3 * t + r) * NC
                    mm = pe.matmul(ps[:, 3 + g, at:at + NC], q, kcT[g * HD:(g + 1) * HD, 0:NC], start=True, stop=True)
            mm.then_inc(s_cs, 1)
            split_quarter(LH + 1, 2)
            split_quarter(LH + 1, 3)
            pe.wait_ge(s_cp, 1)
            for h in range(NSAH):
                for t in range(NT):
                    at = (h % 2) * T + t * P
                    mm = pe.transpose(ps[0:NC, 5 + h // 2, at:at + P], pcm[:, t * NSAH + h, :], ident)
            mm.then_inc(s_cpt, 1)
            pe.wait_ge(s_cpc, 3)
            pe.wait_ge(s_fsc, 1)
            emptied(pe, GI["h3"])

            def scores2(b, kind, h):
                if kind == "fox":
                    r, q, k = h % 2, fmT[:, h // 2, :], fmT[:, 2 + h // 2, :]
                elif kind == "dil":
                    r, q, k = h % 2, fmT[:, 4 + h // 2, :], fmT[:, 7 + h // 2, :]
                else:
                    r, q, k = h // 3, fmT[:, 10 + h % 3, :], fmT[:, 15 if kind == "sel" else 16, :]
                r = r * HD
                for lo, q0, n in ((0, 0, P), (P, P, T)):
                    mm = pe.matmul(b[:, lo:lo + n], q[r:r + HD, q0:q0 + P], k[r:r + HD, 0:n], start=True,
                                   stop=kind != "fox")
                    if kind == "fox":
                        mm = pe.matmul(b[:, lo:lo + n], ident[0:FOXH, h:h + 1].to_broadcast([FOXH, P]),
                                       fox[0:FOXH, 3, 0:n], start=False, stop=True)
                return mm

            def value2(kind, h):
                if kind == "fox":
                    return tv[:, 0, h * HD:(h + 1) * HD], tv[:, 1, h * HD:(h + 1) * HD]
                if kind == "dil":
                    return tvb[:, 0, h * HD:(h + 1) * HD], tvb[:, 1, h * HD:(h + 1) * HD]
                at = (256 if kind == "sel" else 384) + (h // 3) * HD
                return tv[:, 0, at:at + HD], tv[:, 1, at:at + HD]

            def outputs2(kind, h):
                r = h // 3 if kind in ("sel", "win") else h % 2
                return r * HD, (r + 1) * HD

            attention(UNITS2, AH, AH, AH, scores2, value2, outputs2,
                      lambda kind: (kind != "win", kind != "sel"),
                      lambda u: split_quarter(LH + 2 + u // 4, u % 4) if u < 16 else None)
            pe.wait_ge(s_y, AH + FOXH + DILH + NSAH)
            for i, (br, c0, nk) in enumerate((("pa", 0, 2), ("pb", 2, 3), ("pc", 5, 3))):
                for half in range(2):
                    landed(pe, f"{br}{half}")
                    w = wtile(f"{br}{half}")
                    for t in range(NT):
                        if i == 2:
                            pe.wait_ge(s_gv, VGROUPS + 2 * half + t + 1)
                        mm = token(ps[:, 4 * (i % 2) + 2 * half + t, :], t, w, 0, 512, yT2[:, c0:c0 + nk, :], nk
                                   ).then_inc(s_br, 1)
            turn_merged(1)
            project_out(1, "wo")
            turn_rows(3)
            hT_ready(3)
            pe.wait_ge(s_hs, 6)
            gate_or_up(0, 4, NE + 1)
            gate_or_up(1, 4, NE + 1)
            open_sums()
            stream(NE, FP)

        @block.scalar
        def _(act):
            link = Chain(act, c_act)
            act.wait_ge(s_const, 32)
            nc.scalar.activation(small[:, 0:KD], v("c"), ACT.Tanh, scale=0.5).then_inc(s_condt, 1)

            def row_squares(k):
                for t in range(NT):
                    link(nc.scalar.activation(hn[:, t, :], xs[:, t, :], ACT.Square,
                                              accum_out=small[:, 16 + t:17 + t]))
                act.nop().then_inc(s_ss, 1)

            def hT_half(k, scale, shift):
                for c in range(4):
                    if c % 2 == 0:
                        act.wait_ge(s_tr, 4 * k + c // 2 + 1)
                    src = ps[:, c // 2, (c % 2) * T:(c % 2 + 1) * T]
                    if shift is None:
                        nc.scalar.activation(hT[:, c, :], src, ACT.Copy, scale=scale[:, c:c + 1]).then_inc(s_hTa, 1)
                    else:
                        nc.scalar.activation(hT[:, c, :], src, ACT.Identity, scale=scale[:, c:c + 1],
                                             bias=shift[:, c:c + 1]).then_inc(s_hTa, 1)

            act.wait_ge(s_x, 16)
            row_squares(0)
            act.wait_ge(s_mev, 1)
            hT_half(0, modT[:, 32:40], modT[:, 0:8])
            for t in range(NT):
                grouped(act, f"misc{t}")
                nc.scalar.copy(raw[:, t, 0:392], bank(f"misc{t}")[:, 0:392]).then_inc(s_ga, 1)
            grouped(act, "ckv")
            for t in range(NT):
                ins = nc.scalar.copy(raw[:, t, 392:RAW], bank("ckv")[:, t * KVL:(t + 1) * KVL])
            ins.then_inc(s_ga, 1)
            act.wait_ge(s_ga, 3)
            for t in range(NT):
                link(nc.scalar.activation(att[:, 0, 0, :], raw[:, t, 0:QL], ACT.Square,
                                          accum_out=small[:, 20 + t:21 + t]))
                link(nc.scalar.activation(att[:, 0, 0, 0:KVL], raw[:, t, 392:RAW], ACT.Square,
                                          accum_out=small[:, 22 + t:23 + t]))
            act.nop().then_inc(s_css, 1)
            for i in range(4):
                act.wait_ge(s_conv, i + 1)
                nc.scalar.activation(att[:, 1, 0:2, 0:T], hn[:, i % 2, 0:512].rearrange("p (a b) -> p a b", a=2), ACT.Tanh,
                                     scale=0.5).then_inc(s_convt, 1)
                if i < 3:
                    act.wait_ge(s_gv, i + 2)

            for i in range(4):
                grouped(act, f"v{i}")
                src = bank(f"v{i}").rearrange("p (h d) -> p h d", h=2)
                nc.scalar.copy(vaug[:, i % 2, 2 * (i // 2):2 * (i // 2) + 2, 0:MV], src).then_inc(s_ga, 1)
            for i in range(4):
                grouped(act, f"o{i}")
                nc.scalar.activation(og[:, i % 2, 512 * (i // 2):512 * (i // 2 + 1)], bank(f"o{i}"), ACT.Tanh,
                                     scale=0.5).then_inc(s_ga, 1)
            for i in range(4):
                grouped(act, f"qn{i}")
                if i == 0:
                    act.wait_ge(s_mpart, NMOD)
                nc.scalar.copy(qnT[:, 2 * i:2 * i + 2, :], bank(f"qn{i}").rearrange("p (a b) -> p a b", a=2)
                               ).then_inc(s_ga, 1)
            act.wait_ge(s_lf, 1)
            link(nc.scalar.activation(lst[0:MH, 6, :], lst[0:MH, 5, :], ACT.Exp, scale=-1.0))
            nc.scalar.activation(lst[0:MH, 7, :], lst[0:MH, 6, :], ACT.Ln, bias=1.0).then_inc(s_le, 1)
            for i in range(4):
                grouped(act, f"kn{i}")
                nc.scalar.copy(knT[:, 2 * i:2 * i + 2, :], bank(f"kn{i}").rearrange("p (a b) -> p a b", a=2)
                               ).then_inc(s_ga, 1)
            act.wait_ge(s_scan, 1)
            nc.scalar.activation(lst[0:MH, 5, :], lst[0:MH, 3, :], ACT.Exp, scale=-1.0).then_inc(s_em, 1)

            def gate_tanh(i):
                if i == 0:
                    act.wait_ge(s_grp, GI["va3"] + 1)
                grouped(act, f"g{i}")
                nc.scalar.activation(gates[:, i % 2, 512 * (i // 2):512 * (i // 2 + 1)], bank(f"g{i}"), ACT.Tanh,
                                     scale=0.5).then_inc(s_ga, 1)

            def m_out(h):
                for t in range(NT):
                    act.wait_ge(s_mr, 2 * h + t + 1)
                    nc.scalar.activation(hn[:, t, h * MV:(h + 1) * MV], ps[:, 5 + t, 0:MV], ACT.Copy,
                                         scale=small[:, 82 + 2 * (h % 2) + t:83 + 2 * (h % 2) + t]).then_inc(s_mh, 1)

            for h in range(MH):
                act.wait_ge(s_mw, 2 * (h + 1))
                w = att[:, h % 2, 0, :]
                nc.scalar.activation(w, w, ACT.Exp).then_inc(s_mexp, 1)
                if h in (1, 3):
                    gate_tanh(h // 2)
                if h >= 1:
                    m_out(h - 1)
            m_out(MH - 1)

            def attention(todo, set0, unit0, out0, scale, dest, last_of, fill):
                n, at = set0, []
                for _, heads in todo:
                    at.append(n)
                    n += len(heads)
                o = out0
                for u in range(len(todo) + 1):
                    if u < len(todo):
                        kind, heads = todo[u]
                        ui = unit0 + u
                        g = len(heads)
                        act.wait_ge(s_nm, ui + 1)
                        a = att[:, ui % 2, 0:g, :]
                        sm = small[:, 32 + 8 * (ui % 2):40 + 8 * (ui % 2)]
                        nc.scalar.activation(a[:, :, 0:P], a[:, :, 0:P], ACT.Exp, scale=scale, bias=sm[:, 0:1],
                                             accum_out=sm[:, 2:3])
                        nc.scalar.activation(a[:, :, P:SPAN], a[:, :, P:SPAN], ACT.Exp, scale=scale, bias=sm[:, 1:2],
                                             accum_out=sm[:, 3:4]).then_inc(s_exp, 1)
                        fill(u)
                    if u >= 1:
                        kind, heads = todo[u - 1]
                        for g, h in enumerate(heads):
                            s = at[u - 1] + g
                            act.wait_ge(s_pt, s + 1)
                            if s >= 3:
                                act.wait_ge(s_pv, s - 2)
                            nc.scalar.copy(pT[:, s % 3, :], ps[:, 3 + s % 2, 0:SPAN]).then_inc(s_pTc, 1)
                        if last_of(kind):
                            for g, h in enumerate(heads):
                                act.wait_ge(s_pv, at[u - 1] + g + 1)
                                d, lo, hi = dest(kind, h)
                                nc.scalar.copy(d, ps[lo:hi, 6 + o % 2, 0:T]).then_inc(s_y, 1)
                                o += 1

            attention(UNITS1, 0, 0, 0, float((NOPE + ROPE) ** -0.5), lambda kind, h: (ya[:, h, :], 0, P),
                      lambda kind: True, lambda u: gate_tanh(GM + u) if GM + u < 8 else None)
            for b in range(4):
                act.wait_ge(s_yt, b + 1)
                nc.scalar.copy(ym[:, 2 * b:2 * b + 2, :], ps[:, b, :].rearrange("p (a b) -> p a b", a=2)
                               ).then_inc(s_ymT, 1)

            def merged_half(k):
                for b in range(4):
                    act.wait_ge(s_mt2, 4 * k + b + 1)
                    nc.scalar.copy(mergedT[:, 2 * b:2 * b + 2, :], ps[:, b, :].rearrange("p (a b) -> p a b", a=2)
                                   ).then_inc(s_mT, 1)

            merged_half(0)

            def high(m, i, b, k, slot0, count0):
                e, half, par = 2 * i + b + k, i + (b + k) // 2, (b + k) % 2
                act.wait_ge((s_gu if m < 2 else s_dn)[par], 16 * (half + 1 + count0 // 2))
                if not (m < 2 and count0 == 0 and k == 0):
                    act.wait_ge((s_gate, s_gup, s_dnp)[m], e + (count0 if m < 2 else (DN2 if count0 else 1)))
                src = dring[:, par, :] if m == 2 else ring[:, (slot0 + par) % 2, m * W3:(m + 1) * W3]
                nc.scalar.activation(wsp[:, m, 0, :], src, ACT.Copy).then_inc(s_hi[m], 1)

            def tokens_high(n, dst):
                act.wait_ge(s_hTa, 4 * (n + 1))
                nc.scalar.activation(dst[:, 0:4, :], hT[:, 0:4, :], ACT.Copy).then_inc(s_hsh, 1)

            n0, n1 = len(LOADS), len(ALL)
            act.wait_ge(s_x1, 4)
            row_squares(1)
            high(0, 0, 0, 0, n0, 0)
            hT_half(1, modT[:, 40:48], modT[:, 16:24])
            tokens_high(1, hTs[:, 0])
            high(1, 0, 0, 0, n0, 0)
            act.wait_ge(s_re, 1)
            nc.scalar.activation(rt[:, 80:88], rt[:, 72:80], ACT.Exp).then_inc(s_rx, 1)
            act.wait_ge(s_re, 2)
            nc.scalar.activation(rt[:, 190:192], rt[:, 188:190], ACT.Exp).then_inc(s_rx, 1)

            def half_tanh(i, b):
                act.wait_ge(s_gate, 2 * i + b + 1)
                act.wait_ge(s_a2, 2 * i + b + 1)
                nc.scalar.activation(tmp[:, b, :], ps[:, 4 + 2 * b, :], ACT.Tanh, scale=0.5).then_inc(s_th, 1)

            def stream(first, second, slot0, count0, total):
                def step(i, b, last=False):
                    first(i, b)
                    if not last:
                        high(0, i, b, 1, slot0, count0)
                        high(1, i, b, 1, slot0, count0)
                    second(i, b)
                    high(2, i, b, 0, slot0, count0)

                pairs = (total - 1) // 2
                with act.Fori(0, pairs) as i:
                    step(i, 0)
                    step(i, 1)
                for e in range(2 * pairs, total):
                    step(e // 2, e % 2, e == total - 1)

            stream(half_tanh, lambda i, b: None, n0, 0, NE)

            def final_norm(k):
                act.wait_ge(s_x1, 8 * (k + 1))
                for t in range(NT):
                    link(nc.scalar.activation(hn[:, t, :], xs[:, t, :], ACT.Square, accum_out=small[:, 16 + t:17 + t]))
                act.nop().then_inc(s_fss, 1)

            final_norm(0)
            act.wait_ge(s_xf, 2)
            row_squares(2)
            hT_half(2, v("g3"), None)
            tokens_high(2, hTh)

            def weights_high(n, quarters=(0, 1, 2, 3)):
                name = SPLIT[n][0]
                for q in quarters:
                    if q == 0:
                        landed(act, name)
                    if n:
                        if q < 3:
                            act.wait_ge(s_qu, 3 * (n - 1) + q + 1)
                        else:
                            grouped(act, SPLIT[n - 1][1][-1])
                    nc.scalar.activation(quarter(name, q, wh), quarter(name, q, ring), ACT.Copy).then_inc(s_qh, 1)

            def keys_out(name, c0, n):
                grouped(act, name)
                for j in range(n):
                    ins = nc.scalar.activation(fmT[:, c0 + j, :], bank(name)[:, j * T:(j + 1) * T], ACT.Identity,
                                               bias=v("b2f", c0 + j, c0 + j + 1))
                ins.then_inc(s_ga, 1)

            weights_high(0)
            for n in range(LH):
                weights_high(n + 1, (0, 1, 2))
                for name, c0, count in (("fox1", 2, 2), ("dil2", 7, 2), ("dil3", 9, 1), ("kk", 15, 2)):
                    if name in SPLIT[n][1]:
                        keys_out(name, c0, count)
                weights_high(n + 1, (3,))
                if SPLIT[n][0] == "kk":
                    act.wait_ge(s_fl, 1)
                    link(nc.scalar.activation(fox[0:FOXH, 1, :], fox[0:FOXH, 1, :], ACT.Exp, scale=-1.0))
                    nc.scalar.activation(fox[0:FOXH, 2, :], fox[0:FOXH, 1, :], ACT.Ln, bias=1.0).then_inc(s_fe, 1)
            nc.scalar.activation(gc, gc, ACT.Tanh, scale=0.5).then_inc(s_gct, 1)
            act.wait_ge(s_hu, 1)
            nc.scalar.activation(gel[:, 3], gel[:, 2], ACT.Tanh, scale=GELU).then_inc(s_hth, 1)

            def gate_tanh2(i):
                act.wait_ge(s_gv, VGROUPS - 12 + i + 1)
                sl = g2[:, i % 2, 512 * (i // 2):512 * (i // 2 + 1)]
                nc.scalar.activation(sl, sl, ACT.Tanh, scale=0.5).then_inc(s_ggu, 1)

            weights_high(LH + 1)
            gate_tanh2(0)
            gate_tanh2(1)
            weights_high(LH + 2, (0, 1))
            act.wait_ge(s_ce, 1)
            nc.scalar.activation(pcm, pcm, ACT.Exp).then_inc(s_cx, 1)
            weights_high(LH + 2, (2, 3))
            act.wait_ge(s_cpt, 1)
            for i in range(3):
                nc.scalar.copy(pcT[0:NC, 2 * i:2 * i + 2, :], ps[0:NC, 5 + i, :].rearrange("p (a b) -> p a b", a=2)
                               ).then_inc(s_cpc, 1)
            gate_tanh2(2)
            gate_tanh2(3)

            def gates_between(u):
                if u < 12:
                    weights_high(LH + 3 + u // 4, (u % 4,))
                if u in (4, 8, 12, 16):
                    gate_tanh2(HM + (u - 4) // 2)
                    gate_tanh2(HM + (u - 4) // 2 + 1)

            def dest2(kind, h):
                if kind == "fox":
                    c, r = h // 2, h % 2
                elif kind == "dil":
                    c, r = 2 + h // 2, h % 2
                else:
                    c, r = 5 + h % 3, h // 3
                return yT2[r * HD:(r + 1) * HD, c, :], r * HD, (r + 1) * HD

            attention(UNITS2, AH, AH, AH, 1.0, dest2, lambda kind: kind != "sel",
                      gates_between)
            merged_half(1)
            act.wait_ge(s_x1, 12)
            row_squares(3)
            high(0, 0, 0, 0, n1, NE)
            hT_half(3, v("g4"), None)
            tokens_high(3, hTs[:, 0])
            high(1, 0, 0, 0, n1, NE)

            def ff_act(i, b):
                act.wait_ge(s_fsq, 2 * i + b + 1)
                nc.scalar.activation(ft[:, 2, :], ft[:, b, :], ACT.Square).then_inc(s_fz, 1)

            def ff_tanh(i, b):
                act.wait_ge(s_fth, 2 * i + b + 1)
                nc.scalar.activation(tmp[:, 0, :], ft[:, 3, :], ACT.Tanh, scale=GELU).then_inc(s_ffn, 1)

            stream(ff_act, ff_tanh, n1, NE, FP)
            final_norm(1)

        @block.gpsimd
        def _(pool):
            link = Chain(pool, c_pool)
            pool.wait_ge(s_zero, 1)

            def power(dst, src, n, ready, count, done):
                pool.wait_ge(ready, count)
                nc.gpsimd.tensor_tensor(dst, src, small[:, 496:496 + n], ALU.pow).then_inc(done, 1)

            power(small[:, 18:20], small[:, 18:20], 2, s_ms, 1, s_rstd)
            power(small[:, 24:28], small[:, 24:28], 4, s_cms, 1, s_crs)

            def low(m, i, b, k, slot0, count0):
                par = (b + k) % 2
                pool.wait_ge(s_hi[m], 2 * i + b + k + 1 + count0)
                src = dring[:, par, :] if m == 2 else ring[:, (slot0 + par) % 2, m * W3:(m + 1) * W3]
                nc.gpsimd.tensor_tensor(wsp[:, m, 1, :], src, wsp[:, m, 0, :], ALU.subtract).then_inc(s_lo[m], 1)

            def stream(slot0, count0, total):
                low(0, 0, 0, 0, slot0, count0)
                low(1, 0, 0, 0, slot0, count0)

                def step(i, b, last=False):
                    if not last:
                        low(0, i, b, 1, slot0, count0)
                    low(2, i, b, 0, slot0, count0)

                pairs = (total - 1) // 2
                with pool.Fori(0, pairs) as i:
                    step(i, 0)
                    step(i, 1)
                for e in range(2 * pairs, total):
                    step(e // 2, e % 2, e == total - 1)

            power(small[:, 18:20], small[:, 18:20], 2, s_ms, 2, s_rstd)
            stream(len(LOADS), 0, NE)
            power(small[:, 18:20], small[:, 18:20], 2, s_fms, 1, s_frs)
            power(small[:, 18:20], small[:, 18:20], 2, s_ms, 3, s_rstd)
            for n, (name, _) in enumerate(SPLIT):
                for q in range(4):
                    pool.wait_ge(s_qh, 4 * n + q + 1)
                    nc.gpsimd.tensor_tensor(quarter(name, q, wl), quarter(name, q, ring), quarter(name, q, wh),
                                            ALU.subtract).then_inc(s_ql, 1)
            power(small[:, 18:20], small[:, 18:20], 2, s_ms, 4, s_rstd)
            stream(len(ALL), NE, FP)
            power(small[:, 18:20], small[:, 18:20], 2, s_fms, 2, s_frs)

        @block.vector
        def _(dve):
            link = Chain(dve, c_dve)
            V = nc.vector
            V.memset(small[:, 496:500], -0.5).then_inc(c_dve, 1)
            link.n += 1
            link(V.memset(zero[:, :], 0.0))
            dve.nop().then_inc(s_zero, 1)
            dve.wait_ge(s_condt, 1)
            link(V.scalar_tensor_tensor(small[:, 8:16], small[:, 0:8], 1.0, v("c"), ALU.add, ALU.mult))
            link(V.tensor_scalar(small[:, 8:16], small[:, 8:16], 0.5, None, ALU.mult))

            def mod_part(j):
                dve.wait_ge(s_mt[j % 2], 16 * (j // 2 + 1))
                if j >= 2:
                    dve.wait_ge(s_msum, j - 1)
                d = mpart[:, j % 2, :]
                w = mtile[j % 2]
                link(V.tensor_scalar(d, w[:, 0, :], small[:, 8:9], None, ALU.mult))
                for c in range(1, KD):
                    ins = V.scalar_tensor_tensor(d, w[:, c, :], small[:, 8 + c:9 + c], d, ALU.mult, ALU.add)
                    if c < KD - 1:
                        link(ins)
                ins.then_inc(s_mpart, 1)

            def mod_gate(j):
                dve.wait_ge(s_msum, j + 1)
                if j == 4:
                    dve.wait_ge(s_brow, 32)
                k, half = (0, j - 4) if j < 6 else (1, j - 10)
                g = gateb[:, k, half * 512:(half + 1) * 512]
                V.tensor_tensor(g, ps[:, 7, :], g, ALU.add).then_inc(s_mev, 1)

            def mod_columns(k):
                link(V.tensor_tensor(modT[:, 16 * k:16 * k + 16], ps[:, 7, 0:16], v(f"mod{k + 1}"), ALU.add))
                V.scalar_tensor_tensor(modT[:, 32 + 8 * k:40 + 8 * k], modT[:, 16 * k + 8:16 * k + 16], 1.0,
                                       v(f"g{k + 1}"), ALU.add, ALU.mult).then_inc(s_mev, 1)

            for j in range(4):
                mod_part(j)
            dve.wait_ge(s_msum, 4)
            mod_columns(0)

            def row_scale(k, sem_in, n_in, sem_ms, sem_rs, n):
                dve.wait_ge(sem_in, n_in)
                V.tensor_scalar(small[:, 18:20], small[:, 16:18], 1.0 / D, EPS, ALU.mult, ALU.add).then_inc(sem_ms, 1)
                dve.wait_ge(sem_rs, n)

            def norm_rows(k):
                row_scale(k, s_ss, k + 1, s_ms, s_rstd, k + 1)
                for t in range(NT):
                    V.tensor_scalar(hn[:, t, :], xs[:, t, :], small[:, 18 + t:19 + t], None, ALU.mult).then_inc(s_hn, 1)

            def hT_half(k, scale, shift):
                for c in range(4, KD):
                    if c % 2 == 0:
                        dve.wait_ge(s_tr, 4 * k + c // 2 + 1)
                    src = ps[:, c // 2, (c % 2) * T:(c % 2 + 1) * T]
                    if shift is None:
                        V.tensor_scalar(hT[:, c, :], src, scale[:, c:c + 1], None, ALU.mult).then_inc(s_hTv, 1)
                    else:
                        V.tensor_scalar(hT[:, c, :], src, scale[:, c:c + 1], shift[:, c:c + 1], ALU.mult, ALU.add
                                        ).then_inc(s_hTv, 1)

            norm_rows(0)
            dve.wait_ge(s_mev, 1)
            hT_half(0, modT[:, 32:40], modT[:, 0:8])

            def rope(dst, src, t1, t2):
                link(V.tensor_tensor(t1, src, const("cos"), ALU.mult))
                for q in range(4):
                    o = q ^ 1
                    ins = V.tensor_tensor(t2[q * 32:(q + 1) * 32, :], src[o * 32:(o + 1) * 32, :],
                                          const("sin")[q * 32:(q + 1) * 32, :], ALU.mult)
                    link(ins)
                return V.tensor_tensor(dst, t1, t2, ALU.add)

            mod_part(4)
            mod_part(5)
            sc1, sc2 = pT[:, 0, 0:T], pT[:, 1, 0:T]
            grouped(dve, "kr")
            krope = pT[:, 2, 0:T]
            link(rope(krope, bank("kr")[:, 0:T], sc1, sc2))
            dve.nop().then_inc(s_gv, 1)
            mod_gate(4)
            mod_part(6)
            mod_gate(5)
            dve.wait_ge(s_css, 1)
            link(V.tensor_scalar(small[:, 24:26], small[:, 20:22], 1.0 / QL, EPS, ALU.mult, ALU.add))
            V.tensor_scalar(small[:, 26:28], small[:, 22:24], 1.0 / KVL, EPS, ALU.mult, ALU.add).then_inc(s_cms, 1)
            dve.wait_ge(s_crs, 1)
            for t in range(NT):
                link(V.tensor_scalar(raw[:, t, 0:QL], raw[:, t, 0:QL], small[:, 24 + t:25 + t], None, ALU.mult))
                V.tensor_scalar(raw[:, t, 392:RAW], raw[:, t, 392:RAW], small[:, 26 + t:27 + t], None, ALU.mult
                                ).then_inc(s_cn, 1)

            def conv(i):
                name = f"qk{i}"
                grouped(dve, name)
                src = bank(name).rearrange("p (a b) -> p a b", a=2)
                acc = hn[:, i % 2, 0:512].rearrange("p (a b) -> p a b", a=2)
                for j in range(2):
                    blk = 2 * i + j
                    wv = v("convw", 4 * blk, 4 * blk + 4)
                    link(V.tensor_scalar(acc[:, j, :], src[:, j, :], wv[:, 3:4], v("convb", blk, blk + 1), ALU.mult,
                                         ALU.add))
                    for d in range(1, CONV):
                        link(V.scalar_tensor_tensor(acc[:, j, d:T], src[:, j, 0:T - d], wv[:, 3 - d:4 - d],
                                                    acc[:, j, d:T], ALU.mult, ALU.add))
                dve.nop().then_inc(s_conv, 1)
                dve.wait_ge(s_convt, i + 1)
                V.scalar_tensor_tensor(qkT[:, 2 * i:2 * i + 2, :], att[:, 1, 0:2, 0:T], 1.0, acc, ALU.add, ALU.mult
                                       ).then_inc(s_gv, 1)

            dve.wait_ge(s_hn, 2)
            dve.wait_ge(s_tr, 4)
            for i in range(4):
                conv(i)
                mod_part(7 + i)
            dve.wait_ge(s_msum, 10)
            mod_columns(1)
            mod_part(11)
            mod_gate(10)
            mod_gate(11)
            V.memset(vaug[:, :, :, MV:MV + 1], 1.0).then_inc(c_dve, 1)
            link.n += 1
            dve.wait_ge(s_ctr, 1)
            for c in range(5):
                g = v("qg", c, c + 1) if c < 3 else v("kvg", c - 3, c - 2)
                V.tensor_scalar(cT[:, c, :], ps[:, 4 + c // 2, (c % 2) * T:(c % 2 + 1) * T], g, None, ALU.mult
                                ).then_inc(c_dve, 1)
                link.n += 1
            link(V.tensor_copy(krT, krope))
            dve.nop().then_inc(s_cT, 1)
            L = lst[0:MH, :, :]
            link(V.tensor_scalar(L[:, 1, :], ps[0:MH, 7, 0:T], v("fb")[0:MH, :], None, ALU.add))
            link(V.tensor_scalar(L[:, 2, :], ps[0:MH, 6, T:2 * T], v("ib")[0:MH, :], None, ALU.add))
            V.scalar_tensor_tensor(L[:, 5, :], L[:, 1, :], -1.0, L[:, 1, :], ALU.mult, ALU.max).then_inc(s_lf, 1)
            dve.wait_ge(s_le, 1)
            link(V.scalar_tensor_tensor(L[:, 1, :], L[:, 1, :], 0.0, L[:, 7, :], ALU.min, ALU.subtract))
            link(V.tensor_tensor_scan(L[:, 6, :], const("ones")[0:MH, 0:1].to_broadcast([MH, T]), L[:, 1, :], 0.0,
                                      ALU.mult, ALU.add))
            link(V.tensor_tensor(L[:, 2, :], L[:, 2, :], L[:, 6, :], ALU.subtract))
            link(V.tensor_tensor_scan(L[:, 4, :], const("ones")[0:MH, 0:1].to_broadcast([MH, T]), L[:, 2, :], 0.0,
                                      ALU.mult, ALU.max))
            link(V.tensor_tensor(L[:, 3, :], L[:, 4, :], L[:, 6, :], ALU.add))
            link(V.tensor_scalar(L[:, 4, :], L[:, 4, :], -1.0, None, ALU.mult))
            dve.nop().then_inc(s_scan, 1)
            for i in range(2):
                grouped(dve, f"qr{i}")
                for j in range(2):
                    link(rope(qrT[:, 2 * i + j, :], bank(f"qr{i}")[:, j * T:(j + 1) * T], sc1, sc2))
                dve.nop().then_inc(s_gv, 1)
            for i in range(4):
                grouped(dve, f"va{i}")
                V.tensor_copy(va[:, i % 2, 512 * (i // 2):512 * (i // 2 + 1)], bank(f"va{i}")).then_inc(s_gv, 1)
            dve.wait_ge(s_gt, 1)
            V.tensor_copy(small[:, 64:80], ps[:, 4, 0:16]).then_inc(s_gte, 1)
            dve.wait_ge(s_gte, 1)

            def m_weights(h):
                dve.wait_ge(s_mS, h + 1)
                w = att[:, h % 2, 0, :]
                V.tensor_scalar(w[:, 0:T], ps[:, h % 2, 0:T], small[:, 64 + h:65 + h], 0.0, ALU.add, ALU.min
                                ).then_inc(s_mw, 1)
                V.tensor_scalar(w[:, T:SPAN], ps[:, h % 2, P:T], small[:, 68 + h:69 + h], 0.0, ALU.add, ALU.min
                                ).then_inc(s_mw, 1)
                dve.wait_ge(s_mexp, h + 1)
                if h >= 2:
                    dve.wait_ge(s_mnum, h - 1)
                d = wmem[:, (h % 2) * SPAN:(h % 2 + 1) * SPAN]
                link(V.scalar_tensor_tensor(d, ps[:, 2 + h % 2, 0:SPAN], 0.25 * MQK ** -0.5, w, ALU.mult, ALU.mult))
                link(V.tensor_tensor(d[:, 0:P], d[:, 0:P], const("tri"), ALU.mult))
                V.tensor_tensor(d[:, T:SPAN], d[:, T:SPAN], const("tri"), ALU.mult).then_inc(s_mst, 1)

            def m_den(h):
                dve.wait_ge(s_mnum, h + 1)
                for t in range(NT):
                    r = small[:, 80 + t:81 + t]
                    link(V.tensor_scalar(r, ps[:, 5 + t, MV:MV + 1], -1.0, small[:, 72 + 4 * t + h:73 + 4 * t + h],
                                         ALU.mult, ALU.max))
                    link(V.tensor_tensor(r, ps[:, 5 + t, MV:MV + 1], r, ALU.max))
                    V.reciprocal(small[:, 82 + 2 * (h % 2) + t:83 + 2 * (h % 2) + t], r).then_inc(s_mr, 1)
                dve.wait_ge(s_mh, 2 * (h + 1))
                for t in range(NT):
                    o = og[:, t, h * MV:(h + 1) * MV]
                    V.scalar_tensor_tensor(o, o, 1.0, hn[:, t, h * MV:(h + 1) * MV], ALU.add, ALU.mult
                                           ).then_inc(s_my, 1)

            for h in range(MH):
                m_weights(h)
                if h >= 1:
                    m_den(h - 1)
            m_den(MH - 1)

            def attention(todo, set0, unit0, scale, bias, fill=None):
                n, at = set0, []
                for _, heads in todo:
                    at.append(n)
                    n += len(heads)
                for u in range(len(todo) + 1):
                    if u < len(todo):
                        kind, heads = todo[u]
                        ui = unit0 + u
                        a = att[:, ui % 2, 0:len(heads), :]
                        sm = small[:, 32 + 8 * (ui % 2):40 + 8 * (ui % 2)]
                        if u >= 2:
                            dve.wait_ge(s_pt, at[u - 1])
                        for g, h in enumerate(heads):
                            s = at[u] + g
                            dve.wait_ge(s_sc, s + 1)
                            tile, slope = bias(kind, g, h)
                            V.scalar_tensor_tensor(a[:, g, :], tile, slope, ps[:, s % 2, 0:SPAN], ALU.mult, ALU.add
                                                   ).then_inc(s_sfree, 1)
                        dve.wait_ge(s_sfree, at[u] + len(heads))
                        V.tensor_reduce(sm[:, 0:1], a[:, :, 0:P], AX.XY, ALU.max, negate=True).then_inc(c_dve, 1)
                        link.n += 1
                        if scale is None:
                            V.tensor_reduce(sm[:, 1:2], a[:, :, P:SPAN], AX.XY, ALU.max, negate=True
                                            ).then_inc(s_nm, 1)
                        else:
                            link(V.tensor_reduce(sm[:, 1:2], a[:, :, P:SPAN], AX.XY, ALU.max, negate=True))
                            V.tensor_scalar(sm[:, 0:2], sm[:, 0:2], scale, None, ALU.mult).then_inc(s_nm, 1)
                    if u >= 1:
                        kind, heads = todo[u - 1]
                        ui = unit0 + u - 1
                        a = att[:, ui % 2, 0:len(heads), :]
                        sm = small[:, 32 + 8 * (ui % 2):40 + 8 * (ui % 2)]
                        dve.wait_ge(s_exp, ui + 1)
                        link(V.tensor_scalar(sm[:, 4:6], sm[:, 2:4], TINY, None, ALU.max))
                        link(V.reciprocal(sm[:, 4:6], sm[:, 4:6]))
                        if kind in ("sel", "win"):
                            j = 3 * heads[0] + (1 if kind == "sel" else 2)
                            link(V.tensor_tensor(sm[:, 4:6], sm[:, 4:6], gc[:, :, j:j + 1].rearrange("p t o -> p (t o)"),
                                                 ALU.mult))
                        V.tensor_scalar(a[:, :, 0:P], a[:, :, 0:P], sm[:, 4:5], None, ALU.mult)
                        V.tensor_scalar(a[:, :, P:SPAN], a[:, :, P:SPAN], sm[:, 5:6], None, ALU.mult).then_inc(s_p, 1)
                    if fill:
                        fill(u)

            attention(UNITS1, 0, 0, float((NOPE + ROPE) ** -0.5), lambda kind, g, h: (const("chunk"), 1.0))

            for half in range(2):
                for t in range(NT):
                    dve.wait_ge(s_br, 2 * half + t + 1)
                    cs = slice(512 * half, 512 * (half + 1))
                    link(V.scalar_tensor_tensor(hn[:, t, cs], gates[:, t, cs], 1.0, ps[:, 2 * half + t, :], ALU.add,
                                                ALU.mult))
            for half in range(2):
                for t in range(NT):
                    dve.wait_ge(s_br, 4 + 2 * half + t + 1)
                    cs = slice(512 * half, 512 * (half + 1))
                    ga = gates[:, t, D + 512 * half:D + 512 * (half + 1)]
                    link(V.scalar_tensor_tensor(ga, ga, 1.0, ps[:, 4 + 2 * half + t, :], ALU.add, ALU.mult))
                    V.scalar_tensor_tensor(merged[:, t, cs], hn[:, t, cs], 0.5, ga, ALU.mult, ALU.add
                                           ).then_inc(s_mrg, 1)
            link(V.tensor_scalar(gateb[:, 0, :], gateb[:, 0, :], 0.5, None, ALU.mult))
            for half in range(2):
                for t in range(NT):
                    dve.wait_ge(s_pr, 2 * half + t + 1)
                    cs = slice(512 * half, 512 * (half + 1))
                    link(V.tensor_tensor(hn[:, t, cs], ps[:, 4 + 2 * half + t, :], gateb[:, 0, cs], ALU.mult))
                    V.tensor_tensor(xs[:, t, cs], xs[:, t, cs], hn[:, t, cs], ALU.add).then_inc(s_x1, 1)
            norm_rows(1)
            hT_half(1, modT[:, 40:48], modT[:, 16:24])

            def split_tokens(n, hi, lo):
                dve.wait_ge(s_hTv, 4 * (n + 1))
                link(V.tensor_copy(hi[:, 4:KD, :], hT[:, 4:KD, :]))
                V.tensor_tensor(lo[:, 4:KD, :], hT[:, 4:KD, :], hi[:, 4:KD, :], ALU.subtract).then_inc(s_hs, 1)
                dve.wait_ge(s_hsh, n)
                V.tensor_tensor(lo[:, 0:4, :], hT[:, 0:4, :], hi[:, 0:4, :], ALU.subtract).then_inc(s_hs, 1)

            split_tokens(1, hTs[:, 0], hTs[:, 1])

            lg = rt[:, 0:72].rearrange("p (t n) -> p t n", t=NT)
            lgrp = lg[:, :, 0:NG]
            lexp = lg[:, :, NG:NG + NE].rearrange("p t (g e) -> p t g e", g=NG)

            def t2(a, n):
                return rt[:, a:a + NT * n].rearrange("p (t n) -> p t n", t=NT)

            def bc(a, shape):
                return a.to_broadcast(shape)

            dve.wait_ge(s_final1, 32)
            dve.wait_ge(s_lg, 1)
            for t in range(NT):
                link(V.tensor_tensor(lg[:, t, :], ps[:, 0, t * 36:(t + 1) * 36], small[:, 448:484], ALU.add))
            gmax, gdif, gexp = t2(88, 1), t2(72, NG), t2(80, NG)
            link(V.tensor_reduce(gmax, lgrp, AX.X, ALU.max))
            ins = V.tensor_tensor(gdif, lgrp, bc(gmax, [P, NT, NG]), ALU.subtract)
            ins.then_inc(s_re, 1)
            gsum, pg, oh, key, kmax = t2(90, 1), t2(92, 1), t2(96, NG), t2(104, EG), t2(120, 1)
            dve.wait_ge(s_rx, 1)
            link(V.tensor_reduce(gsum, gexp, AX.X, ALU.add))
            link(V.reciprocal(pg, gsum))

            def first_max(dst, src, top, rank, n):
                k = t2(104, n)
                link(V.tensor_tensor(dst, src, bc(top, [P, NT, n]), ALU.is_equal))
                for t in range(NT):
                    link(V.tensor_tensor(k[:, t, :], dst[:, t, :], rank, ALU.mult))
                link(V.tensor_reduce(kmax, k, AX.X, ALU.max))
                link(V.tensor_tensor(dst, k, bc(kmax, [P, NT, n]), ALU.is_equal))

            first_max(oh, lgrp, gmax, const("rank4"), NG)
            prod = rt[:, 512:512 + 64].rearrange("p (t g e) -> p t g e", t=NT, g=NG)
            for t in range(NT):
                link(V.tensor_tensor(prod[:, t], lexp[:, t], bc(oh[:, t, :].rearrange("p (g o) -> p g o", o=1), [P, NG, EG]),
                                     ALU.mult))
            l8, top1, oh1, l8b, top2, oh2 = t2(122, EG), t2(138, 1), t2(140, EG), t2(156, EG), t2(172, 1), t2(194, EG)
            link(V.tensor_reduce(l8, prod.rearrange("p t g e -> p t e g"), AX.X, ALU.add))
            link(V.tensor_reduce(top1, l8, AX.X, ALU.max))
            first_max(oh1, l8, top1, const("rank8"), EG)
            link(V.scalar_tensor_tensor(l8b, oh1, NEG, l8, ALU.mult, ALU.add))
            link(V.tensor_reduce(top2, l8b, AX.X, ALU.max))
            first_max(oh2, l8b, top2, const("rank8"), EG)
            e2, w1, w2 = rt[:, 190:192], rt[:, 174:176], rt[:, 176:178]
            V.tensor_tensor(rt[:, 188:190], rt[:, 172:174], rt[:, 138:140], ALU.subtract).then_inc(s_re, 1)
            dve.wait_ge(s_rx, 2)
            link(V.tensor_scalar(w1, e2, 1.0, None, ALU.add))
            link(V.reciprocal(w1, w1))
            link(V.tensor_tensor(w1, w1, rt[:, 92:94], ALU.mult))
            link(V.tensor_scalar(w1, w1, 0.5, None, ALU.mult))
            link(V.tensor_tensor(w2, w1, e2, ALU.mult))
            w8 = t2(210, EG)
            w32 = rt[:, 256:256 + 64].rearrange("p (t g e) -> p t g e", t=NT, g=NG)
            for t in range(NT):
                link(V.tensor_scalar(w8[:, t, :], oh1[:, t, :], w1[:, t:t + 1], None, ALU.mult))
                link(V.scalar_tensor_tensor(w8[:, t, :], oh2[:, t, :], w2[:, t:t + 1], w8[:, t, :], ALU.mult, ALU.add))
                for g in range(NG):
                    link(V.tensor_scalar(w32[:, t, g, :], w8[:, t, :], oh[:, t, g:g + 1], None, ALU.mult))
            dve.nop().then_inc(s_w32, 1)
            dve.wait_ge(s_wt, 1)
            V.tensor_copy(rt[0:NE, 384:384 + T], ps[0:NE, 1, 0:T]).then_inc(s_wtc, 1)

            def split_act(src, b, e, down0):
                dve.wait_ge(s_dnp, e + down0)
                flat = [aTs[:, b, s].rearrange("p f n -> p (f n)") for s in range(2)]
                link(V.tensor_copy(flat[0], src))
                V.tensor_tensor(flat[1], src, flat[0], ALU.subtract).then_inc(s_aT, 1)

            def up_low(i, b, slot0, count0):
                par = 1 - b
                dve.wait_ge(s_hi[1], 2 * i + b + 2 + count0)
                V.tensor_tensor(wsp[:, 1, 1, :], ring[:, (slot0 + par) % 2, W3:2 * W3], wsp[:, 1, 0, :], ALU.subtract
                                ).then_inc(s_lo[1], 1)

            def expert(i, b, low):
                e = 2 * i + b
                dve.wait_ge(s_th, e + 1)
                t0, g, u = tmp[:, b, :], ps[:, 4 + 2 * b, :], ps[:, 5 + 2 * b, :]
                link(V.scalar_tensor_tensor(t0, t0, 1.0, g, ALU.add, ALU.mult))
                dve.wait_ge(s_gup, e + 1)
                V.tensor_tensor(t0, t0, u, ALU.mult).then_inc(s_a2, 1)
                dve.wait_ge(s_a2, e + 2)
                dve.wait_ge(s_wb[b], 16 * (i + 1))
                for f in range(2):
                    link(V.tensor_tensor(act32[:, f * T:(f + 1) * T], t0[:, f * T:(f + 1) * T], wbe[:, b, :], ALU.mult))
                split_act(act32, b, e, 1)
                low()

            def stream(work, per, slot0, count0, total):
                loops = (total - 1) // 2
                with dve.Fori(0, loops) as i:
                    n = link.n
                    link.start(i, per)
                    for b in range(2):
                        work(i, b, lambda: up_low(i, b, slot0, count0))
                    assert link.n - n == per, link.n - n
                link.end(loops)
                for e in range(2 * loops, total):
                    work(e // 2, e % 2, lambda: up_low(e // 2, e % 2, slot0, count0) if e < total - 1 else None)

            dve.nop().then_inc(s_a2, 1)
            stream(expert, 8, len(LOADS), 0, NE)
            dve.wait_ge(s_dnp, NE + 1)
            for t in range(NT):
                for half in range(2):
                    cs = slice(512 * half, 512 * (half + 1))
                    link(V.tensor_tensor(hn[:, t, cs], ps[:, 2 * t + half, :], gateb[:, 1, cs], ALU.mult))
                    V.tensor_tensor(xs[:, t, cs], xs[:, t, cs], hn[:, t, cs], ALU.add).then_inc(s_x1, 1)

            def final_norm(k, dst):
                row_scale(k, s_fss, k + 1, s_fms, s_frs, k + 1)
                if k == 1:
                    dve.wait_ge(s_final2, 16)
                for t in range(NT):
                    V.scalar_tensor_tensor(dst[:, t, :], xs[:, t, :], small[:, 18 + t:19 + t], finalb[:, :], ALU.mult,
                                           ALU.mult).then_inc(s_xf, 1)

            final_norm(0, xs)
            dve.wait_ge(s_xf, 2)
            norm_rows(2)
            hT_half(2, v("g3"), None)
            split_tokens(2, hTh, hTl)

            def columns_out(name, c0, n, scale):
                grouped(dve, name)
                for j in range(n):
                    src = bank(name)[:, j * T:(j + 1) * T]
                    if scale:
                        ins = V.tensor_scalar(fmT[:, c0 + j, :], src, v("b2f", c0 + j, c0 + j + 1), 0.125, ALU.add,
                                              ALU.mult)
                    else:
                        ins = V.tensor_scalar(fmT[:, c0 + j, :], src, v("b2f", c0 + j, c0 + j + 1), None, ALU.add)
                ins.then_inc(s_gv, 1)

            columns_out("fox0", 0, 2, True)
            columns_out("dil0", 4, 2, True)
            columns_out("dil1", 6, 1, True)
            columns_out("nsa0", 10, 2, True)
            columns_out("nsa1", 12, 1, True)
            columns_out("kcv", 13, 2, False)
            emptied(dve, GI["kcv"])
            for i in range(2):
                for g in range(KVG):
                    for jj in range(2):
                        src = fmT[g * HD:(g + 1) * HD, 13 + i, :]
                        d = kvc[jj * HD:(jj + 1) * HD, i, :, g * NC:(g + 1) * NC]
                        for q in range(2):
                            s3 = src[:, 16 * q:16 * q + 240].rearrange("p (c j two) -> p two j c", j=8, two=2)[:, jj]
                            link(V.tensor_copy(d[:, 8 * q:8 * q + 8, :], s3))
                link(V.tensor_tensor(kvc[:, i], kvc[:, i],
                                     v("pe").rearrange("p (j o) -> p j o", o=1).to_broadcast([P, CB // 2, KVG * NC]),
                                     ALU.add))
            dve.nop().then_inc(s_F, 1)
            dve.wait_ge(s_bias2, 16)
            grouped(dve, "gf")
            f = fox[0:FOXH]
            for t in range(NT):
                V.tensor_tensor(gc[:, t, :], bank("gf")[:, t * 3 * NSAH:(t + 1) * 3 * NSAH], bias2[:, 896:914], ALU.add)
            V.tensor_scalar(f[:, 0, :], bank("gf")[0:FOXH, T:2 * T], v("fab")[0:FOXH, :], None, ALU.add).then_inc(s_gv, 1)
            emptied(dve, GI["gf"])
            V.scalar_tensor_tensor(f[:, 1, :], f[:, 0, :], -1.0, f[:, 0, :], ALU.mult, ALU.max).then_inc(s_fl, 1)
            for t in range(NT):
                grouped(dve, f"vv{t}")
                V.tensor_tensor(tv[:, t, :], bank(f"vv{t}"), bias2[:, 0:512], ALU.add).then_inc(s_gv, 1)
            for t in range(NT):
                grouped(dve, f"vb{t}")
                V.tensor_tensor(tvb[:, t, :], bank(f"vb{t}")[:, 0:384], bias2[:, 512:896], ALU.add).then_inc(s_gv, 1)
            dve.wait_ge(s_fe, 1)
            link(V.scalar_tensor_tensor(f[:, 0, :], f[:, 0, :], 0.0, f[:, 2, :], ALU.min, ALU.subtract))
            link(V.tensor_tensor_scan(f[:, 3, :], const("ones")[0:MH, 0:1].to_broadcast([MH, T]), f[:, 0, :], 0.0,
                                      ALU.mult, ALU.add))
            V.tensor_scalar(f[:, 3, :], f[:, 3, :], -1.0, None, ALU.mult).then_inc(s_fsc, 1)
            dve.wait_ge(s_hid, 2)
            hu, hw, hz, ht = (gel[:, k] for k in range(4))
            link(V.tensor_copy(hu, ps[:, 4:6, 0:60]))
            link(V.tensor_tensor(hw, hu, hu, ALU.mult))
            link(V.tensor_scalar(hw, hw, 0.044715, 1.0, ALU.mult, ALU.add))
            V.tensor_tensor(hz, hw, hu, ALU.mult).then_inc(s_hu, 1)
            dve.wait_ge(s_hth, 1)
            link(V.scalar_tensor_tensor(hw, ht, 1.0, hu, ALU.add, ALU.mult))
            V.tensor_scalar(hidT.rearrange("p a b c -> p a (b c)"), hw, 0.5, None, ALU.mult).then_inc(s_hg, 1)

            def gate_bias(i):
                grouped(dve, f"h{i}")
                V.tensor_tensor(g2[:, i % 2, 512 * (i // 2):512 * (i // 2 + 1)], bank(f"h{i}"),
                                bias2[:, 914 + 512 * (i // 2):914 + 512 * (i // 2 + 1)], ALU.add).then_inc(s_gv, 1)
            gate_bias(0)
            gate_bias(1)
            dve.wait_ge(s_kc, 1)
            link(V.tensor_copy(kcT[:, 0:NC], ps[:, 6, 0:NC]))
            V.tensor_copy(vc[0:NC], ps[0:NC, 7, 0:2 * HD].rearrange("p (g d) -> p g d", g=KVG)).then_inc(s_kce, 1)
            dve.wait_ge(s_gct, 1)
            gcf = gc.rearrange("p t n -> p (t n)")
            link(V.tensor_scalar(gcf, gcf, 0.5, 0.5, ALU.mult, ALU.add))
            dve.wait_ge(s_cs, 1)
            pf = pcm.rearrange("p a b -> p (a b)")
            for g in range(KVG):
                link(V.tensor_tensor(pf.rearrange("p (t g n) -> p t g n", t=NT, g=KVG)[:, :, g, :],
                                     ps[:, 3 + g, 0:NT * 3 * NC].rearrange("p (t n) -> p t n", t=NT),
                                     const("cbias").rearrange("p (t g n) -> p t g n", t=NT, g=KVG)[:, :, g, :], ALU.add))
            cm, cl = small[:, 420:432], small[:, 432:444]
            m3 = cm.rearrange("p (a o) -> p a o", o=1)
            link(V.tensor_reduce(m3, pcm, AX.X, ALU.max))
            V.tensor_tensor(pcm, pcm, m3.to_broadcast([P, NT * NSAH, NC]), ALU.subtract).then_inc(s_ce, 1)
            gate_bias(2)
            gate_bias(3)
            dve.wait_ge(s_cx, 1)
            link(V.tensor_tensor(pf, pf, const("cmask"), ALU.mult))
            link(V.tensor_reduce(cl.rearrange("p (a o) -> p a o", o=1), pcm, AX.X, ALU.add))
            link(V.tensor_scalar(cl, cl, TINY, None, ALU.max))
            link(V.reciprocal(cl, cl))
            link(V.tensor_tensor(cl.rearrange("p (t h) -> p t h", t=NT), cl.rearrange("p (t h) -> p t h", t=NT),
                                 gc[:, :, 0:3 * NSAH:3], ALU.mult))
            V.tensor_tensor(pcm, pcm, cl.rearrange("p (a o) -> p a o", o=1).to_broadcast([P, NT * NSAH, NC]), ALU.mult
                            ).then_inc(s_cp, 1)

            def bias2_tile(kind, g, h):
                if kind == "fox":
                    return const("causal"), 1.0
                if kind == "dil":
                    return const("dil", g * SPAN, (g + 1) * SPAN), DIL_SLOPE[h]
                return const("dist"), NSA_SLOPE[h]

            attention(UNITS2, AH, AH, None, bias2_tile,
                      lambda u: [gate_bias(HM + u // 2 - 1 + k) for k in range(2)] if u % 4 == 3 and u < 16 else None)

            for i in range(3):
                for half in range(2):
                    for t in range(NT):
                        dve.wait_ge(s_br, 8 + 4 * i + 2 * half + t + 1)
                        if i == 0:
                            dve.wait_ge(s_ggu, 12)
                        cs = slice(512 * half, 512 * (half + 1))
                        gsl = g2[:, t, i * D + 512 * half:i * D + 512 * (half + 1)]
                        p = ps[:, 4 * (i % 2) + 2 * half + t, :]
                        if i == 0:
                            V.scalar_tensor_tensor(merged2[:, t, cs], gsl, 1.0, p, ALU.add, ALU.mult
                                                   ).then_inc(s_gv, 1)
                        else:
                            link(V.scalar_tensor_tensor(gsl, gsl, 1.0, p, ALU.add, ALU.mult))
                            ins = V.tensor_tensor(merged2[:, t, cs], merged2[:, t, cs], gsl, ALU.add)
                            if i == 1:
                                link(ins)
                            else:
                                ins.then_inc(s_mrg, 1)
            for half in range(2):
                for t in range(NT):
                    dve.wait_ge(s_pr, 4 + 2 * half + t + 1)
                    cs = slice(512 * half, 512 * (half + 1))
                    V.scalar_tensor_tensor(xs[:, t, cs], ps[:, 4 + 2 * half + t, :], 0.5, xs[:, t, cs], ALU.mult,
                                           ALU.add).then_inc(s_x1, 1)
            norm_rows(3)
            hT_half(3, v("g4"), None)
            split_tokens(3, hTs[:, 0], hTs[:, 1])

            cw = v("conv2").rearrange("p (f n) -> p f n", n=4)

            def feed(i, b, low):
                dve.wait_ge(s_gate, NE + 2 * i + b + 1)
                acc, z, th = ft[:, b, :], ft[:, 3, :], tmp[:, 0, :]
                for f in range(2):
                    src = ps[:, 4 + 2 * b, f * T:(f + 1) * T]
                    par = cw[:, bass.ds(4 * i + 2 * b + f, 1), :].rearrange("p a n -> p (a n)")
                    d = acc[:, f * T:(f + 1) * T]
                    link(V.tensor_scalar(d, src, par[:, 2:3], par[:, 3:4], ALU.mult, ALU.add))
                    for k in (1, 2):
                        ins = V.scalar_tensor_tensor(d[:, k:T], src[:, 0:T - k], par[:, 2 - k:3 - k], d[:, k:T],
                                                     ALU.mult, ALU.add)
                        if (f, k) != (1, 2):
                            link(ins)
                ins.then_inc(s_fsq, 1)
                dve.wait_ge(s_fz, 2 * i + b + 1)
                link(V.tensor_scalar(z, ft[:, 2, :], 0.044715, 1.0, ALU.mult, ALU.add))
                V.tensor_tensor(z, z, acc, ALU.mult).then_inc(s_fth, 1)
                low()
                dve.wait_ge(s_ffn, 2 * i + b + 1)
                link(V.scalar_tensor_tensor(z, th, 1.0, acc, ALU.add, ALU.mult))
                dve.wait_ge(s_gup, NE + 2 * i + b + 1)
                V.tensor_tensor(z, z, ps[:, 5 + 2 * b, :], ALU.mult).then_inc(s_a2, 1)
                dve.wait_ge(s_a2, NE + 2 * i + b + 2)
                split_act(z, b, 2 * i + b, DN2)

            stream(feed, 16, len(ALL), NE, FP)
            dve.wait_ge(s_dnp, DN2 + FP)
            for t in range(NT):
                for half in range(2):
                    cs = slice(512 * half, 512 * (half + 1))
                    V.scalar_tensor_tensor(xs[:, t, cs], ps[:, 2 * t + half, :], 0.5, xs[:, t, cs], ALU.mult, ALU.add
                                           ).then_inc(s_x1, 1)
            final_norm(1, hn)


def constants():
    c = np.zeros((P, NCONST), np.float32)

    def put(name, value):
        lo, hi = CONST[name]
        c[:, lo:hi] = np.asarray(value, np.float32).reshape(-1, hi - lo)

    put("ident", np.eye(P))
    put("ones", np.ones((P, P)))
    p = np.arange(P)
    put("tri", p[:, None] <= p[None, :])
    inv = np.float32(1.0) / (np.float32(10000.0) ** (np.arange(0, ROPE, 2, dtype=np.float32) / np.float32(ROPE)))
    ang = (np.arange(T, dtype=np.float32)[:, None] * inv[None, :]).T.astype(np.float32)
    put("cos", np.tile(np.cos(ang), (4, 1)))
    put("sin", np.concatenate([-np.sin(ang), np.sin(ang)] * 2, 0))
    q = np.concatenate([np.repeat(p[:, None], P, 1), np.repeat(P + p[:, None], T, 1)], 1)
    k = np.concatenate([np.repeat(p[None, :], P, 0), np.repeat(np.arange(T)[None, :], P, 0)], 1)
    put("chunk", np.where(k // 64 <= q // 64, 0.0, NEG))
    d = q - k
    put("causal", np.where(d >= 0, 0.0, NEG))
    put("dist", np.where(d >= 0, -d, NEG))
    put("dil", np.concatenate([np.where((d >= 0) & (d <= w) & (d % r == 0), -d, NEG)
                               for w, r in zip(DILW, DILR)], 1))
    end = np.arange(NC) * CS + CB - 1
    tok = (np.arange(NT)[None, :] * P + p[:, None])[:, :, None, None]
    seen = np.broadcast_to(end <= tok, (P, NT, NSAH, NC))
    slope = np.float32(NSA_SLOPE)[None, None, :, None]
    put("cbias", np.where(seen, -slope * (tok - end).astype(np.float32), np.float32(NEG)))
    put("cmask", seen)
    put("rank4", np.arange(NG, 0, -1)[None, :])
    put("rank8", np.arange(EG, 0, -1)[None, :])
    return c


def kernel(**inputs):
    import concourse.bacc as bacc
    from concourse.bass_utils import run_bass_kernel_spmd

    a = {k: np.asarray(x) for k, x in inputs.items()}

    def chunks(w):
        w = np.asarray(w)
        return w.reshape(w.shape[0] // P, P, -1).transpose(1, 0, 2)

    def flat(w):
        return chunks(w).reshape(P, -1)

    w1 = a["w_in"][0]
    o = np.cumsum([0, 512, 512, 1024, 1024, 4, 4, 384, 256, 64, 2048])
    qm, km, vm, om, im, fm, cq, ckv, kr, gp = (w1[:, o[i]:o[i + 1]] for i in range(10))
    uq = a["w_uq"][0].reshape(QL, AH, NOPE + ROPE)
    ukv = a["w_ukv"][0].reshape(KVL, AH, NOPE + VH)
    tiles = {"cq": np.concatenate([cq, im, fm], 1), "ckr": np.concatenate([ckv, kr, kr], 1), "qk0": qm, "qk1": km,
             "uqn": uq[:, :, :NOPE].reshape(QL, -1), "uqr": uq[:, :, NOPE:].reshape(QL, -1),
             "ukv": np.concatenate([ukv[:, :, :NOPE].reshape(KVL, -1), ukv[:, :, NOPE:].reshape(KVL, -1)], 1)}

    def halves(name, w):
        for i in range(w.shape[1] // 512):
            tiles[f"{name}{i}"] = w[:, 512 * i:512 * (i + 1)]

    for name, w in (("v", vm), ("o", om), ("g", gp), ("bm", a["w_branch_m"][0]), ("ba", a["w_branch_a"][0]),
                    ("out", a["w_out"][0])):
        halves(name, w)
    wa = np.ascontiguousarray(np.concatenate([flat(tiles[n]) for n, _, _ in LOADS], 1))

    w2, b2 = a["w_in_2"][0], a["b_in_2"][0]
    o2 = np.cumsum([0, 256, 256, 256, 4, 384, 384, 384, 384, 128, 128, 128, 128, 128, 128, 18, 3072])
    names = ("qa", "ka", "va", "fa", "qb", "kb", "vb", "qc", "kc", "vc", "ksl", "vsl", "kwn", "vwn", "gc", "gates")
    c2 = {n: w2[:, o2[i]:o2[i + 1]] for i, n in enumerate(names)}
    d2 = {n: b2[o2[i]:o2[i + 1]] for i, n in enumerate(names)}

    def pairs(w):
        return w.reshape(*w.shape[:-1], KVG, 3, HD).swapaxes(-3, -2).reshape(*w.shape)

    tiles.update({"fox": np.concatenate([c2["qa"], c2["ka"]], 1), "dilq": c2["qb"], "dilk": c2["kb"],
                  "nsaq": pairs(c2["qc"]), "kcvw": np.concatenate([c2["kc"], c2["vc"]], 1),
                  "kk": np.concatenate([c2["ksl"], c2["kwn"], c2["gc"], c2["fa"]], 1),
                  "vv": np.concatenate([c2["va"], c2["vsl"], c2["vwn"]], 1), "vb": c2["vb"],
                  "ck": a["cmp_k_w1_2"][0], "cv": a["cmp_v_w1_2"][0]})
    pc = a["w_pc_2"][0].reshape(KVG, 3, HD, D).swapaxes(0, 1).reshape(-1, D)
    for name, w in (("h", c2["gates"]), ("pa", a["w_pa_2"][0]), ("pb", a["w_pb_2"][0]), ("pc", pc),
                    ("wo", a["w_o_2"][0])):
        halves(name, w)
    wb = np.ascontiguousarray(np.concatenate([flat(tiles[n]) for n, _, _ in LOADS2 + LOADS3], 1))

    def triple(gate, up, dn):
        n = gate.shape[0]
        gu = [w.reshape(n, KD, P, DE).transpose(0, 2, 1, 3).reshape(n, P, -1) for w in (gate, up)]
        dn = dn.reshape(n, 2, P, D).transpose(0, 2, 1, 3).reshape(n, P, -1)
        return np.ascontiguousarray(np.concatenate(gu + [dn], 2))

    experts = triple(a["w_expert_gate"][0], a["w_expert_up"][0], a["w_expert_down"][0])
    up = a["w_up_2"][0]
    ffn = triple(up[:, :DFF].reshape(D, FP, DE).swapaxes(0, 1), up[:, DFF:].reshape(D, FP, DE).swapaxes(0, 1),
                 a["w_down_2"][0].reshape(FP, DE, D))
    mod = np.ascontiguousarray(a["mod_w"][0].reshape(KD, P, 12, 512).transpose(2, 1, 0, 3).reshape(12, P, -1))

    vecs = np.zeros((P, NVEC), np.float32)

    def put(name, value, rows=P):
        lo, hi = VEC[name]
        vecs[:rows, lo:hi] = np.asarray(value).reshape(rows, hi - lo)

    def col(x):
        return np.asarray(x).reshape(-1, P).T

    mb = a["mod_b"][0]
    put("c", col(a["c"][0]))
    put("mod1", col(mb[:2048]))
    put("mod2", col(mb[3072:5120]))
    for name, key in (("g1", "norm1_g"), ("g2", "norm2_g"), ("g3", "norm1_g_2"), ("g4", "norm2_g_2"),
                      ("convb", "conv_b"), ("qg", "q_norm_g"), ("kvg", "kv_norm_g")):
        put(name, col(a[key][0]))
    put("convw", a["conv_w"][0].reshape(CONV, 8, P).transpose(2, 1, 0))
    put("ib", a["igate_b"][0], MH)
    put("fb", a["fgate_b"][0], MH)
    put("b2f", col(np.concatenate([d2["qa"], d2["ka"], d2["qb"], d2["kb"], pairs(d2["qc"]), d2["kc"], d2["vc"],
                                   d2["ksl"], d2["kwn"]])))
    put("fab", d2["fa"], FOXH)
    put("conv2", np.concatenate([a["conv_w_2"][0], a["conv_b_2"]], 0).reshape(4, FB, P).transpose(2, 1, 0))
    put("pe", a["cmp_pe_2"][0].reshape(CB // 2, P).T)
    put("w2k", flat(a["cmp_k_w2_2"][0]))
    put("w2v", flat(a["cmp_v_w2_2"][0]))
    put("router", flat(np.concatenate([a["w_group"][0], a["w_router"][0]], 1)))
    rows = np.concatenate([mb[2048:3072], mb[5120:], a["final_norm_g"], a["final_g_2"], a["b_group"][0],
                           a["b_router"][0], d2["va"], d2["vsl"], d2["vwn"], d2["vb"], d2["gc"], d2["gates"]])[None, :]
    assert rows.shape[1] == NROW

    arrays = {"x": np.ascontiguousarray(a["x"]), "consts": constants(), "vecs": vecs,
              "rows": np.ascontiguousarray(rows), "mod": mod, "wa": wa, "experts": experts, "wb": wb, "ffn": ffn}
    nc = bacc.Bacc("TRN2", target_bir_lowering=False, num_devices=1)
    args = [nc.dram_tensor(f"in_{k}_dram", v.shape, F32, kind="ExternalInput").ap() for k, v in arrays.items()]
    out = nc.dram_tensor("out_dram", (1, T, D), F32, kind="ExternalOutput").ap()
    routing = nc.dram_tensor("routing_dram", (NE, T), F32).ap()
    build(nc, routing, *args, out)
    r = run_bass_kernel_spmd(nc, [{f"in_{k}_dram": v for k, v in arrays.items()}], core_ids=[0])
    return r.results[0]["out_dram"]
```

```python
from contextlib import ExitStack

import numpy as np

import concourse.bass as bass
from concourse import mybir

F32 = mybir.dt.float32
F32R = mybir.dt.float32r
BF16 = mybir.dt.bfloat16
ALU = mybir.AluOpType
ACT = mybir.ActivationFunctionType
AX = mybir.AxisListType

GELU = 0.7978845608028654
P = 128
RAW = 648
T, D = 256, 1024
NT, KD = T // P, D // P
EPS = 1e-6
NEG = -1e30
TINY = 1e-30
MH, MQK, MV = 4, 128, 256
AH, QL, KVL, NOPE, ROPE, VH = 8, 384, 256, 128, 64, 128
CONV = 4
NG, EG, NE, DE = 4, 8, 32, 256
HD = 64
FOXH, DILH, NSAH, KVG = 4, 6, 6, 2
DILW, DILR = (128, 512, 2048), (1, 4, 16)
CB, CS, CH = 32, 16, 256
NC = (T - CB) // CS + 1
DFF, FB = 2816, 2816 // 128
FP = FB // 2

SPAN = P + T


def columns(sizes):
    at, out = 0, {}
    for name, n in sizes:
        out[name] = (at, at + n)
        at += n
    return out, at


CONST, NCONST = columns([
    ("ident", P), ("ones", P), ("tri", P), ("cos", T), ("sin", T), ("chunk", SPAN), ("causal", SPAN),
    ("rank4", NG), ("rank8", EG), ("dist", SPAN), ("dil", 3 * SPAN), ("cbias", NT * NSAH * NC),
    ("cmask", NT * NSAH * NC)])
CONST1 = CONST["dist"][0]
VEC, NVEC = columns([
    ("c", KD), ("mod1", 16), ("mod2", 16), ("g1", KD), ("g2", KD), ("g3", KD), ("g4", KD), ("convw", 8 * CONV),
    ("convb", 8), ("qg", 3), ("kvg", 2), ("ib", 1), ("fb", 1), ("b2f", 17), ("fab", 1), ("conv2", FB * 4),
    ("pe", CB // 2), ("w2k", 2 * HD), ("w2v", 2 * HD), ("router", KD * (NG + NE))])
ROW, NROW = columns([("gate1", D), ("gate2", D), ("final1", D), ("final2", D), ("brouter", NG + NE),
                     ("b2v", 512), ("b2vb", 384), ("b2gc", 3 * NSAH), ("b2g", 3 * D)])

LOADS = [("cq", KD, QL + 2 * MH), ("ckr", KD, KVL + P), ("qk0", KD, 512), ("qk1", KD, 512), ("v0", KD, 512),
         ("v1", KD, 512), ("o0", KD, 512), ("o1", KD, 512), ("uqn", 3, 1024), ("uqr", 3, 512), ("ukv", 2, 2048),
         ("g0", KD, 512), ("g1", KD, 512), ("g2", KD, 512), ("g3", KD, 512),
         ("ba0", KD, 512), ("ba1", KD, 512), ("bm0", KD, 512), ("bm1", KD, 512), ("out0", KD, 512), ("out1", KD, 512)]
LOADS2 = [("fox", KD, 512), ("dilq", KD, 384), ("dilk", KD, 384), ("nsaq", KD, 384), ("kcvw", KD, 256),
          ("kk", KD, 256 + 3 * NSAH + FOXH), ("vv", KD, 512), ("vb", KD, 384),
          ("h0", KD, 512), ("h1", KD, 512), ("h2", KD, 512), ("h3", KD, 512), ("h4", KD, 512), ("h5", KD, 512),
          ("pa0", 2, 512), ("pa1", 2, 512), ("pb0", 3, 512), ("pb1", 3, 512), ("pc0", 3, 512), ("pc1", 3, 512),
          ("wo0", KD, 512), ("wo1", KD, 512)]
LOADS3 = [("ck", 16, CH), ("cv", 16, CH)]
SLOT = max(c * n for _, c, n in LOADS + LOADS2)
BIG = 21352
W3 = KD * DE
GU, DN = 2 * KD * DE, 2 * D


class Chain:

    def __init__(self, eng, sem):
        self.eng, self.sem, self.n, self.loop = eng, sem, 0, None

    def __call__(self, ins):
        self.n += 1
        ins.then_inc(self.sem, 1)
        self.eng.wait_ge(self.sem, self.n if self.loop is None else self.loop + self.n)

    def later(self, ins):
        self.n += 1
        ins.then_inc(self.sem, 1)

    def start(self, i, per):
        self.loop, self.per = i * per, per

    def end(self, trips):
        self.n += self.per * (trips - 1)
        self.loop = None


def units():
    out = [("fox", (h,)) for h in range(FOXH)]
    out += [("dil", tuple(2 * g + p for g in range(3))) for p in range(2)]
    for h in range(NSAH):
        out += [("sel", (h,)), ("win", (h,))]
    return out


UNITS1 = [("mla", (h,)) for h in range(AH)]
UNITS2 = units()
DIL_SLOPE = [2.0 ** (-8.0 * (2 * h + 1) / 12) for h in range(DILH)]
NSA_SLOPE = [2.0 ** (-8.0 * (2 * h + 2) / 12) for h in range(NSAH)]


def build(nc, routing, x, consts, vecs, rows, mod, wa, experts, wb, ffn, out):
    with ExitStack() as ctx:
        def sb(name, *shape, dt=F32):
            return ctx.enter_context(nc.sbuf_tensor(name, [P, *shape], dt))

        def here():
            return -(-nc.sbuf_base // 32) * 32

        def sem(name):
            return ctx.enter_context(nc.semaphore(name))

        ring_at = here()
        ring = sb("ring", 2, SLOT)
        dring_at = here()
        dring = sb("dring", 2, DN)
        cst_at = here()
        cst = sb("cst", NCONST)
        finalb = sb("finalb", D)
        sb("spare", 1200)
        vec_at = here()
        vec = sb("vec", NVEC)
        xs = sb("xs", NT, D)
        hn = sb("hn", NT, D)
        hT_at = here()
        hT = sb("hT", KD, T)
        gateb_at = here()
        gateb = sb("gateb", 2, D)
        modT = sb("modT", 48)
        small = sb("small", 512)
        att = sb("att", 2, 3, SPAN)
        pT = sb("pT", 3, SPAN)
        zero = sb("zero", 512, dt=BF16)
        big_at = here()
        big = sb("big", BIG)

        def const(name, a=0, b=None):
            lo, hi = CONST[name]
            return cst[:, lo + a:(hi if b is None else lo + b)]

        def v(name, a=0, b=None):
            lo, hi = VEC[name]
            return vec[:, lo + a:(hi if b is None else lo + b)]

        def row(name, a=0, b=None):
            lo, hi = ROW[name]
            return rows[0:1, lo + a:(hi if b is None else lo + b)].partition_broadcast(P)

        ident = const("ident")
        ones = const("ones")

        place = {}

        def part(name, at, *shape):
            n = int(np.prod(shape))
            place[name] = (at, at + n)
            assert at + n <= BIG, name
            ap = big[:, at:at + n]
            if len(shape) == 2:
                return ap.rearrange("p (a b) -> p a b", a=shape[0])
            if len(shape) == 3:
                return ap.rearrange("p (a b c) -> p a b c", a=shape[0], b=shape[1])
            return ap

        def after(name):
            return place[name][1]

        qkT = part("qkT", 0, 8, T)
        vaug = part("vaug", after("qkT"), NT, MH, MV + 1)
        og = part("og", after("vaug"), NT, D)
        qnT = part("qnT", after("og"), AH, T)
        qrT = part("qrT", after("qnT"), AH // 2, T)
        knT = part("knT", after("qrT"), AH, T)
        krT = part("krT", after("knT"), T)
        va = part("va", after("krT"), NT, D)
        ya = part("ya", after("va"), KD, T)
        wmem = part("wmem", after("ya"), 2 * SPAN)
        mpart = part("mpart", after("wmem"), 2, 512)
        lst = part("lst", after("wmem"), 8, T)
        part("ym", place["qkT"][0], KD, T)
        merged = part("merged", place["va"][0], NT, D)
        mtile = [part("mtile0", place["qnT"][0], KD, 512), part("mtile1", place["qnT"][0] + KD * 512, KD, 512)]
        assert after("mtile1") <= after("ya")
        gates = dring[:, :, :].rearrange("p a b -> p (a b)").rearrange("p (t n) -> p t n", t=NT)
        dflat = dring[:, :, :].rearrange("p a b -> p (a b)")
        raw = dflat[:, 0:NT * RAW].rearrange("p (t n) -> p t n", t=NT)
        cT = dflat[:, NT * RAW:NT * RAW + 5 * T].rearrange("p (c n) -> p c n", c=5)
        hflat = hn[:, :, :].rearrange("p t n -> p (t n)")
        aflat = att[:, :, :, :].rearrange("p a b c -> p (a b c)")
        rt = aflat[:, 0:1024]
        tmp = pT[:, :, :].rearrange("p a b -> p (a b)")[:, 0:2 * 2 * T].rearrange("p (b n) -> p b n", b=2)
        act32 = hflat[:, 0:2 * T]
        wbe = hflat[:, 2 * T:4 * T].rearrange("p (b n) -> p b n", b=2)

        def split(name, at, *shape):
            assert at + int(np.prod(shape)) <= BIG
            return nc.alloc_sbuf_tensor_at(name, [P, *shape], F32R, offset=big_at + 4 * at)

        wsp = split("wsp", 0, 3, 2, W3)
        hTs = split("hTs", 6 * W3, 2, KD, T)
        aTs = split("aTs", 6 * W3 + 2 * KD * T, 2, 2, 2, T)
        fmT = part("fmT", 0, 17, T)
        kvc = part("kvc", after("fmT"), 2, CB // 2, KVG * NC)
        tv = part("tv", after("kvc"), NT, 512)
        tvb = part("tvb", after("tv"), NT, 384)
        gc = part("gc", after("tvb"), NT, 3 * NSAH)
        g2 = part("g2", after("gc"), NT, 3 * D)
        hidT = part("hidT", after("g2"), 2, 2, KVG * NC)
        kcT = part("kcT", after("hidT"), KVG * NC)
        vc = part("vc", after("kcT"), KVG, HD)
        pcm = part("pcm", after("vc"), NT * NSAH, NC)
        fox = part("fox", after("pcm"), 4, T)
        gel = part("gel", after("fox"), 4, 2, 2 * KVG * NC)
        bias2 = part("bias2", after("gel"), NROW - ROW["b2v"][0])
        yT2 = hflat.rearrange("p (c n) -> p c n", c=8)
        pcT = part("pcT", after("bias2"), NSAH, T)
        merged2 = part("merged2", place["fmT"][0], NT, D)
        ckw = big[:, place["g2"][0]:place["g2"][0] + 4096].rearrange("p (c n) -> p c n", c=16)
        cvw = [big[:, place["g2"][0] + 4096:after("g2")].rearrange("p (c n) -> p c n", c=8),
               aflat[:, 0:2048].rearrange("p (c n) -> p c n", c=8)]
        hTh1 = nc.alloc_sbuf_tensor_at("hTh1", [P, KD, T], F32R, offset=big_at + 4 * (BIG - KD * T))
        hTh2 = nc.alloc_sbuf_tensor_at("hTh2", [P, KD, T], F32R, offset=gateb_at)
        hTl = nc.alloc_sbuf_tensor_at("hTl", [P, KD, T], F32R, offset=hT_at)
        wh1_at = -(-(cst_at + 4 * CONST1) // 32) * 32
        assert wh1_at + 4 * 4096 <= vec_at and after("lst") <= BIG - KD * T
        wh1 = nc.alloc_sbuf_tensor_at("wh1", [P, 4, 1024], F32R, offset=wh1_at)
        yah = split("yah", place["vaug"][0], KD, T)
        yal = split("yal", place["ya"][0], KD, T)
        yml = split("yml", place["ym"][0], KD, T)
        wh2 = nc.alloc_sbuf_tensor_at("wh2", [P, 4, 1024], F32R, offset=dring_at)
        wl = nc.alloc_sbuf_tensor_at("wl", [P, 2, SLOT], F32R, offset=ring_at)
        ft = hflat.rearrange("p (a n) -> p a n", a=4)

        ps = ctx.enter_context(nc.psum_tensor("ps", [P, 8, 512], F32))

        s_vec, s_const, s_const2, s_x, s_brow, s_final1, s_final2, s_bias2, s_out = (
            sem(n) for n in ("s_vec", "s_const", "s_const2", "s_x", "s_brow", "s_final1", "s_final2", "s_bias2", "s_out"))
        s_ring = [sem("s_ring0"), sem("s_ring1")]
        s_gu = [sem("s_gu0"), sem("s_gu1")]
        s_dn = [sem("s_dn0"), sem("s_dn1")]
        s_mt = [sem("s_mt0"), sem("s_mt1")]
        s_dnp = sem("s_dnp")
        c_dve, c_act, c_pool = sem("c_dve"), sem("c_act"), sem("c_pool")
        s_condt, s_mpart, s_msum, s_mev = (
            sem(n) for n in ("s_condt", "s_mpart", "s_msum", "s_mev"))
        s_ss, s_ms, s_rstd, s_tr, s_hTv, s_hTa = (
            sem(n) for n in ("s_ss", "s_ms", "s_rstd", "s_tr", "s_hTv", "s_hTa"))
        s_hn = [sem("s_hn0"), sem("s_hn1")]
        s_grp, s_gv, s_ga = sem("s_grp"), sem("s_gv"), sem("s_ga")
        s_conv, s_convt = sem("s_conv"), sem("s_convt")
        s_css, s_cms, s_crs, s_cn, s_ctr, s_cT = (sem(n) for n in ("s_css", "s_cms", "s_crs", "s_cn", "s_ctr", "s_cT"))
        s_lf, s_le, s_scan, s_em, s_gt, s_gte = (sem(n) for n in ("s_lf", "s_le", "s_scan", "s_em", "s_gt", "s_gte"))
        s_mS, s_mw, s_mexp, s_mst, s_mnum, s_mr, s_mh, s_my = (
            sem(n) for n in ("s_mS", "s_mw", "s_mexp", "s_mst", "s_mnum", "s_mr", "s_mh", "s_my"))
        s_sc, s_sfree, s_nm, s_exp, s_p, s_pt, s_pTc, s_pv, s_y = (
            sem(n) for n in ("s_sc", "s_sfree", "s_nm", "s_exp", "s_p", "s_pt", "s_pTc", "s_pv", "s_y"))
        s_yt, s_ymT = sem("s_yt"), sem("s_ymT")
        s_ya, s_yml, s_ml = sem("s_ya"), sem("s_yml"), sem("s_ml")
        s_brout = sem("s_brout")
        s_br, s_mrg, s_mt2, s_mT, s_pr, s_x1 = (sem(n) for n in ("s_br", "s_mrg", "s_mt2", "s_mT", "s_pr", "s_x1"))
        s_lg, s_re, s_rx, s_w32, s_wt, s_wtc, s_wst = (
            sem(n) for n in ("s_lg", "s_re", "s_rx", "s_w32", "s_wt", "s_wtc", "s_wst"))
        s_wb = [sem("s_wb0"), sem("s_wb1")]
        s_hi = [sem("s_hi_gate"), sem("s_hi_up"), sem("s_hi_down")]
        s_lo = [sem("s_lo_gate"), sem("s_lo_up"), sem("s_lo_down")]
        s_gate = sem("s_gate")
        s_hs = sem("s_hs")
        s_hsh = sem("s_hsh")
        s_qh, s_ql, s_qu = sem("s_qh"), sem("s_ql"), sem("s_qu")
        s_rq = [[sem(f"s_rq{slot}{q}") for q in range(4)] for slot in range(2)]
        s_cw = [sem("s_cw0"), sem("s_cw1")]
        s_gup, s_th, s_aT, s_a2 = (sem(n) for n in ("s_gup", "s_th", "s_aT", "s_a2"))
        s_xf, s_fss, s_fms, s_frs = (sem(n) for n in ("s_xf", "s_fss", "s_fms", "s_frs"))
        s_F, s_hid, s_hu, s_hth, s_hg, s_kc, s_kce = (
            sem(n) for n in ("s_F", "s_hid", "s_hu", "s_hth", "s_hg", "s_kc", "s_kce"))
        s_cs, s_ce, s_cx, s_cp, s_cpt, s_cpc = (sem(n) for n in ("s_cs", "s_ce", "s_cx", "s_cp", "s_cpt", "s_cpc"))
        s_fl, s_fsc, s_zero = sem("s_fl"), sem("s_fsc"), sem("s_zero")
        s_ggu, s_fsq, s_fz, s_fth, s_ffn = (sem(n) for n in ("s_ggu", "s_fsq", "s_fz", "s_fth", "s_ffn"))
        s_fe, s_gct = sem("s_fe"), sem("s_gct")

        ALL = LOADS + LOADS2
        NL = {name: n for n, (name, _, _) in enumerate(ALL)}
        offs = {}
        for stream in (LOADS, LOADS2 + LOADS3):
            at = 0
            for name, c, n in stream:
                offs[name] = (at, c * n)
                at += c * n

        def wtile(name):
            n = NL[name]
            _, c, m = ALL[n]
            return ring[:, n % 2, 0:c * m].rearrange("p (c n) -> p c n", c=c)

        def landed(eng, name):
            n = NL[name]
            eng.wait_ge(s_ring[n % 2], 16 * sum(1 for m in range(n % 2, n + 1, 2) if ALL[m][0] not in LI))

        GROUPS = [("misc0", "a"), ("misc1", "a"), ("ckv", "a"), ("kr", "v"), ("qk0", "v"), ("qk1", "v"), ("qk2", "v"),
                  ("qk3", "v")] + [(f"v{i}", "a") for i in range(4)] + [(f"o{i}", "a") for i in range(4)]
        GROUPS += [(f"qn{i}", "a") for i in range(4)] + [("qr0", "v"), ("qr1", "v")]
        GROUPS += [(f"kn{i}", "a") for i in range(4)] + [(f"va{i}", "v") for i in range(4)]
        GROUPS += [(f"g{i}", "a") for i in range(8)]
        GROUPS += [("fox0", "v"), ("fox1", "a"), ("dil0", "v"), ("dil1", "v"), ("dil2", "a"), ("dil3", "a"),
                   ("nsa0", "v"), ("nsa1", "v"), ("kcv", "v"), ("kk", "a"), ("gf", "v"), ("vv0", "v"), ("vv1", "v"),
                   ("vb0", "v"), ("vb1", "v")]
        GROUPS += [(f"h{i}", "v") for i in range(12)]
        VGROUPS = sum(1 for g in GROUPS if g[1] == "v")
        GI = {name: n for n, (name, _) in enumerate(GROUPS)}

        SPLIT = [("cq", ("misc0", "misc1")), ("ckr", ("ckv", "kr")), ("qk0", ("qk0", "qk1")), ("qk1", ("qk2", "qk3"))]
        SPLIT += [(f"{n}{q}", (f"{n}{2 * q}", f"{n}{2 * q + 1}")) for n, count in (("v", 2), ("o", 2), ("g", 4))
                  for q in range(count)]
        SPLIT += [(name, (f"{name}.0", f"{name}.1")) for name in ("ba0", "ba1", "bm0", "bm1", "out0", "out1")]
        L2 = len(SPLIT)
        SPLIT += [("fox", ("fox0", "fox1")), ("dilq", ("dil0", "dil1")), ("dilk", ("dil2", "dil3")),
                  ("nsaq", ("nsa0", "nsa1")), ("kcvw", ("kcv",)), ("kk", ("kk", "gf")), ("vv", ("vv0", "vv1")),
                  ("vb", ("vb0", "vb1"))] + [(f"h{q}", (f"h{2 * q}", f"h{2 * q + 1}")) for q in range(6)]
        SPLIT += [(name, (f"{name}.0", f"{name}.1")) for name in ("wo0", "wo1")]
        LI = {name: n for n, (name, _) in enumerate(SPLIT)}
        LG, LH = LI["g0"], LI["h0"]

        def quarter(name, q, kind):
            _, c, n = ALL[NL[name]]
            if kind == "high":
                return (wh1 if LI[name] < L2 else wh2)[:, q, 0:2 * n]
            return (wl if kind == "low" else ring)[:, NL[name] % 2, 1024 * q:1024 * q + 2 * n]

        def quarter_used(eng, n, q):
            if q < 3:
                eng.wait_ge(s_qu, 3 * n + q + 1)
            else:
                eng.wait_ge(*USED[SPLIT[n][0]])

        def quarter_landed(eng, name, q):
            slot = NL[name] % 2
            before = sum(1 for other, _ in SPLIT[:LI[name]] if NL[other] % 2 == slot)
            eng.wait_ge(s_rq[slot][q], 16 * (before + 1))

        GM = 2
        HM = 4
        BANK = {name: n % 4 for n, (name, _) in enumerate(GROUPS)}
        BANK.update({"v2": 4, "v3": 5, "qr0": 4, "qr1": 5})
        BANK.update({f"g{i}": 7 - 3 * i if i < GM else 5 - 3 * (i % 2) for i in range(8)})
        BANK.update({f"h{i}": (0, 1, 2, 0)[i] if i < HM else 5 - 3 * (i % 2) for i in range(12)})

        def bank(name):
            return ps[:, BANK[name], :]

        def emptied(eng, n):
            who = GROUPS[n][1]
            count = sum(1 for g in GROUPS[:n + 1] if g[1] == who)
            eng.wait_ge(s_ga if who == "a" else s_gv, count)

        def grouped(eng, name):
            eng.wait_ge(s_grp, GI[name] + 1)

        USED = {"cq": "misc1", "ckr": "kr", "qk0": "qk1", "qk1": "qk3", "v0": "v1", "v1": "v3", "uqn": "qn3",
                "uqr": "qr1", "ukv": "va3", "o0": "o1", "o1": "o3", "fox": "fox1", "dilq": "dil1", "dilk": "dil3",
                "nsaq": "nsa1", "kcvw": "kcv", "kk": "gf", "vv": "vv1", "vb": "vb1"}
        USED.update({f"g{q}": f"g{2 * q + 1}" for q in range(4)})
        USED.update({f"h{q}": f"h{2 * q + 1}" for q in range(6)})
        USED = {name: (s_grp, GI[g] + 1) for name, g in USED.items()}
        for n, name in enumerate(("ba0", "ba1", "bm0", "bm1", "pa0", "pa1", "pb0", "pb1", "pc0", "pc1")):
            USED[name] = (s_br, 2 * (n + 1))
        for n, name in enumerate(("out0", "out1", "wo0", "wo1")):
            USED[name] = (s_pr, 2 * (n + 1))

        def used(eng, n):
            eng.wait_ge(*USED[ALL[n][0]])

        DN2 = NE + 2

        NMOD = 12
        block = ctx.enter_context(nc.Block())

        @block.sync
        def _(sp):
            sp.dma_start(vec[:, :], vecs).then_inc(s_vec, 16)

            def mod_tile(j):
                if j >= 2:
                    sp.wait_ge(s_mpart, j - 1)
                sp.dma_start(mtile[j % 2], mod[j].rearrange("p (c n) -> p c n", c=KD)).then_inc(s_mt[j % 2], 16)

            def load(name, stream):
                n = NL[name]
                load_into(name, stream, n >= 2 and n - 2)

            def load_into(name, stream, last):
                n = NL[name]
                at, size = offs[name]
                if name not in LI:
                    if last is not False:
                        used(sp, last)
                    sp.dma_start(ring[:, n % 2, 0:size], stream[:, at:at + size]).then_inc(s_ring[n % 2], 16)
                    return
                for q in range(4):
                    if last is not False and ALL[last][0] in LI:
                        quarter_used(sp, LI[ALL[last][0]], q)
                    elif last is not False and q == 0:
                        used(sp, last)
                    sp.dma_start(quarter(name, q, "raw"), stream[:, at + q * size // 4:at + (q + 1) * size // 4]
                                 ).then_inc(s_rq[n % 2][q], 16)

            mod_tile(0)
            sp.dma_start(cst[:, 0:CONST1], consts[:, 0:CONST1]).then_inc(s_const, 16)
            mod_tile(1)
            sp.dma_start(xs[:, :, :], x.rearrange("b (t p) d -> p (b t) d", p=P)).then_inc(s_x, 16)
            mod_tile(2)
            mod_tile(3)
            load("cq", wa)
            load("ckr", wa)
            mod_tile(4)
            mod_tile(5)
            load("qk0", wa)
            sp.dma_start(gateb[:, 0, :], row("gate1")).then_inc(s_brow, 16)
            sp.dma_start(gateb[:, 1, :], row("gate2")).then_inc(s_brow, 16)
            mod_tile(6)
            load("qk1", wa)
            mod_tile(7)
            mod_tile(8)
            load("v0", wa)
            load("v1", wa)
            load("o0", wa)
            mod_tile(9)
            load("o1", wa)
            mod_tile(10)
            mod_tile(11)
            for name, _, _ in LOADS[8:]:
                load(name, wa)
            sp.dma_start(small[:, 448:448 + 36], row("brouter")).then_inc(s_brout, 16)

            n0 = len(LOADS)
            for e in range(2):
                used(sp, n0 - 2 + e)
                sp.dma_start(ring[:, (n0 + e) % 2, 0:GU], experts[e, :, 0:GU]).then_inc(s_gu[e], 16)
                if e == 0:
                    sp.wait_ge(s_mrg, 4)
                sp.dma_start(dring[:, e, :], experts[e, :, GU:GU + DN]).then_inc(s_dn[e], 16)
            sp.wait_ge(s_pr, 4)
            sp.dma_start(finalb[:, :], row("final1")).then_inc(s_final1, 16)
            sp.dma_start(cst[:, CONST1:], consts[:, CONST1:]).then_inc(s_const2, 16)
            sp.wait_ge(s_wtc, 1)
            sp.dma_start(routing, rt[0:NE, 384:384 + T]).then_inc(s_wst, 16)
            sp.wait_ge(s_wst, 16)
            for e in range(2):
                sp.dma_start(wbe[:, e, :], routing[e:e + 1, :].partition_broadcast(P)).then_inc(s_wb[e], 16)

            def element(i, b, src, slot0, count0):
                for m in (0, 1):
                    sp.wait_ge(s_lo[m], 2 * i + b + 1 + count0)
                row = src[bass.ds(2 * i + b + 2, 1)]
                sp.dma_start(ring[:, (slot0 + b) % 2, 0:GU], row[:, :, 0:GU].rearrange("a p n -> p (a n)")
                             ).then_inc(s_gu[b], 16)
                sp.wait_ge(s_lo[2], 2 * i + b + 1 + count0)
                sp.dma_start(dring[:, b, :], row[:, :, GU:GU + DN].rearrange("a p n -> p (a n)")
                             ).then_inc(s_dn[b], 16)

            with sp.Fori(0, NE // 2 - 1) as i:
                for b in range(2):
                    element(i, b, experts, n0, 0)
                    sp.wait_ge(s_aT, 2 * i + b + 1)
                    sp.dma_start(wbe[:, b, :], routing[bass.ds(2 * i + b + 2, 1), :].partition_broadcast(P)
                                 ).then_inc(s_wb[b], 16)

            first = True
            for name, _, _ in LOADS2:
                n = NL[name]
                if n - n0 < 2:
                    for m in (0, 1):
                        sp.wait_ge(s_lo[m], NE - 1 + (n - n0))
                load_into(name, wb, n - n0 >= 2 and n - 2)
                if first:
                    sp.wait_ge(s_dnp, NE + 1)
                    sp.dma_start(bias2, rows[0:1, ROW["b2v"][0]:NROW].partition_broadcast(P)
                                 ).then_inc(s_bias2, 16)
                    for i, name in enumerate(("ck", "cv")):
                        at, size = offs[name]
                        parts = ((ckw, size),) if i == 0 else ((cvw[0], size // 2), (cvw[1], size // 2))
                        for dst, size in parts:
                            sp.dma_start(dst, wb[:, at:at + size].rearrange("p (c n) -> p c n", n=CH)
                                         ).then_inc(s_cw[i], 16)
                            at += size
                    first = False

            n1 = len(ALL)
            for f in range(2):
                used(sp, n1 - 2 + f)
                sp.dma_start(ring[:, (n1 + f) % 2, 0:GU], ffn[f, :, 0:GU]).then_inc(s_gu[f], 16)
            sp.wait_ge(s_pr, 8)
            for f in range(2):
                sp.dma_start(dring[:, f, :], ffn[f, :, GU:GU + DN]).then_inc(s_dn[f], 16)
            sp.wait_ge(s_xf, 2)
            sp.dma_start(finalb[:, :], row("final2")).then_inc(s_final2, 16)
            with sp.Fori(0, FP // 2 - 1) as i:
                for b in range(2):
                    element(i, b, ffn, n1, NE)
            element(FP // 2 - 1, 0, ffn, n1, NE)

            sp.wait_ge(s_xf, 4)
            sp.dma_start(out.rearrange("b (t p) d -> p (b t) d", p=P), hn[:, :, :]).then_inc(s_out, 16)
            sp.wait_ge(s_out, 16)

        @block.tensor
        def _(pe):
            def group_start(name):
                last = [m for m in range(GI[name]) if BANK[GROUPS[m][0]] == BANK[name]]
                if last:
                    emptied(pe, last[-1])

            def mod_sum(j):
                pe.wait_ge(s_mpart, j + 1)
                if j in (4, 5, 6, 10, 11):
                    pe.wait_ge(s_mev, {4: 1, 5: 2, 6: 3, 10: 4, 11: 5}[j])
                pp = mpart[:, j % 2, :]
                if j in (4, 5, 10, 11):
                    mm = pe.matmul(ps[:, 7, :], ones, pp, start=True, stop=True)
                else:
                    col = 4 * j if j < 4 else 4 * (j - 6)
                    for i in range(4):
                        mm = pe.matmul(ps[:, 7, col + i:col + i + 1], pp[:, i * P:(i + 1) * P], ones[:, 0:1],
                                       start=True, stop=True)
                mm.then_inc(s_msum, 1)

            def turn_rows(k):
                for t in range(NT):
                    pe.wait_ge(s_hn[t], k + 1)
                    for c in range(KD):
                        mm = pe.transpose(ps[:, c // 2, (c % 2) * T + t * P:(c % 2) * T + (t + 1) * P],
                                          hn[:, t, c * P:(c + 1) * P], ident)
                        if t == NT - 1 and c % 2:
                            mm.then_inc(s_tr, 1)

            def hT_ready(k):
                pe.wait_ge(s_hTv, 4 * (k + 1))
                pe.wait_ge(s_hTa, 4 * (k + 1))

            def feature(name, w, cols, src, nk, out0=0, m=P):
                b = bank(name)
                for j, c0 in enumerate(cols):
                    for c in range(nk):
                        mm = pe.matmul(b[0:m, out0 + j * T:out0 + (j + 1) * T], w[:, c, c0:c0 + m], src[:, c, :],
                                       start=(c == 0), stop=(c == nk - 1))
                return mm

            def token(b, t, w, c0, c1, src, nk, at=0):
                for c in range(nk):
                    mm = pe.matmul(b[:, at:at + c1 - c0], src[:, c, t * P:(t + 1) * P], w[:, c, c0:c1],
                                   start=(c == 0), stop=(c == nk - 1))
                return mm

            def outputs_of(name):
                load = next(n for n, groups in SPLIT if name in groups)
                width = ALL[NL[load]][2]
                hl = (hTh1 if LI[load] < L2 else hTh2, hTl)

                def weights(c, a, b):
                    return [w.rearrange("p (c n) -> p c n", c=2)[:, c % 2, a:b] for w in
                            (quarter(load, c // 2, "high"), quarter(load, c // 2, "low"))]

                def tokens_by(t, a, b):
                    return lambda c: ([h[:, c, t * P:(t + 1) * P] for h in hl], weights(c, a, b))

                def features(a, m):
                    return lambda c: (weights(c, a, a + m), [h[:, c, :] for h in hl])

                if "." in name:
                    t, half = int(name[-1]), int(load[-1])
                    hl = {"ba": (yah, yal), "bm": (hTh1, yml), "out": (hTh1, hTl), "wo": (hTh2, hTl)}[load[:-1]]
                    return [(ps[:, (0 if load[:-1] == "bm" else 4) + 2 * half + t, :], tokens_by(t, 0, width))]
                b = bank(name)
                if load in ("cq", "vv", "vb") or (load[0] in "vogh" and load[1:].isdigit()):
                    return [(b[:, 0:width], tokens_by(dict(SPLIT)[load].index(name), 0, width))]
                if name == "ckv":
                    return [(b[:, t * KVL:(t + 1) * KVL], tokens_by(t, 0, KVL)) for t in range(NT)]
                if name == "kr":
                    return [(b[:, 0:T], features(KVL, P))]
                if name == "gf":
                    out = [(b[:, t * 3 * NSAH:(t + 1) * 3 * NSAH], tokens_by(t, 2 * P, 2 * P + 3 * NSAH))
                           for t in range(NT)]
                    return out + [(b[0:FOXH, T:2 * T], features(2 * P + 3 * NSAH, FOXH))]
                j = dict(SPLIT)[load].index(name)
                last = 2 * P if load == "kk" else width
                return [(b[:, n * T:(n + 1) * T], features(a, P))
                        for n, a in enumerate(range(2 * P * j, min(2 * P * (j + 1), last), P))]

            def split_quarter(n, q):
                load, groups = SPLIT[n]
                pe.wait_ge(s_ql, 4 * n + q + 1)
                if n in (0, L2) and q in (0, 2):
                    pe.wait_ge(s_hs, (0 if n == 0 else 4) + 1 + q // 2)
                for name in groups:
                    if q == 0 and name in GI:
                        group_start(name)
                    for p, (out, operands) in enumerate(outputs_of(name)):
                        for c in (2 * q, 2 * q + 1):
                            for k, (i, j) in enumerate(((0, 0), (0, 1), (1, 0))):
                                x, y = operands(c)
                                mm = pe.matmul(out, x[i], y[j], start=(p, c, k) == (0, 0, 0),
                                               stop=(c, k) == (KD - 1, 2), skip_group_check=True)
                    if q == 3:
                        mm.then_inc(USED[load][0], 1)
                if q < 3:
                    mm.then_inc(s_qu, 1)

            pe.wait_ge(s_const, 16)
            for j in range(3):
                mod_sum(j)
            turn_rows(0)
            mod_sum(3)
            hT_ready(0)
            def split_load(name):
                for q in range(4):
                    split_quarter(LI[name], q)

            split_load("cq")
            mod_sum(4)
            split_load("ckr")
            mod_sum(5)
            split_load("qk0")
            mod_sum(6)
            split_load("qk1")
            split_load("v0")
            split_load("v1")
            for name, sums in (("o0", ((7,), (8,))), ("o1", ((9,), (10, 11)))):
                for half in range(2):
                    split_quarter(LI[name], 2 * half)
                    split_quarter(LI[name], 2 * half + 1)
                    for j in sums[half]:
                        mod_sum(j)
            pe.wait_ge(s_cn, 2)
            emptied(pe, GI["v3"])
            for c in range(5):
                for t in range(NT):
                    at = (c % 2) * T + t * P
                    src = raw[:, t, c * P:(c + 1) * P] if c < 3 else raw[:, t, 392 + (c - 3) * P:392 + (c - 2) * P]
                    pe.transpose(ps[:, 4 + c // 2, at:at + P], src, ident)
            for t in range(NT):
                pe.transpose(ps[0:MH, 6, T + t * P:T + (t + 1) * P], raw[:, t, QL:QL + MH], ident)
            pe.wait_ge(s_mev, 6)
            for t in range(NT):
                mm = pe.transpose(ps[0:MH, 7, t * P:(t + 1) * P], raw[:, t, QL + MH:QL + 2 * MH], ident)
            mm.then_inc(s_ctr, 1)
            pe.wait_ge(s_cT, 1)
            landed(pe, "uqn")
            w = wtile("uqn")
            for i in range(4):
                group_start(f"qn{i}")
                mm = feature(f"qn{i}", w, [2 * i * P, (2 * i + 1) * P], cT, 3).then_inc(s_grp, 1)
            landed(pe, "uqr")
            w = wtile("uqr")
            for i in range(2):
                group_start(f"qr{i}")
                mm = feature(f"qr{i}", w, [2 * i * P, (2 * i + 1) * P], cT, 3).then_inc(s_grp, 1)
            landed(pe, "ukv")
            w = wtile("ukv")
            for i in range(4):
                group_start(f"kn{i}")
                feature(f"kn{i}", w, [2 * i * P, (2 * i + 1) * P], cT[:, 3:5, :], 2).then_inc(s_grp, 1)
            for i in range(4):
                group_start(f"va{i}")
                mm = token(bank(f"va{i}"), i % 2, w, 1024 + 512 * (i // 2), 1536 + 512 * (i // 2), cT[:, 3:5, :], 2)
                mm.then_inc(s_grp, 1)

            emptied(pe, GI["qr0"])
            pe.wait_ge(s_scan, 1)
            pe.wait_ge(s_em, 1)
            for t in range(NT):
                pe.transpose(ps[:, 4, t * MH:(t + 1) * MH], lst[0:MH, 2, t * P:(t + 1) * P], ident[0:MH, 0:MH])
                mm = pe.transpose(ps[:, 4, (2 + t) * MH:(3 + t) * MH], lst[0:MH, 5, t * P:(t + 1) * P],
                                  ident[0:MH, 0:MH])
            mm.then_inc(s_gt, 1)
            emptied(pe, GI["kn3"])
            emptied(pe, GI["va3"])

            def m_scores(h):
                if h >= 2:
                    pe.wait_ge(s_mst, h - 1)
                pe.matmul(ps[:, h % 2, 0:T], ident[0:MH, h:h + 1].to_broadcast([MH, P]), lst[0:MH, 4, :],
                          start=True, stop=True)
                pe.matmul(ps[:, 2 + h % 2, 0:T], qkT[:, 4 + h, 0:P], qkT[:, h, :], start=True, stop=True)
                pe.matmul(ps[:, 2 + h % 2, T:SPAN], qkT[:, 4 + h, P:T], qkT[:, h, P:T], start=True, stop=True
                          ).then_inc(s_mS, 1)

            def m_values(h):
                pe.wait_ge(s_mst, h + 1)
                if h >= 1:
                    pe.wait_ge(s_mh, 2 * h)
                w = wmem[:, (h % 2) * SPAN:(h % 2 + 1) * SPAN]
                pe.matmul(ps[:, 5, 0:MV + 1], w[:, 0:P], vaug[:, 0, h, :], start=True, stop=True)
                pe.matmul(ps[:, 6, 0:MV + 1], w[:, P:T], vaug[:, 0, h, :], start=True, stop=False)
                pe.matmul(ps[:, 6, 0:MV + 1], w[:, T:SPAN], vaug[:, 1, h, :], start=False, stop=True
                          ).then_inc(s_mnum, 1)

            pe.wait_ge(s_gte, 1)
            for h in range(MH + 1):
                if h < MH:
                    m_scores(h)
                if h >= 1:
                    split_quarter(LG, h - 1)
                if h >= 1:
                    m_values(h - 1)

            def attention(todo, set0, unit0, out0, scores, value, outputs, finished, fill):
                at = []
                n = set0
                for _, heads in todo:
                    at.append(n)
                    n += len(heads)
                o = out0
                for u in range(len(todo) + 1):
                    if u < len(todo):
                        kind, heads = todo[u]
                        for g, h in enumerate(heads):
                            s = at[u] + g
                            if s - set0 >= 2:
                                pe.wait_ge(s_sfree, s - 1)
                            scores(ps[:, s % 2, 0:SPAN], kind, h).then_inc(s_sc, 1)
                    if u < 1:
                        fill(u)
                    if u >= 1:
                        kind, heads = todo[u - 1]
                        pe.wait_ge(s_p, unit0 + u)
                        for g, h in enumerate(heads):
                            s = at[u - 1] + g
                            if s - set0 >= 2:
                                pe.wait_ge(s_pTc, s - 1)
                            src = att[:, (unit0 + u - 1) % 2, g, :]
                            b = ps[:, 3 + s % 2, :]
                            pe.transpose(b[:, 0:P], src[:, 0:P], ident)
                            pe.transpose(b[:, P:T], src[:, P:T], ident)
                            pe.transpose(b[:, T:SPAN], src[:, T:SPAN], ident).then_inc(s_pt, 1)
                        if u < len(todo):
                            fill(u)
                        for g, h in enumerate(heads):
                            s = at[u - 1] + g
                            pe.wait_ge(s_pTc, s + 1)
                            lo, hi = outputs(kind, h)
                            first, last = finished(kind)
                            if first and o - out0 >= 2:
                                pe.wait_ge(s_y, o - 1)
                            dst = ps[lo:hi, 6 + o % 2, :]
                            if first and kind == "sel":
                                pe.matmul(dst[:, 0:T], vc[0:NC, h // 3, :], pcT[0:NC, h, :], start=True, stop=False,
                                          skip_group_check=True)
                            v0, v1 = value(kind, h)
                            pe.matmul(dst[:, 0:T], v0, pT[:, s % 3, 0:T], start=first and kind != "sel", stop=False,
                                      skip_group_check=True)
                            pe.matmul(dst[:, P:T], v1, pT[:, s % 3, T:SPAN], start=False, stop=last,
                                      skip_group_check=True).then_inc(s_pv, 1)
                            if last:
                                o += 1

            def scores1(b, kind, h):
                r = (h % 2) * ROPE
                for lo, q0, n in ((0, 0, P), (P, P, T)):
                    pe.matmul(b[:, lo:lo + n], qnT[:, h, q0:q0 + P], knT[:, h, 0:n], start=True, stop=False)
                    mm = pe.matmul(b[:, lo:lo + n], qrT[r:r + ROPE, h // 2, q0:q0 + P], krT[r:r + ROPE, 0:n],
                                   start=False, stop=True)
                return mm

            pe.wait_ge(s_mw, 2 * MH)
            pe.wait_ge(s_mh, 2 * MH)
            emptied(pe, GI["g1"])
            attention(UNITS1, 0, 0, 0, scores1,
                      lambda kind, h: (va[:, 0, h * VH:(h + 1) * VH], va[:, 1, h * VH:(h + 1) * VH]),
                      lambda kind, h: (0, P), lambda kind: (True, True),
                      lambda u: [split_quarter(LG + 1 + u // 2, 2 * (u % 2) + k) for k in range(2)] if u < 6 else None)
            pe.wait_ge(s_my, 2 * MH)
            pe.wait_ge(s_sfree, AH)
            pe.wait_ge(s_pTc, AH)
            emptied(pe, GI["g7"])
            for c in range(KD):
                for t in range(NT):
                    mm = pe.transpose(ps[:, c // 2, (c % 2) * T + t * P:(c % 2) * T + (t + 1) * P],
                                      og[:, t, c * P:(c + 1) * P], ident)
                if c % 2:
                    mm.then_inc(s_yt, 1)
            pe.wait_ge(s_y, AH)
            pe.wait_ge(s_ya, AH)
            split_load("ba0")
            split_load("ba1")
            pe.wait_ge(s_yml, 4)
            split_load("bm0")
            split_load("bm1")

            def turn_merged(k):
                pe.wait_ge(s_mrg, 4 * (k + 1))
                for c in range(KD):
                    for t in range(NT):
                        mm = pe.transpose(ps[:, c // 2, (c % 2) * T + t * P:(c % 2) * T + (t + 1) * P],
                                          (merged if k == 0 else merged2)[:, t, c * P:(c + 1) * P], ident)
                    if c % 2:
                        mm.then_inc(s_mt2, 1)
                pe.wait_ge(s_ml, 4 * (k + 1))

            turn_merged(0)
            split_load("out0")
            split_load("out1")
            turn_rows(1)
            hT_ready(1)
            wr = v("router").rearrange("p (c n) -> p c n", c=KD)
            for t in range(NT):
                mm = token(ps[:, 0, :], t, wr, 0, NG + NE, hT, KD, at=t * (NG + NE))
            mm.then_inc(s_lg, 1)

            def prod(out, w, x, start, stop, skip=False):
                for n, (a, b) in enumerate(((0, 0), (0, 1), (1, 0))):
                    mm = pe.matmul(out, w[a], x[b], start=start and n == 0, stop=stop and n == 2,
                                   skip_group_check=skip)
                return mm

            def gate_or_up(m, pb, count, tokens=None):
                pe.wait_ge(s_lo[m], count)
                w = wsp[:, m, :, :].rearrange("p s (c n) -> p s c n", c=KD)
                for f in range(2):
                    for c in range(KD):
                        if tokens is not None and f == 0 and c in (0, 4):
                            pe.wait_ge(s_hs, tokens + 1 + c // 4)
                        mm = prod(ps[:, pb + m, f * T:(f + 1) * T], [w[:, s, c, f * P:(f + 1) * P] for s in range(2)],
                                  [hTs[:, s, c, :] for s in range(2)], c == 0, c == KD - 1)
                mm.then_inc(s_gup if m else s_gate, 1)

            def down(b, count):
                pe.wait_ge(s_lo[2], count)
                w = wsp[:, 2, :, :].rearrange("p s (f n) -> p s f n", f=2)
                for f in range(2):
                    for t in range(NT):
                        for n in range(2):
                            mm = prod(ps[:, 2 * t + n, :], [aTs[:, b, s, f, t * P:(t + 1) * P] for s in range(2)],
                                      [w[:, s, f, n * 512:(n + 1) * 512] for s in range(2)], False, False, True)
                mm.then_inc(s_dnp, 1)

            gate_or_up(0, 4, 1, 2)
            gate_or_up(1, 4, 1)
            pe.wait_ge(s_w32, 1)
            for t in range(NT):
                mm = pe.transpose(ps[0:NE, 1, t * P:(t + 1) * P], rt[:, 256 + t * NE:256 + (t + 1) * NE], ident)
            mm.then_inc(s_wt, 1)
            pe.wait_ge(s_wtc, 1)

            def open_sums():
                for b in range(4):
                    mm = pe.matmul(ps[:, b, :], zero[:, 0:P], zero[:, :], start=True, stop=False,
                                   skip_group_check=True)
                mm.then_inc(s_dnp, 1)

            pe.wait_ge(s_zero, 1)
            open_sums()

            def stream(count0, total):
                read0 = count0 + 1

                def step(i, b):
                    e = 2 * i + b
                    pb = 6 - 2 * b
                    pe.wait_ge(s_a2, e + read0)
                    gate_or_up(0, pb, e + count0 + 2)
                    gate_or_up(1, pb, e + count0 + 2)
                    pe.wait_ge(s_aT, e + count0 + 1)
                    down(b, e + count0 + 1)

                pairs = (total - 1) // 2
                with pe.Fori(0, pairs) as i:
                    step(i, 0)
                    step(i, 1)
                if 2 * pairs < total - 1:
                    step(pairs, 0)
                pe.wait_ge(s_aT, count0 + total)
                down((total - 1) % 2, count0 + total)

            stream(0, NE)

            turn_rows(2)
            hT_ready(2)

            for n in range(L2, LH):
                for q in range(4):
                    split_quarter(n, q)
            pe.wait_ge(s_F, 1)
            for i in range(2):
                pe.wait_ge(s_cw[i], 16 * (i + 1))
                for m in range(2):
                    for j in range(CB // 2):
                        w = ckw[:, j] if i == 0 else cvw[j // 8][:, j % 8]
                        mm = pe.matmul(ps[:, 4 + i, m * 30:(m + 1) * 30], w[:, m * P:(m + 1) * P], kvc[:, i, j, :],
                                       start=(j == 0), stop=(j == CB // 2 - 1))
                mm.then_inc(s_hid, 1)
            for q in range(4):
                split_quarter(LH, q)
            pe.wait_ge(s_hg, 1)
            w2k = v("w2k").rearrange("p (c n) -> p c n", c=2)
            w2v = v("w2v").rearrange("p (c n) -> p c n", c=2)
            for g in range(KVG):
                for c in range(2):
                    pe.matmul(ps[g * HD:(g + 1) * HD, 6, 0:NC], w2k[:, c, :], hidT[:, 0, c, g * NC:(g + 1) * NC],
                              start=(c == 0), stop=(c == 1))
                for c in range(2):
                    mm = pe.matmul(ps[0:NC, 7, g * HD:(g + 1) * HD], hidT[:, 1, c, g * NC:(g + 1) * NC], w2v[:, c, :],
                                   start=(c == 0), stop=(c == 1))
            mm.then_inc(s_kc, 1)
            split_quarter(LH + 1, 0)
            split_quarter(LH + 1, 1)
            pe.wait_ge(s_kce, 1)
            emptied(pe, GI["vb1"])
            for t in range(NT):
                for h in range(NSAH):
                    g, r = h // 3, h % 3
                    q = fmT[g * HD:(g + 1) * HD, 10 + r, t * P:(t + 1) * P]
                    at = (3 * t + r) * NC
                    mm = pe.matmul(ps[:, 3 + g, at:at + NC], q, kcT[g * HD:(g + 1) * HD, 0:NC], start=True, stop=True)
            mm.then_inc(s_cs, 1)
            split_quarter(LH + 1, 2)
            split_quarter(LH + 1, 3)
            pe.wait_ge(s_cp, 1)
            for h in range(NSAH):
                for t in range(NT):
                    at = (h % 2) * T + t * P
                    mm = pe.transpose(ps[0:NC, 5 + h // 2, at:at + P], pcm[:, t * NSAH + h, :], ident)
            mm.then_inc(s_cpt, 1)
            pe.wait_ge(s_cpc, 3)
            pe.wait_ge(s_fsc, 1)
            emptied(pe, GI["h3"])

            def scores2(b, kind, h):
                if kind == "fox":
                    r, q, k = h % 2, fmT[:, h // 2, :], fmT[:, 2 + h // 2, :]
                elif kind == "dil":
                    r, q, k = h % 2, fmT[:, 4 + h // 2, :], fmT[:, 7 + h // 2, :]
                else:
                    r, q, k = h // 3, fmT[:, 10 + h % 3, :], fmT[:, 15 if kind == "sel" else 16, :]
                r = r * HD
                for lo, q0, n in ((0, 0, P), (P, P, T)):
                    mm = pe.matmul(b[:, lo:lo + n], q[r:r + HD, q0:q0 + P], k[r:r + HD, 0:n], start=True,
                                   stop=kind != "fox")
                    if kind == "fox":
                        mm = pe.matmul(b[:, lo:lo + n], ident[0:FOXH, h:h + 1].to_broadcast([FOXH, P]),
                                       fox[0:FOXH, 3, 0:n], start=False, stop=True)
                return mm

            def value2(kind, h):
                if kind == "fox":
                    return tv[:, 0, h * HD:(h + 1) * HD], tv[:, 1, h * HD:(h + 1) * HD]
                if kind == "dil":
                    return tvb[:, 0, h * HD:(h + 1) * HD], tvb[:, 1, h * HD:(h + 1) * HD]
                at = (256 if kind == "sel" else 384) + (h // 3) * HD
                return tv[:, 0, at:at + HD], tv[:, 1, at:at + HD]

            def outputs2(kind, h):
                r = h // 3 if kind in ("sel", "win") else h % 2
                return r * HD, (r + 1) * HD

            attention(UNITS2, AH, AH, AH, scores2, value2, outputs2,
                      lambda kind: (kind != "win", kind != "sel"),
                      lambda u: split_quarter(LH + 2 + u // 4, u % 4) if u < 16 else None)
            pe.wait_ge(s_y, AH + FOXH + DILH + NSAH)
            for i, (br, c0, nk) in enumerate((("pa", 0, 2), ("pb", 2, 3), ("pc", 5, 3))):
                for half in range(2):
                    landed(pe, f"{br}{half}")
                    w = wtile(f"{br}{half}")
                    for t in range(NT):
                        if i == 2:
                            pe.wait_ge(s_gv, VGROUPS + 2 * half + t + 1)
                        mm = token(ps[:, 4 * (i % 2) + 2 * half + t, :], t, w, 0, 512, yT2[:, c0:c0 + nk, :], nk
                                   ).then_inc(s_br, 1)
            turn_merged(1)
            split_load("wo0")
            split_load("wo1")
            turn_rows(3)
            hT_ready(3)
            gate_or_up(0, 4, NE + 1, 6)
            gate_or_up(1, 4, NE + 1)
            open_sums()
            stream(NE, FP)

        @block.scalar
        def _(act):
            link = Chain(act, c_act)
            act.wait_ge(s_vec, 16)
            nc.scalar.activation(small[:, 0:KD], v("c"), ACT.Tanh, scale=0.5).then_inc(s_condt, 1)

            def row_squares(k):
                for t in range(NT):
                    if k == 2:
                        act.wait_ge(s_xf, t + 1)
                    link(nc.scalar.activation(hn[:, t, :], xs[:, t, :], ACT.Square,
                                              accum_out=small[:, 16 + t:17 + t]))
                act.nop().then_inc(s_ss, 1)

            def scaled_rows(k):
                act.wait_ge(s_rstd, k + 1)
                nc.scalar.activation(hn[:, 1, :], xs[:, 1, :], ACT.Copy, scale=small[:, 19:20]).then_inc(s_hn[1], 1)

            def hT_half(k, scale, shift):
                for c in range(4):
                    if c % 2 == 0:
                        act.wait_ge(s_tr, 4 * k + c // 2 + 1)
                    src = ps[:, c // 2, (c % 2) * T:(c % 2 + 1) * T]
                    if shift is None:
                        nc.scalar.activation(hT[:, c, :], src, ACT.Copy, scale=scale[:, c:c + 1]).then_inc(s_hTa, 1)
                    else:
                        nc.scalar.activation(hT[:, c, :], src, ACT.Identity, scale=scale[:, c:c + 1],
                                             bias=shift[:, c:c + 1]).then_inc(s_hTa, 1)

            def tokens_high(n, dst):
                act.wait_ge(s_hTa, 4 * (n + 1))
                nc.scalar.activation(dst[:, 0:4, :], hT[:, 0:4, :], ACT.Copy).then_inc(s_hsh, 1)

            def weights_high(n, quarters=(0, 1, 2, 3)):
                name = SPLIT[n][0]
                for q in quarters:
                    quarter_landed(act, name, q)
                    if n:
                        quarter_used(act, n - 1, q)
                    nc.scalar.activation(quarter(name, q, "high"), quarter(name, q, "raw"), ACT.Copy).then_inc(s_qh, 1)

            act.wait_ge(s_x, 16)
            row_squares(0)
            scaled_rows(0)
            weights_high(LI["cq"], (0,))
            act.wait_ge(s_mev, 1)
            hT_half(0, modT[:, 32:40], modT[:, 0:8])
            tokens_high(0, hTh1)
            weights_high(LI["cq"], (1, 2, 3))
            weights_high(LI["ckr"], (0, 1, 2))
            for t in range(NT):
                grouped(act, f"misc{t}")
                nc.scalar.copy(raw[:, t, 0:392], bank(f"misc{t}")[:, 0:392]).then_inc(s_ga, 1)
            weights_high(LI["ckr"], (3,))
            weights_high(LI["qk0"], (0, 1, 2))
            grouped(act, "ckv")
            for t in range(NT):
                ins = nc.scalar.copy(raw[:, t, 392:RAW], bank("ckv")[:, t * KVL:(t + 1) * KVL])
            ins.then_inc(s_ga, 1)
            weights_high(LI["qk0"], (3,))
            act.wait_ge(s_ga, 3)
            for t in range(NT):
                link(nc.scalar.activation(att[:, 0, 0, :], raw[:, t, 0:QL], ACT.Square,
                                          accum_out=small[:, 20 + t:21 + t]))
                link(nc.scalar.activation(att[:, 0, 0, 0:KVL], raw[:, t, 392:RAW], ACT.Square,
                                          accum_out=small[:, 22 + t:23 + t]))
            act.nop().then_inc(s_css, 1)
            weights_high(LI["qk1"])

            def conv_tanh(i):
                if i >= 1:
                    act.wait_ge(s_gv, i + 1)
                act.wait_ge(s_conv, i + 1)
                nc.scalar.activation(att[:, 1, 0:2, 0:T], hn[:, i % 2, 0:512].rearrange("p (a b) -> p a b", a=2), ACT.Tanh,
                                     scale=0.5).then_inc(s_convt, 1)

            def values_out(i):
                grouped(act, f"v{i}")
                src = bank(f"v{i}").rearrange("p (h d) -> p h d", h=2)
                nc.scalar.copy(vaug[:, i % 2, 2 * (i // 2):2 * (i // 2) + 2, 0:MV], src).then_inc(s_ga, 1)

            def out_gate(i):
                grouped(act, f"o{i}")
                nc.scalar.activation(og[:, i % 2, 512 * (i // 2):512 * (i // 2 + 1)], bank(f"o{i}"), ACT.Tanh,
                                     scale=0.5).then_inc(s_ga, 1)

            weights_high(LI["v0"], (0,))
            conv_tanh(0)
            weights_high(LI["v0"], (1, 2))
            conv_tanh(1)
            weights_high(LI["v0"], (3,))
            weights_high(LI["v1"], (0,))
            conv_tanh(2)
            weights_high(LI["v1"], (1, 2))
            conv_tanh(3)
            values_out(0)
            values_out(1)
            weights_high(LI["v1"], (3,))
            weights_high(LI["o0"], (0, 1, 2))
            values_out(2)
            values_out(3)
            weights_high(LI["o0"], (3,))
            weights_high(LI["o1"], (0, 1, 2))
            out_gate(0)
            out_gate(1)
            weights_high(LI["o1"], (3,))
            out_gate(2)
            out_gate(3)
            for i in range(4):
                grouped(act, f"qn{i}")
                if i == 0:
                    act.wait_ge(s_mpart, NMOD)
                nc.scalar.copy(qnT[:, 2 * i:2 * i + 2, :], bank(f"qn{i}").rearrange("p (a b) -> p a b", a=2)
                               ).then_inc(s_ga, 1)
            act.wait_ge(s_lf, 1)
            link(nc.scalar.activation(lst[0:MH, 6, :], lst[0:MH, 5, :], ACT.Exp, scale=-1.0))
            nc.scalar.activation(lst[0:MH, 7, :], lst[0:MH, 6, :], ACT.Ln, bias=1.0).then_inc(s_le, 1)
            for i in range(4):
                grouped(act, f"kn{i}")
                nc.scalar.copy(knT[:, 2 * i:2 * i + 2, :], bank(f"kn{i}").rearrange("p (a b) -> p a b", a=2)
                               ).then_inc(s_ga, 1)
            act.wait_ge(s_scan, 1)
            nc.scalar.activation(lst[0:MH, 5, :], lst[0:MH, 3, :], ACT.Exp, scale=-1.0).then_inc(s_em, 1)

            def gate_tanh(i):
                if i == 0:
                    act.wait_ge(s_grp, GI["va3"] + 1)
                grouped(act, f"g{i}")
                nc.scalar.activation(gates[:, i % 2, 512 * (i // 2):512 * (i // 2 + 1)], bank(f"g{i}"), ACT.Tanh,
                                     scale=0.5).then_inc(s_ga, 1)

            weights_high(LG)

            def m_out(h):
                for t in range(NT):
                    act.wait_ge(s_mr, 2 * h + t + 1)
                    nc.scalar.activation(hn[:, t, h * MV:(h + 1) * MV], ps[:, 5 + t, 0:MV], ACT.Copy,
                                         scale=small[:, 82 + 2 * (h % 2) + t:83 + 2 * (h % 2) + t]).then_inc(s_mh, 1)

            for h in range(MH):
                act.wait_ge(s_mw, 2 * (h + 1))
                w = att[:, h % 2, 0, :]
                nc.scalar.activation(w, w, ACT.Exp).then_inc(s_mexp, 1)
                if h >= 1:
                    weights_high(LG + 1, (h - 1,))
                if h >= 1:
                    m_out(h - 1)
            weights_high(LG + 1, (3,))
            gate_tanh(0)
            gate_tanh(1)
            m_out(MH - 1)

            def gates_beside(u):
                if u in (1, 3, 5):
                    gate_tanh(u + 1)
                    gate_tanh(u + 2)
                if u < 6:
                    weights_high(LG + 2 + u // 2, (2 * (u % 2), 2 * (u % 2) + 1))


            def attention(todo, set0, unit0, out0, scale, dest, last_of, fill):
                n, at = set0, []
                for _, heads in todo:
                    at.append(n)
                    n += len(heads)
                o = out0
                for u in range(len(todo) + 1):
                    if u < len(todo):
                        kind, heads = todo[u]
                        ui = unit0 + u
                        g = len(heads)
                        act.wait_ge(s_nm, ui + 1)
                        a = att[:, ui % 2, 0:g, :]
                        sm = small[:, 32 + 8 * (ui % 2):40 + 8 * (ui % 2)]
                        nc.scalar.activation(a[:, :, 0:P], a[:, :, 0:P], ACT.Exp, scale=scale, bias=sm[:, 0:1],
                                             accum_out=sm[:, 2:3])
                        nc.scalar.activation(a[:, :, P:SPAN], a[:, :, P:SPAN], ACT.Exp, scale=scale, bias=sm[:, 1:2],
                                             accum_out=sm[:, 3:4]).then_inc(s_exp, 1)
                    if u >= 1:
                        kind, heads = todo[u - 1]
                        for g, h in enumerate(heads):
                            s = at[u - 1] + g
                            act.wait_ge(s_pt, s + 1)
                            if s >= 3:
                                act.wait_ge(s_pv, s - 2)
                            nc.scalar.copy(pT[:, s % 3, :], ps[:, 3 + s % 2, 0:SPAN]).then_inc(s_pTc, 1)
                        if last_of(kind):
                            for g, h in enumerate(heads):
                                act.wait_ge(s_pv, at[u - 1] + g + 1)
                                d, lo, hi = dest(kind, h)
                                nc.scalar.copy(d, ps[lo:hi, 6 + o % 2, 0:T]).then_inc(s_y, 1)
                                o += 1
                    fill(u)

            attention(UNITS1, 0, 0, 0, float((NOPE + ROPE) ** -0.5), lambda kind, h: (ya[:, h, :], 0, P),
                      lambda kind: True, gates_beside)
            for b in range(4):
                act.wait_ge(s_yt, b + 1)
                nc.scalar.copy(hTh1[:, 2 * b:2 * b + 2, :], ps[:, b, :].rearrange("p (a b) -> p a b", a=2)
                               ).then_inc(s_ymT, 1)

            def merged_high(k, dst):
                for b in range(4):
                    act.wait_ge(s_mt2, 4 * k + b + 1)
                    nc.scalar.copy(dst[:, 2 * b:2 * b + 2, :], ps[:, b, :].rearrange("p (a b) -> p a b", a=2)
                                   ).then_inc(s_mT, 1)

            for name in ("ba1", "bm0", "bm1", "out0"):
                weights_high(LI[name])
            merged_high(0, hTh1)
            weights_high(LI["out1"])

            def high(m, i, b, k, slot0, count0):
                e, half, par = 2 * i + b + k, i + (b + k) // 2, (b + k) % 2
                act.wait_ge((s_gu if m < 2 else s_dn)[par], 16 * (half + 1 + count0 // 2))
                if not (m < 2 and count0 == 0 and k == 0):
                    act.wait_ge((s_gate, s_gup, s_dnp)[m], e + (count0 if m < 2 else (DN2 if count0 else 1)))
                src = dring[:, par, :] if m == 2 else ring[:, (slot0 + par) % 2, m * W3:(m + 1) * W3]
                nc.scalar.activation(wsp[:, m, 0, :], src, ACT.Copy).then_inc(s_hi[m], 1)

            n0, n1 = len(LOADS), len(ALL)
            act.wait_ge(s_x1, 4)
            row_squares(1)
            scaled_rows(1)
            high(0, 0, 0, 0, n0, 0)
            hT_half(1, modT[:, 40:48], modT[:, 16:24])
            tokens_high(1, hTs[:, 0])
            high(1, 0, 0, 0, n0, 0)
            act.wait_ge(s_re, 1)
            nc.scalar.activation(rt[:, 80:88], rt[:, 72:80], ACT.Exp).then_inc(s_rx, 1)
            act.wait_ge(s_re, 2)
            nc.scalar.activation(rt[:, 190:192], rt[:, 188:190], ACT.Exp).then_inc(s_rx, 1)

            def half_tanh(i, b):
                act.wait_ge(s_gate, 2 * i + b + 1)
                act.wait_ge(s_a2, 2 * i + b + 1)
                nc.scalar.activation(tmp[:, b, :], ps[:, 4 + 2 * b, :], ACT.Tanh, scale=0.5).then_inc(s_th, 1)

            def stream(first, second, slot0, count0, total):
                def step(i, b, last=False):
                    first(i, b)
                    if not last:
                        high(0, i, b, 1, slot0, count0)
                        high(1, i, b, 1, slot0, count0)
                    second(i, b)
                    high(2, i, b, 0, slot0, count0)

                pairs = (total - 1) // 2
                with act.Fori(0, pairs) as i:
                    step(i, 0)
                    step(i, 1)
                for e in range(2 * pairs, total):
                    step(e // 2, e % 2, e == total - 1)

            stream(half_tanh, lambda i, b: None, n0, 0, NE)

            def final_norm(k):
                for t in range(NT):
                    act.wait_ge(s_x1, 8 * (k + 1) - 2 * (NT - 1 - t))
                    link(nc.scalar.activation(hn[:, t, :], xs[:, t, :], ACT.Square, accum_out=small[:, 16 + t:17 + t]))
                act.nop().then_inc(s_fss, 1)

            final_norm(0)
            row_squares(2)
            scaled_rows(2)
            weights_high(L2)
            hT_half(2, v("g3"), None)
            tokens_high(2, hTh2)

            def keys_out(name, c0, n):
                grouped(act, name)
                for j in range(n):
                    ins = nc.scalar.activation(fmT[:, c0 + j, :], bank(name)[:, j * T:(j + 1) * T], ACT.Identity,
                                               bias=v("b2f", c0 + j, c0 + j + 1))
                ins.then_inc(s_ga, 1)

            for n in range(L2, LH):
                weights_high(n + 1, (0, 1, 2))
                for name, c0, count in (("fox1", 2, 2), ("dil2", 7, 2), ("dil3", 9, 1), ("kk", 15, 2)):
                    if name in SPLIT[n][1]:
                        keys_out(name, c0, count)
                weights_high(n + 1, (3,))
                if SPLIT[n][0] == "kk":
                    act.wait_ge(s_fl, 1)
                    link(nc.scalar.activation(fox[0:FOXH, 1, :], fox[0:FOXH, 1, :], ACT.Exp, scale=-1.0))
                    nc.scalar.activation(fox[0:FOXH, 2, :], fox[0:FOXH, 1, :], ACT.Ln, bias=1.0).then_inc(s_fe, 1)
            nc.scalar.activation(gc, gc, ACT.Tanh, scale=0.5).then_inc(s_gct, 1)
            act.wait_ge(s_hu, 1)
            nc.scalar.activation(gel[:, 3], gel[:, 2], ACT.Tanh, scale=GELU).then_inc(s_hth, 1)

            def gate_tanh2(i):
                act.wait_ge(s_gv, VGROUPS - 12 + i + 1)
                sl = g2[:, i % 2, 512 * (i // 2):512 * (i // 2 + 1)]
                nc.scalar.activation(sl, sl, ACT.Tanh, scale=0.5).then_inc(s_ggu, 1)

            weights_high(LH + 1)
            gate_tanh2(0)
            gate_tanh2(1)
            weights_high(LH + 2, (0, 1))
            act.wait_ge(s_ce, 1)
            nc.scalar.activation(pcm, pcm, ACT.Exp).then_inc(s_cx, 1)
            weights_high(LH + 2, (2, 3))
            act.wait_ge(s_cpt, 1)
            for i in range(3):
                nc.scalar.copy(pcT[0:NC, 2 * i:2 * i + 2, :], ps[0:NC, 5 + i, :].rearrange("p (a b) -> p a b", a=2)
                               ).then_inc(s_cpc, 1)
            gate_tanh2(2)
            gate_tanh2(3)

            def gates_between(u):
                if u < 12:
                    weights_high(LH + 3 + u // 4, (u % 4,))
                if u in (4, 8, 12, 16):
                    gate_tanh2(HM + (u - 4) // 2)
                    gate_tanh2(HM + (u - 4) // 2 + 1)

            def dest2(kind, h):
                if kind == "fox":
                    c, r = h // 2, h % 2
                elif kind == "dil":
                    c, r = 2 + h // 2, h % 2
                else:
                    c, r = 5 + h % 3, h // 3
                return yT2[r * HD:(r + 1) * HD, c, :], r * HD, (r + 1) * HD

            attention(UNITS2, AH, AH, AH, 1.0, dest2, lambda kind: kind != "sel",
                      gates_between)
            weights_high(LI["wo0"])
            merged_high(1, hTh2)
            weights_high(LI["wo1"])
            act.wait_ge(s_x1, 12)
            row_squares(3)
            scaled_rows(3)
            high(0, 0, 0, 0, n1, NE)
            hT_half(3, v("g4"), None)
            tokens_high(3, hTs[:, 0])
            high(1, 0, 0, 0, n1, NE)

            def ff_act(i, b):
                act.wait_ge(s_fsq, 2 * i + b + 1)
                nc.scalar.activation(ft[:, 2, :], ft[:, b, :], ACT.Square).then_inc(s_fz, 1)

            def ff_tanh(i, b):
                act.wait_ge(s_fth, 2 * i + b + 1)
                nc.scalar.activation(tmp[:, 0, :], ft[:, 3, :], ACT.Tanh, scale=GELU).then_inc(s_ffn, 1)

            stream(ff_act, ff_tanh, n1, NE, FP)
            final_norm(1)

        @block.gpsimd
        def _(pool):
            link = Chain(pool, c_pool)
            pool.wait_ge(s_zero, 1)

            def power(dst, src, n, ready, count, done):
                pool.wait_ge(ready, count)
                nc.gpsimd.tensor_tensor(dst, src, small[:, 496:496 + n], ALU.pow).then_inc(done, 1)

            power(small[:, 18:20], small[:, 18:20], 2, s_ms, 1, s_rstd)

            def weights_low(first, last):
                for n in range(first, last):
                    name = SPLIT[n][0]
                    for q in range(4):
                        pool.wait_ge(s_qh, 4 * n + q + 1)
                        nc.gpsimd.tensor_tensor(quarter(name, q, "low"), quarter(name, q, "raw"),
                                                quarter(name, q, "high"), ALU.subtract).then_inc(s_ql, 1)

            weights_low(0, LI["o1"])
            power(small[:, 24:28], small[:, 24:28], 4, s_cms, 1, s_crs)
            weights_low(LI["o1"], LI["ba0"])

            def output_parts(h):
                pool.wait_ge(s_y, h + 1)
                link(nc.gpsimd.tensor_copy(yah[:, h, :], ya[:, h, :]))
                nc.gpsimd.tensor_tensor(yal[:, h, :], ya[:, h, :], yah[:, h, :], ALU.subtract).then_inc(s_ya, 1)

            for h in range(AH - 2):
                output_parts(h)
            weights_low(LI["ba0"], LI["ba1"])
            for h in range(AH - 2, AH):
                output_parts(h)
            weights_low(LI["ba1"], L2)

            def low(m, i, b, k, slot0, count0):
                par = (b + k) % 2
                pool.wait_ge(s_hi[m], 2 * i + b + k + 1 + count0)
                src = dring[:, par, :] if m == 2 else ring[:, (slot0 + par) % 2, m * W3:(m + 1) * W3]
                nc.gpsimd.tensor_tensor(wsp[:, m, 1, :], src, wsp[:, m, 0, :], ALU.subtract).then_inc(s_lo[m], 1)

            def stream(slot0, count0, total):
                low(0, 0, 0, 0, slot0, count0)
                low(1, 0, 0, 0, slot0, count0)

                def step(i, b, last=False):
                    if not last:
                        low(0, i, b, 1, slot0, count0)
                    low(2, i, b, 0, slot0, count0)

                pairs = (total - 1) // 2
                with pool.Fori(0, pairs) as i:
                    step(i, 0)
                    step(i, 1)
                for e in range(2 * pairs, total):
                    step(e // 2, e % 2, e == total - 1)

            power(small[:, 18:20], small[:, 18:20], 2, s_ms, 2, s_rstd)
            stream(len(LOADS), 0, NE)
            power(small[:, 18:20], small[:, 18:20], 2, s_fms, 1, s_frs)
            power(small[:, 18:20], small[:, 18:20], 2, s_ms, 3, s_rstd)
            weights_low(L2, len(SPLIT))
            power(small[:, 18:20], small[:, 18:20], 2, s_ms, 4, s_rstd)
            stream(len(ALL), NE, FP)
            power(small[:, 18:20], small[:, 18:20], 2, s_fms, 2, s_frs)

        @block.vector
        def _(dve):
            link = Chain(dve, c_dve)
            V = nc.vector
            V.memset(small[:, 496:500], -0.5).then_inc(c_dve, 1)
            link.n += 1
            link(V.memset(zero[:, :], 0.0))
            dve.nop().then_inc(s_zero, 1)
            dve.wait_ge(s_condt, 1)
            link(V.scalar_tensor_tensor(small[:, 8:16], small[:, 0:8], 1.0, v("c"), ALU.add, ALU.mult))
            link(V.tensor_scalar(small[:, 8:16], small[:, 8:16], 0.5, None, ALU.mult))

            def mod_part(j):
                dve.wait_ge(s_mt[j % 2], 16 * (j // 2 + 1))
                if j >= 2:
                    dve.wait_ge(s_msum, j - 1)
                d = mpart[:, j % 2, :]
                w = mtile[j % 2]
                link(V.tensor_scalar(d, w[:, 0, :], small[:, 8:9], None, ALU.mult))
                for c in range(1, KD):
                    ins = V.scalar_tensor_tensor(d, w[:, c, :], small[:, 8 + c:9 + c], d, ALU.mult, ALU.add)
                    if c < KD - 1:
                        link(ins)
                ins.then_inc(s_mpart, 1)

            def mod_gate(j):
                dve.wait_ge(s_msum, j + 1)
                if j == 4:
                    dve.wait_ge(s_brow, 32)
                k, half = (0, j - 4) if j < 6 else (1, j - 10)
                g = gateb[:, k, half * 512:(half + 1) * 512]
                V.tensor_tensor(g, ps[:, 7, :], g, ALU.add).then_inc(s_mev, 1)

            def mod_columns(k):
                link(V.tensor_tensor(modT[:, 16 * k:16 * k + 16], ps[:, 7, 0:16], v(f"mod{k + 1}"), ALU.add))
                V.scalar_tensor_tensor(modT[:, 32 + 8 * k:40 + 8 * k], modT[:, 16 * k + 8:16 * k + 16], 1.0,
                                       v(f"g{k + 1}"), ALU.add, ALU.mult).then_inc(s_mev, 1)

            def row_scale(k, sem_in, n_in, sem_ms, sem_rs, n):
                dve.wait_ge(sem_in, n_in)
                V.tensor_scalar(small[:, 18:20], small[:, 16:18], 1.0 / D, EPS, ALU.mult, ALU.add).then_inc(sem_ms, 1)
                dve.wait_ge(sem_rs, n)

            def norm_rows(k):
                row_scale(k, s_ss, k + 1, s_ms, s_rstd, k + 1)
                V.tensor_scalar(hn[:, 0, :], xs[:, 0, :], small[:, 18:19], None, ALU.mult).then_inc(s_hn[0], 1)

            for j in range(3):
                mod_part(j)
            norm_rows(0)
            mod_part(3)
            dve.wait_ge(s_msum, 4)
            mod_columns(0)

            def hT_half(k, scale, shift):
                for c in range(4, KD):
                    if c % 2 == 0:
                        dve.wait_ge(s_tr, 4 * k + c // 2 + 1)
                    src = ps[:, c // 2, (c % 2) * T:(c % 2 + 1) * T]
                    if shift is None:
                        V.tensor_scalar(hT[:, c, :], src, scale[:, c:c + 1], None, ALU.mult).then_inc(s_hTv, 1)
                    else:
                        V.tensor_scalar(hT[:, c, :], src, scale[:, c:c + 1], shift[:, c:c + 1], ALU.mult, ALU.add
                                        ).then_inc(s_hTv, 1)

            dve.wait_ge(s_mev, 1)
            def split_tokens(n, hi, lo):
                dve.wait_ge(s_hTv, 4 * (n + 1))
                link(V.tensor_copy(hi[:, 4:KD, :], hT[:, 4:KD, :]))
                dve.wait_ge(s_hsh, n + 1)
                V.tensor_tensor(lo[:, 0:4, :], hT[:, 0:4, :], hi[:, 0:4, :], ALU.subtract).then_inc(s_hs, 1)
                V.tensor_tensor(lo[:, 4:KD, :], hT[:, 4:KD, :], hi[:, 4:KD, :], ALU.subtract).then_inc(s_hs, 1)

            hT_half(0, modT[:, 32:40], modT[:, 0:8])
            split_tokens(0, hTh1, hTl)

            def rope(dst, src, t1, t2):
                link(V.tensor_tensor(t1, src, const("cos"), ALU.mult))
                for q in range(4):
                    o = q ^ 1
                    ins = V.tensor_tensor(t2[q * 32:(q + 1) * 32, :], src[o * 32:(o + 1) * 32, :],
                                          const("sin")[q * 32:(q + 1) * 32, :], ALU.mult)
                    link(ins)
                return V.tensor_tensor(dst, t1, t2, ALU.add)

            mod_part(4)
            mod_part(5)
            sc1, sc2 = pT[:, 0, 0:T], pT[:, 1, 0:T]
            grouped(dve, "kr")
            krope = pT[:, 2, 0:T]
            link(rope(krope, bank("kr")[:, 0:T], sc1, sc2))
            dve.nop().then_inc(s_gv, 1)
            mod_gate(4)
            mod_part(6)
            mod_gate(5)
            def conv(i):
                name = f"qk{i}"
                grouped(dve, name)
                src = bank(name).rearrange("p (a b) -> p a b", a=2)
                acc = hn[:, i % 2, 0:512].rearrange("p (a b) -> p a b", a=2)
                for d in range(CONV):
                    for j in range(2):
                        blk = 2 * i + j
                        wv = v("convw", 4 * blk, 4 * blk + 4)
                        if d == 0:
                            ins = V.tensor_scalar(acc[:, j, :], src[:, j, :], wv[:, 3:4], v("convb", blk, blk + 1),
                                                  ALU.mult, ALU.add)
                        else:
                            ins = V.scalar_tensor_tensor(acc[:, j, d:T], src[:, j, 0:T - d], wv[:, 3 - d:4 - d],
                                                         acc[:, j, d:T], ALU.mult, ALU.add)
                        if j == 0:
                            link.later(ins)
                        else:
                            link(ins)
                dve.nop().then_inc(s_conv, 1)
                dve.wait_ge(s_convt, i + 1)
                V.scalar_tensor_tensor(qkT[:, 2 * i:2 * i + 2, :], att[:, 1, 0:2, 0:T], 1.0, acc, ALU.add, ALU.mult
                                       ).then_inc(s_gv, 1)

            dve.wait_ge(s_hn[1], 1)
            dve.wait_ge(s_tr, 4)
            for i in range(4):
                conv(i)
            mod_part(7)
            mod_part(8)
            mod_part(9)
            dve.wait_ge(s_css, 1)
            link(V.tensor_scalar(small[:, 24:26], small[:, 20:22], 1.0 / QL, EPS, ALU.mult, ALU.add))
            V.tensor_scalar(small[:, 26:28], small[:, 22:24], 1.0 / KVL, EPS, ALU.mult, ALU.add).then_inc(s_cms, 1)
            dve.wait_ge(s_crs, 1)
            for t in range(NT):
                link(V.tensor_scalar(raw[:, t, 0:QL], raw[:, t, 0:QL], small[:, 24 + t:25 + t], None, ALU.mult))
                V.tensor_scalar(raw[:, t, 392:RAW], raw[:, t, 392:RAW], small[:, 26 + t:27 + t], None, ALU.mult
                                ).then_inc(s_cn, 1)

            mod_part(10)
            dve.wait_ge(s_msum, 10)
            mod_columns(1)
            mod_part(11)
            mod_gate(10)
            mod_gate(11)
            V.memset(vaug[:, :, :, MV:MV + 1], 1.0).then_inc(c_dve, 1)
            link.n += 1
            dve.wait_ge(s_ctr, 1)
            for c in range(5):
                g = v("qg", c, c + 1) if c < 3 else v("kvg", c - 3, c - 2)
                V.tensor_scalar(cT[:, c, :], ps[:, 4 + c // 2, (c % 2) * T:(c % 2 + 1) * T], g, None, ALU.mult
                                ).then_inc(c_dve, 1)
                link.n += 1
            link(V.tensor_copy(krT, krope))
            dve.nop().then_inc(s_cT, 1)
            L = lst[0:MH, :, :]
            link(V.tensor_scalar(L[:, 1, :], ps[0:MH, 7, 0:T], v("fb")[0:MH, :], None, ALU.add))
            link(V.tensor_scalar(L[:, 2, :], ps[0:MH, 6, T:2 * T], v("ib")[0:MH, :], None, ALU.add))
            V.scalar_tensor_tensor(L[:, 5, :], L[:, 1, :], -1.0, L[:, 1, :], ALU.mult, ALU.max).then_inc(s_lf, 1)
            dve.wait_ge(s_le, 1)
            link(V.scalar_tensor_tensor(L[:, 1, :], L[:, 1, :], 0.0, L[:, 7, :], ALU.min, ALU.subtract))
            link(V.tensor_tensor_scan(L[:, 6, :], const("ones")[0:MH, 0:1].to_broadcast([MH, T]), L[:, 1, :], 0.0,
                                      ALU.mult, ALU.add))
            link(V.tensor_tensor(L[:, 2, :], L[:, 2, :], L[:, 6, :], ALU.subtract))
            link(V.tensor_tensor_scan(L[:, 4, :], const("ones")[0:MH, 0:1].to_broadcast([MH, T]), L[:, 2, :], 0.0,
                                      ALU.mult, ALU.max))
            link(V.tensor_tensor(L[:, 3, :], L[:, 4, :], L[:, 6, :], ALU.add))
            link(V.tensor_scalar(L[:, 4, :], L[:, 4, :], -1.0, None, ALU.mult))
            dve.nop().then_inc(s_scan, 1)
            for i in range(2):
                grouped(dve, f"qr{i}")
                for j in range(2):
                    link(rope(qrT[:, 2 * i + j, :], bank(f"qr{i}")[:, j * T:(j + 1) * T], sc1, sc2))
                dve.nop().then_inc(s_gv, 1)
            for i in range(4):
                grouped(dve, f"va{i}")
                V.tensor_copy(va[:, i % 2, 512 * (i // 2):512 * (i // 2 + 1)], bank(f"va{i}")).then_inc(s_gv, 1)
            dve.wait_ge(s_gt, 1)
            V.tensor_copy(small[:, 64:80], ps[:, 4, 0:16]).then_inc(s_gte, 1)
            dve.wait_ge(s_gte, 1)

            def m_weights(h):
                dve.wait_ge(s_mS, h + 1)
                w = att[:, h % 2, 0, :]
                V.tensor_scalar(w[:, 0:T], ps[:, h % 2, 0:T], small[:, 64 + h:65 + h], 0.0, ALU.add, ALU.min
                                ).then_inc(s_mw, 1)
                V.tensor_scalar(w[:, T:SPAN], ps[:, h % 2, P:T], small[:, 68 + h:69 + h], 0.0, ALU.add, ALU.min
                                ).then_inc(s_mw, 1)
                dve.wait_ge(s_mexp, h + 1)
                if h >= 2:
                    dve.wait_ge(s_mnum, h - 1)
                d = wmem[:, (h % 2) * SPAN:(h % 2 + 1) * SPAN]
                link(V.scalar_tensor_tensor(d, ps[:, 2 + h % 2, 0:SPAN], 0.25 * MQK ** -0.5, w, ALU.mult, ALU.mult))
                link(V.tensor_tensor(d[:, 0:P], d[:, 0:P], const("tri"), ALU.mult))
                V.tensor_tensor(d[:, T:SPAN], d[:, T:SPAN], const("tri"), ALU.mult).then_inc(s_mst, 1)

            def m_den(h):
                dve.wait_ge(s_mnum, h + 1)
                for t in range(NT):
                    r = small[:, 80 + t:81 + t]
                    link(V.tensor_scalar(r, ps[:, 5 + t, MV:MV + 1], -1.0, small[:, 72 + 4 * t + h:73 + 4 * t + h],
                                         ALU.mult, ALU.max))
                    link(V.tensor_tensor(r, ps[:, 5 + t, MV:MV + 1], r, ALU.max))
                    V.reciprocal(small[:, 82 + 2 * (h % 2) + t:83 + 2 * (h % 2) + t], r).then_inc(s_mr, 1)
                dve.wait_ge(s_mh, 2 * (h + 1))
                for t in range(NT):
                    o = og[:, t, h * MV:(h + 1) * MV]
                    V.scalar_tensor_tensor(o, o, 1.0, hn[:, t, h * MV:(h + 1) * MV], ALU.add, ALU.mult
                                           ).then_inc(s_my, 1)

            for h in range(MH):
                m_weights(h)
                if h >= 1:
                    m_den(h - 1)
            m_den(MH - 1)

            def attention(todo, set0, unit0, scale, bias, fill=None):
                n, at = set0, []
                for _, heads in todo:
                    at.append(n)
                    n += len(heads)
                for u in range(len(todo) + 1):
                    if u >= 1:
                        kind, heads = todo[u - 1]
                        ui = unit0 + u - 1
                        a = att[:, ui % 2, 0:len(heads), :]
                        sm = small[:, 32 + 8 * (ui % 2):40 + 8 * (ui % 2)]
                        dve.wait_ge(s_exp, ui + 1)
                        link(V.tensor_scalar(sm[:, 4:6], sm[:, 2:4], TINY, None, ALU.max))
                        link(V.reciprocal(sm[:, 4:6], sm[:, 4:6]))
                        if kind in ("sel", "win"):
                            j = 3 * heads[0] + (1 if kind == "sel" else 2)
                            link(V.tensor_tensor(sm[:, 4:6], sm[:, 4:6], gc[:, :, j:j + 1].rearrange("p t o -> p (t o)"),
                                                 ALU.mult))
                        V.tensor_scalar(a[:, :, 0:P], a[:, :, 0:P], sm[:, 4:5], None, ALU.mult)
                        V.tensor_scalar(a[:, :, P:SPAN], a[:, :, P:SPAN], sm[:, 5:6], None, ALU.mult).then_inc(s_p, 1)
                    if u < len(todo):
                        kind, heads = todo[u]
                        ui = unit0 + u
                        a = att[:, ui % 2, 0:len(heads), :]
                        sm = small[:, 32 + 8 * (ui % 2):40 + 8 * (ui % 2)]
                        if u >= 2:
                            dve.wait_ge(s_pt, at[u - 1])
                        for g, h in enumerate(heads):
                            s = at[u] + g
                            dve.wait_ge(s_sc, s + 1)
                            tile, slope = bias(kind, g, h)
                            V.scalar_tensor_tensor(a[:, g, :], tile, slope, ps[:, s % 2, 0:SPAN], ALU.mult, ALU.add
                                                   ).then_inc(s_sfree, 1)
                        dve.wait_ge(s_sfree, at[u] + len(heads))
                        V.tensor_reduce(sm[:, 0:1], a[:, :, 0:P], AX.XY, ALU.max, negate=True).then_inc(c_dve, 1)
                        link.n += 1
                        if scale is None:
                            V.tensor_reduce(sm[:, 1:2], a[:, :, P:SPAN], AX.XY, ALU.max, negate=True
                                            ).then_inc(s_nm, 1)
                        else:
                            link(V.tensor_reduce(sm[:, 1:2], a[:, :, P:SPAN], AX.XY, ALU.max, negate=True))
                            V.tensor_scalar(sm[:, 0:2], sm[:, 0:2], scale, None, ALU.mult).then_inc(s_nm, 1)
                    if fill:
                        fill(u)

            attention(UNITS1, 0, 0, float((NOPE + ROPE) ** -0.5), lambda kind, g, h: (const("chunk"), 1.0))

            def pairs_low(done, base, hi, lo, sem_low):
                for b in range(4):
                    dve.wait_ge(done, base + b + 1)
                    V.tensor_tensor(lo[:, 2 * b:2 * b + 2, :], ps[:, b, :].rearrange("p (a b) -> p a b", a=2),
                                    hi[:, 2 * b:2 * b + 2, :], ALU.subtract).then_inc(sem_low, 1)

            pairs_low(s_ymT, 0, hTh1, yml, s_yml)
            for half in range(2):
                for t in range(NT):
                    dve.wait_ge(s_br, 2 * half + t + 1)
                    ga = gates[:, t, D + 512 * half:D + 512 * (half + 1)]
                    link(V.scalar_tensor_tensor(ga, ga, 1.0, ps[:, 4 + 2 * half + t, :], ALU.add, ALU.mult))
            for half in range(2):
                for t in range(NT):
                    dve.wait_ge(s_br, 4 + 2 * half + t + 1)
                    cs = slice(512 * half, 512 * (half + 1))
                    link(V.scalar_tensor_tensor(hn[:, t, cs], gates[:, t, cs], 1.0, ps[:, 2 * half + t, :], ALU.add,
                                                ALU.mult))
                    V.scalar_tensor_tensor(merged[:, t, cs], hn[:, t, cs], 0.5,
                                           gates[:, t, D + 512 * half:D + 512 * (half + 1)], ALU.mult, ALU.add
                                           ).then_inc(s_mrg, 1)
            pairs_low(s_mT, 0, hTh1, hTl, s_ml)
            link(V.tensor_scalar(gateb[:, 0, :], gateb[:, 0, :], 0.5, None, ALU.mult))
            for half in range(2):
                for t in range(NT):
                    dve.wait_ge(s_pr, 2 * half + t + 1)
                    cs = slice(512 * half, 512 * (half + 1))
                    link(V.tensor_tensor(hn[:, t, cs], ps[:, 4 + 2 * half + t, :], gateb[:, 0, cs], ALU.mult))
                    V.tensor_tensor(xs[:, t, cs], xs[:, t, cs], hn[:, t, cs], ALU.add).then_inc(s_x1, 1)
            norm_rows(1)
            hT_half(1, modT[:, 40:48], modT[:, 16:24])

            split_tokens(1, hTs[:, 0], hTs[:, 1])

            lg = rt[:, 0:72].rearrange("p (t n) -> p t n", t=NT)
            lgrp = lg[:, :, 0:NG]
            lexp = lg[:, :, NG:NG + NE].rearrange("p t (g e) -> p t g e", g=NG)

            def t2(a, n):
                return rt[:, a:a + NT * n].rearrange("p (t n) -> p t n", t=NT)

            def bc(a, shape):
                return a.to_broadcast(shape)

            dve.wait_ge(s_brout, 16)
            dve.wait_ge(s_lg, 1)
            for t in range(NT):
                link(V.tensor_tensor(lg[:, t, :], ps[:, 0, t * 36:(t + 1) * 36], small[:, 448:484], ALU.add))
            gmax, gdif, gexp = t2(88, 1), t2(72, NG), t2(80, NG)
            link(V.tensor_reduce(gmax, lgrp, AX.X, ALU.max))
            ins = V.tensor_tensor(gdif, lgrp, bc(gmax, [P, NT, NG]), ALU.subtract)
            ins.then_inc(s_re, 1)
            gsum, pg, oh, key, kmax = t2(90, 1), t2(92, 1), t2(96, NG), t2(104, EG), t2(120, 1)
            dve.wait_ge(s_rx, 1)
            link(V.tensor_reduce(gsum, gexp, AX.X, ALU.add))
            link(V.reciprocal(pg, gsum))

            def first_max(dst, src, top, rank, n):
                k = t2(104, n)
                link(V.tensor_tensor(dst, src, bc(top, [P, NT, n]), ALU.is_equal))
                for t in range(NT):
                    link(V.tensor_tensor(k[:, t, :], dst[:, t, :], rank, ALU.mult))
                link(V.tensor_reduce(kmax, k, AX.X, ALU.max))
                link(V.tensor_tensor(dst, k, bc(kmax, [P, NT, n]), ALU.is_equal))

            first_max(oh, lgrp, gmax, const("rank4"), NG)
            prod = rt[:, 512:512 + 64].rearrange("p (t g e) -> p t g e", t=NT, g=NG)
            for t in range(NT):
                link(V.tensor_tensor(prod[:, t], lexp[:, t], bc(oh[:, t, :].rearrange("p (g o) -> p g o", o=1), [P, NG, EG]),
                                     ALU.mult))
            l8, top1, oh1, l8b, top2, oh2 = t2(122, EG), t2(138, 1), t2(140, EG), t2(156, EG), t2(172, 1), t2(194, EG)
            link(V.tensor_reduce(l8, prod.rearrange("p t g e -> p t e g"), AX.X, ALU.add))
            link(V.tensor_reduce(top1, l8, AX.X, ALU.max))
            first_max(oh1, l8, top1, const("rank8"), EG)
            link(V.scalar_tensor_tensor(l8b, oh1, NEG, l8, ALU.mult, ALU.add))
            link(V.tensor_reduce(top2, l8b, AX.X, ALU.max))
            first_max(oh2, l8b, top2, const("rank8"), EG)
            e2, w1, w2 = rt[:, 190:192], rt[:, 174:176], rt[:, 176:178]
            V.tensor_tensor(rt[:, 188:190], rt[:, 172:174], rt[:, 138:140], ALU.subtract).then_inc(s_re, 1)
            dve.wait_ge(s_rx, 2)
            link(V.tensor_scalar(w1, e2, 1.0, None, ALU.add))
            link(V.reciprocal(w1, w1))
            link(V.tensor_tensor(w1, w1, rt[:, 92:94], ALU.mult))
            link(V.tensor_scalar(w1, w1, 0.5, None, ALU.mult))
            link(V.tensor_tensor(w2, w1, e2, ALU.mult))
            w8 = t2(210, EG)
            w32 = rt[:, 256:256 + 64].rearrange("p (t g e) -> p t g e", t=NT, g=NG)
            for t in range(NT):
                link(V.tensor_scalar(w8[:, t, :], oh1[:, t, :], w1[:, t:t + 1], None, ALU.mult))
                link(V.scalar_tensor_tensor(w8[:, t, :], oh2[:, t, :], w2[:, t:t + 1], w8[:, t, :], ALU.mult, ALU.add))
                for g in range(NG):
                    link(V.tensor_scalar(w32[:, t, g, :], w8[:, t, :], oh[:, t, g:g + 1], None, ALU.mult))
            dve.nop().then_inc(s_w32, 1)
            dve.wait_ge(s_wt, 1)
            V.tensor_copy(rt[0:NE, 384:384 + T], ps[0:NE, 1, 0:T]).then_inc(s_wtc, 1)

            def split_act(src, b, e, down0):
                dve.wait_ge(s_dnp, e + down0)
                flat = [aTs[:, b, s].rearrange("p f n -> p (f n)") for s in range(2)]
                link(V.tensor_copy(flat[0], src))
                V.tensor_tensor(flat[1], src, flat[0], ALU.subtract).then_inc(s_aT, 1)

            def up_low(i, b, slot0, count0):
                par = 1 - b
                dve.wait_ge(s_hi[1], 2 * i + b + 2 + count0)
                V.tensor_tensor(wsp[:, 1, 1, :], ring[:, (slot0 + par) % 2, W3:2 * W3], wsp[:, 1, 0, :], ALU.subtract
                                ).then_inc(s_lo[1], 1)

            def expert(i, b, low):
                e = 2 * i + b
                dve.wait_ge(s_th, e + 1)
                t0, g, u = tmp[:, b, :], ps[:, 4 + 2 * b, :], ps[:, 5 + 2 * b, :]
                link(V.scalar_tensor_tensor(t0, t0, 1.0, g, ALU.add, ALU.mult))
                dve.wait_ge(s_gup, e + 1)
                V.tensor_tensor(t0, t0, u, ALU.mult).then_inc(s_a2, 1)
                dve.wait_ge(s_a2, e + 2)
                dve.wait_ge(s_wb[b], 16 * (i + 1))
                for f in range(2):
                    link(V.tensor_tensor(act32[:, f * T:(f + 1) * T], t0[:, f * T:(f + 1) * T], wbe[:, b, :], ALU.mult))
                split_act(act32, b, e, 1)
                low()

            def stream(work, per, slot0, count0, total):
                loops = (total - 1) // 2
                with dve.Fori(0, loops) as i:
                    n = link.n
                    link.start(i, per)
                    for b in range(2):
                        work(i, b, lambda: up_low(i, b, slot0, count0))
                    assert link.n - n == per, link.n - n
                link.end(loops)
                for e in range(2 * loops, total):
                    work(e // 2, e % 2, lambda: up_low(e // 2, e % 2, slot0, count0) if e < total - 1 else None)

            dve.nop().then_inc(s_a2, 1)
            stream(expert, 8, len(LOADS), 0, NE)
            dve.wait_ge(s_dnp, NE + 1)
            for t in range(NT):
                for half in range(2):
                    cs = slice(512 * half, 512 * (half + 1))
                    link(V.tensor_tensor(hn[:, t, cs], ps[:, 2 * t + half, :], gateb[:, 1, cs], ALU.mult))
                    V.tensor_tensor(xs[:, t, cs], xs[:, t, cs], hn[:, t, cs], ALU.add).then_inc(s_x1, 1)

            def final_norm(k, dst):
                row_scale(k, s_fss, k + 1, s_fms, s_frs, k + 1)
                dve.wait_ge((s_final1, s_final2)[k], 16)
                for t in range(NT):
                    V.scalar_tensor_tensor(dst[:, t, :], xs[:, t, :], small[:, 18 + t:19 + t], finalb[:, :], ALU.mult,
                                           ALU.mult).then_inc(s_xf, 1)

            final_norm(0, xs)
            dve.wait_ge(s_xf, 2)
            norm_rows(2)
            hT_half(2, v("g3"), None)
            split_tokens(2, hTh2, hTl)

            def columns_out(name, c0, n, scale):
                grouped(dve, name)
                for j in range(n):
                    src = bank(name)[:, j * T:(j + 1) * T]
                    if scale:
                        ins = V.tensor_scalar(fmT[:, c0 + j, :], src, v("b2f", c0 + j, c0 + j + 1), 0.125, ALU.add,
                                              ALU.mult)
                    else:
                        ins = V.tensor_scalar(fmT[:, c0 + j, :], src, v("b2f", c0 + j, c0 + j + 1), None, ALU.add)
                ins.then_inc(s_gv, 1)

            columns_out("fox0", 0, 2, True)
            columns_out("dil0", 4, 2, True)
            columns_out("dil1", 6, 1, True)
            columns_out("nsa0", 10, 2, True)
            columns_out("nsa1", 12, 1, True)
            columns_out("kcv", 13, 2, False)
            emptied(dve, GI["kcv"])
            for i in range(2):
                for g in range(KVG):
                    for jj in range(2):
                        src = fmT[g * HD:(g + 1) * HD, 13 + i, :]
                        d = kvc[jj * HD:(jj + 1) * HD, i, :, g * NC:(g + 1) * NC]
                        for q in range(2):
                            s3 = src[:, 16 * q:16 * q + 240].rearrange("p (c j two) -> p two j c", j=8, two=2)[:, jj]
                            link(V.tensor_copy(d[:, 8 * q:8 * q + 8, :], s3))
                link(V.tensor_tensor(kvc[:, i], kvc[:, i],
                                     v("pe").rearrange("p (j o) -> p j o", o=1).to_broadcast([P, CB // 2, KVG * NC]),
                                     ALU.add))
            dve.nop().then_inc(s_F, 1)
            dve.wait_ge(s_bias2, 16)
            grouped(dve, "gf")
            f = fox[0:FOXH]
            for t in range(NT):
                V.tensor_tensor(gc[:, t, :], bank("gf")[:, t * 3 * NSAH:(t + 1) * 3 * NSAH], bias2[:, 896:914], ALU.add)
            V.tensor_scalar(f[:, 0, :], bank("gf")[0:FOXH, T:2 * T], v("fab")[0:FOXH, :], None, ALU.add).then_inc(s_gv, 1)
            emptied(dve, GI["gf"])
            V.scalar_tensor_tensor(f[:, 1, :], f[:, 0, :], -1.0, f[:, 0, :], ALU.mult, ALU.max).then_inc(s_fl, 1)
            for t in range(NT):
                grouped(dve, f"vv{t}")
                V.tensor_tensor(tv[:, t, :], bank(f"vv{t}"), bias2[:, 0:512], ALU.add).then_inc(s_gv, 1)
            for t in range(NT):
                grouped(dve, f"vb{t}")
                V.tensor_tensor(tvb[:, t, :], bank(f"vb{t}")[:, 0:384], bias2[:, 512:896], ALU.add).then_inc(s_gv, 1)
            dve.wait_ge(s_fe, 1)
            link(V.scalar_tensor_tensor(f[:, 0, :], f[:, 0, :], 0.0, f[:, 2, :], ALU.min, ALU.subtract))
            link(V.tensor_tensor_scan(f[:, 3, :], const("ones")[0:MH, 0:1].to_broadcast([MH, T]), f[:, 0, :], 0.0,
                                      ALU.mult, ALU.add))
            V.tensor_scalar(f[:, 3, :], f[:, 3, :], -1.0, None, ALU.mult).then_inc(s_fsc, 1)
            dve.wait_ge(s_hid, 2)
            hu, hw, hz, ht = (gel[:, k] for k in range(4))
            link(V.tensor_copy(hu, ps[:, 4:6, 0:60]))
            link(V.tensor_tensor(hw, hu, hu, ALU.mult))
            link(V.tensor_scalar(hw, hw, 0.044715, 1.0, ALU.mult, ALU.add))
            V.tensor_tensor(hz, hw, hu, ALU.mult).then_inc(s_hu, 1)
            dve.wait_ge(s_hth, 1)
            link(V.scalar_tensor_tensor(hw, ht, 1.0, hu, ALU.add, ALU.mult))
            V.tensor_scalar(hidT.rearrange("p a b c -> p a (b c)"), hw, 0.5, None, ALU.mult).then_inc(s_hg, 1)

            def gate_bias(i):
                grouped(dve, f"h{i}")
                V.tensor_tensor(g2[:, i % 2, 512 * (i // 2):512 * (i // 2 + 1)], bank(f"h{i}"),
                                bias2[:, 914 + 512 * (i // 2):914 + 512 * (i // 2 + 1)], ALU.add).then_inc(s_gv, 1)
            gate_bias(0)
            gate_bias(1)
            dve.wait_ge(s_kc, 1)
            link(V.tensor_copy(kcT[:, 0:NC], ps[:, 6, 0:NC]))
            V.tensor_copy(vc[0:NC], ps[0:NC, 7, 0:2 * HD].rearrange("p (g d) -> p g d", g=KVG)).then_inc(s_kce, 1)
            dve.wait_ge(s_gct, 1)
            gcf = gc.rearrange("p t n -> p (t n)")
            link(V.tensor_scalar(gcf, gcf, 0.5, 0.5, ALU.mult, ALU.add))
            dve.wait_ge(s_const2, 16)
            dve.wait_ge(s_cs, 1)
            pf = pcm.rearrange("p a b -> p (a b)")
            for g in range(KVG):
                link(V.tensor_tensor(pf.rearrange("p (t g n) -> p t g n", t=NT, g=KVG)[:, :, g, :],
                                     ps[:, 3 + g, 0:NT * 3 * NC].rearrange("p (t n) -> p t n", t=NT),
                                     const("cbias").rearrange("p (t g n) -> p t g n", t=NT, g=KVG)[:, :, g, :], ALU.add))
            cm, cl = small[:, 420:432], small[:, 432:444]
            m3 = cm.rearrange("p (a o) -> p a o", o=1)
            link(V.tensor_reduce(m3, pcm, AX.X, ALU.max))
            V.tensor_tensor(pcm, pcm, m3.to_broadcast([P, NT * NSAH, NC]), ALU.subtract).then_inc(s_ce, 1)
            gate_bias(2)
            gate_bias(3)
            dve.wait_ge(s_cx, 1)
            link(V.tensor_tensor(pf, pf, const("cmask"), ALU.mult))
            link(V.tensor_reduce(cl.rearrange("p (a o) -> p a o", o=1), pcm, AX.X, ALU.add))
            link(V.tensor_scalar(cl, cl, TINY, None, ALU.max))
            link(V.reciprocal(cl, cl))
            link(V.tensor_tensor(cl.rearrange("p (t h) -> p t h", t=NT), cl.rearrange("p (t h) -> p t h", t=NT),
                                 gc[:, :, 0:3 * NSAH:3], ALU.mult))
            V.tensor_tensor(pcm, pcm, cl.rearrange("p (a o) -> p a o", o=1).to_broadcast([P, NT * NSAH, NC]), ALU.mult
                            ).then_inc(s_cp, 1)

            def bias2_tile(kind, g, h):
                if kind == "fox":
                    return const("causal"), 1.0
                if kind == "dil":
                    return const("dil", g * SPAN, (g + 1) * SPAN), DIL_SLOPE[h]
                return const("dist"), NSA_SLOPE[h]

            attention(UNITS2, AH, AH, None, bias2_tile,
                      lambda u: [gate_bias(HM + u // 2 - 1 + k) for k in range(2)] if u % 4 == 3 and u < 16 else None)

            for i in range(3):
                for half in range(2):
                    for t in range(NT):
                        dve.wait_ge(s_br, 8 + 4 * i + 2 * half + t + 1)
                        if i == 0:
                            dve.wait_ge(s_ggu, 12)
                        cs = slice(512 * half, 512 * (half + 1))
                        gsl = g2[:, t, i * D + 512 * half:i * D + 512 * (half + 1)]
                        p = ps[:, 4 * (i % 2) + 2 * half + t, :]
                        if i == 0:
                            V.scalar_tensor_tensor(merged2[:, t, cs], gsl, 1.0, p, ALU.add, ALU.mult
                                                   ).then_inc(s_gv, 1)
                        else:
                            link(V.scalar_tensor_tensor(gsl, gsl, 1.0, p, ALU.add, ALU.mult))
                            ins = V.tensor_tensor(merged2[:, t, cs], merged2[:, t, cs], gsl, ALU.add)
                            if i == 1:
                                link(ins)
                            else:
                                ins.then_inc(s_mrg, 1)
            pairs_low(s_mT, 4, hTh2, hTl, s_ml)
            for half in range(2):
                for t in range(NT):
                    dve.wait_ge(s_pr, 4 + 2 * half + t + 1)
                    cs = slice(512 * half, 512 * (half + 1))
                    V.scalar_tensor_tensor(xs[:, t, cs], ps[:, 4 + 2 * half + t, :], 0.5, xs[:, t, cs], ALU.mult,
                                           ALU.add).then_inc(s_x1, 1)
            norm_rows(3)
            hT_half(3, v("g4"), None)
            split_tokens(3, hTs[:, 0], hTs[:, 1])

            cw = v("conv2").rearrange("p (f n) -> p f n", n=4)

            def feed(i, b, low):
                dve.wait_ge(s_gate, NE + 2 * i + b + 1)
                acc, z, th = ft[:, b, :], ft[:, 3, :], tmp[:, 0, :]
                for k in range(3):
                    for f in range(2):
                        src = ps[:, 4 + 2 * b, f * T:(f + 1) * T]
                        par = cw[:, bass.ds(4 * i + 2 * b + f, 1), :].rearrange("p a n -> p (a n)")
                        d = acc[:, f * T:(f + 1) * T]
                        if k == 0:
                            ins = V.tensor_scalar(d, src, par[:, 2:3], par[:, 3:4], ALU.mult, ALU.add)
                        else:
                            ins = V.scalar_tensor_tensor(d[:, k:T], src[:, 0:T - k], par[:, 2 - k:3 - k], d[:, k:T],
                                                         ALU.mult, ALU.add)
                        if f == 0:
                            link.later(ins)
                        elif k < 2:
                            link(ins)
                ins.then_inc(s_fsq, 1)
                dve.wait_ge(s_fz, 2 * i + b + 1)
                link(V.tensor_scalar(z, ft[:, 2, :], 0.044715, 1.0, ALU.mult, ALU.add))
                V.tensor_tensor(z, z, acc, ALU.mult).then_inc(s_fth, 1)
                low()
                dve.wait_ge(s_ffn, 2 * i + b + 1)
                link(V.scalar_tensor_tensor(z, th, 1.0, acc, ALU.add, ALU.mult))
                dve.wait_ge(s_gup, NE + 2 * i + b + 1)
                V.tensor_tensor(z, z, ps[:, 5 + 2 * b, :], ALU.mult).then_inc(s_a2, 1)
                dve.wait_ge(s_a2, NE + 2 * i + b + 2)
                split_act(z, b, 2 * i + b, DN2)

            stream(feed, 16, len(ALL), NE, FP)
            dve.wait_ge(s_dnp, DN2 + FP)
            for t in range(NT):
                for half in range(2):
                    cs = slice(512 * half, 512 * (half + 1))
                    V.scalar_tensor_tensor(xs[:, t, cs], ps[:, 2 * t + half, :], 0.5, xs[:, t, cs], ALU.mult, ALU.add
                                           ).then_inc(s_x1, 1)
            final_norm(1, hn)


def constants():
    c = np.zeros((P, NCONST), np.float32)

    def put(name, value):
        lo, hi = CONST[name]
        c[:, lo:hi] = np.asarray(value, np.float32).reshape(-1, hi - lo)

    put("ident", np.eye(P))
    put("ones", np.ones((P, P)))
    p = np.arange(P)
    put("tri", p[:, None] <= p[None, :])
    inv = np.float32(1.0) / (np.float32(10000.0) ** (np.arange(0, ROPE, 2, dtype=np.float32) / np.float32(ROPE)))
    ang = (np.arange(T, dtype=np.float32)[:, None] * inv[None, :]).T.astype(np.float32)
    put("cos", np.tile(np.cos(ang), (4, 1)))
    put("sin", np.concatenate([-np.sin(ang), np.sin(ang)] * 2, 0))
    q = np.concatenate([np.repeat(p[:, None], P, 1), np.repeat(P + p[:, None], T, 1)], 1)
    k = np.concatenate([np.repeat(p[None, :], P, 0), np.repeat(np.arange(T)[None, :], P, 0)], 1)
    put("chunk", np.where(k // 64 <= q // 64, 0.0, NEG))
    d = q - k
    put("causal", np.where(d >= 0, 0.0, NEG))
    put("dist", np.where(d >= 0, -d, NEG))
    put("dil", np.concatenate([np.where((d >= 0) & (d <= w) & (d % r == 0), -d, NEG)
                               for w, r in zip(DILW, DILR)], 1))
    end = np.arange(NC) * CS + CB - 1
    tok = (np.arange(NT)[None, :] * P + p[:, None])[:, :, None, None]
    seen = np.broadcast_to(end <= tok, (P, NT, NSAH, NC))
    slope = np.float32(NSA_SLOPE)[None, None, :, None]
    put("cbias", np.where(seen, -slope * (tok - end).astype(np.float32), np.float32(NEG)))
    put("cmask", seen)
    put("rank4", np.arange(NG, 0, -1)[None, :])
    put("rank8", np.arange(EG, 0, -1)[None, :])
    return c


def kernel(**inputs):
    import concourse.bacc as bacc
    from concourse.bass_utils import run_bass_kernel_spmd

    a = {k: np.asarray(x) for k, x in inputs.items()}

    def chunks(w):
        w = np.asarray(w)
        return w.reshape(w.shape[0] // P, P, -1).transpose(1, 0, 2)

    def flat(w):
        return chunks(w).reshape(P, -1)

    w1 = a["w_in"][0]
    o = np.cumsum([0, 512, 512, 1024, 1024, 4, 4, 384, 256, 64, 2048])
    qm, km, vm, om, im, fm, cq, ckv, kr, gp = (w1[:, o[i]:o[i + 1]] for i in range(10))
    uq = a["w_uq"][0].reshape(QL, AH, NOPE + ROPE)
    ukv = a["w_ukv"][0].reshape(KVL, AH, NOPE + VH)
    tiles = {"cq": np.concatenate([cq, im, fm], 1), "ckr": np.concatenate([ckv, kr, kr], 1), "qk0": qm, "qk1": km,
             "uqn": uq[:, :, :NOPE].reshape(QL, -1), "uqr": uq[:, :, NOPE:].reshape(QL, -1),
             "ukv": np.concatenate([ukv[:, :, :NOPE].reshape(KVL, -1), ukv[:, :, NOPE:].reshape(KVL, -1)], 1)}

    def halves(name, w):
        for i in range(w.shape[1] // 512):
            tiles[f"{name}{i}"] = w[:, 512 * i:512 * (i + 1)]

    for name, w in (("v", vm), ("o", om), ("g", gp), ("bm", a["w_branch_m"][0]), ("ba", a["w_branch_a"][0]),
                    ("out", a["w_out"][0])):
        halves(name, w)
    wa = np.ascontiguousarray(np.concatenate([flat(tiles[n]) for n, _, _ in LOADS], 1))

    w2, b2 = a["w_in_2"][0], a["b_in_2"][0]
    o2 = np.cumsum([0, 256, 256, 256, 4, 384, 384, 384, 384, 128, 128, 128, 128, 128, 128, 18, 3072])
    names = ("qa", "ka", "va", "fa", "qb", "kb", "vb", "qc", "kc", "vc", "ksl", "vsl", "kwn", "vwn", "gc", "gates")
    c2 = {n: w2[:, o2[i]:o2[i + 1]] for i, n in enumerate(names)}
    d2 = {n: b2[o2[i]:o2[i + 1]] for i, n in enumerate(names)}

    def pairs(w):
        return w.reshape(*w.shape[:-1], KVG, 3, HD).swapaxes(-3, -2).reshape(*w.shape)

    tiles.update({"fox": np.concatenate([c2["qa"], c2["ka"]], 1), "dilq": c2["qb"], "dilk": c2["kb"],
                  "nsaq": pairs(c2["qc"]), "kcvw": np.concatenate([c2["kc"], c2["vc"]], 1),
                  "kk": np.concatenate([c2["ksl"], c2["kwn"], c2["gc"], c2["fa"]], 1),
                  "vv": np.concatenate([c2["va"], c2["vsl"], c2["vwn"]], 1), "vb": c2["vb"],
                  "ck": a["cmp_k_w1_2"][0], "cv": a["cmp_v_w1_2"][0]})
    pc = a["w_pc_2"][0].reshape(KVG, 3, HD, D).swapaxes(0, 1).reshape(-1, D)
    for name, w in (("h", c2["gates"]), ("pa", a["w_pa_2"][0]), ("pb", a["w_pb_2"][0]), ("pc", pc),
                    ("wo", a["w_o_2"][0])):
        halves(name, w)
    wb = np.ascontiguousarray(np.concatenate([flat(tiles[n]) for n, _, _ in LOADS2 + LOADS3], 1))

    def triple(gate, up, dn):
        n = gate.shape[0]
        gu = [w.reshape(n, KD, P, DE).transpose(0, 2, 1, 3).reshape(n, P, -1) for w in (gate, up)]
        dn = dn.reshape(n, 2, P, D).transpose(0, 2, 1, 3).reshape(n, P, -1)
        return np.ascontiguousarray(np.concatenate(gu + [dn], 2))

    experts = triple(a["w_expert_gate"][0], a["w_expert_up"][0], a["w_expert_down"][0])
    up = a["w_up_2"][0]
    ffn = triple(up[:, :DFF].reshape(D, FP, DE).swapaxes(0, 1), up[:, DFF:].reshape(D, FP, DE).swapaxes(0, 1),
                 a["w_down_2"][0].reshape(FP, DE, D))
    mod = np.ascontiguousarray(a["mod_w"][0].reshape(KD, P, 12, 512).transpose(2, 1, 0, 3).reshape(12, P, -1))

    vecs = np.zeros((P, NVEC), np.float32)

    def put(name, value, rows=P):
        lo, hi = VEC[name]
        vecs[:rows, lo:hi] = np.asarray(value).reshape(rows, hi - lo)

    def col(x):
        return np.asarray(x).reshape(-1, P).T

    mb = a["mod_b"][0]
    put("c", col(a["c"][0]))
    put("mod1", col(mb[:2048]))
    put("mod2", col(mb[3072:5120]))
    for name, key in (("g1", "norm1_g"), ("g2", "norm2_g"), ("g3", "norm1_g_2"), ("g4", "norm2_g_2"),
                      ("convb", "conv_b"), ("qg", "q_norm_g"), ("kvg", "kv_norm_g")):
        put(name, col(a[key][0]))
    put("convw", a["conv_w"][0].reshape(CONV, 8, P).transpose(2, 1, 0))
    put("ib", a["igate_b"][0], MH)
    put("fb", a["fgate_b"][0], MH)
    put("b2f", col(np.concatenate([d2["qa"], d2["ka"], d2["qb"], d2["kb"], pairs(d2["qc"]), d2["kc"], d2["vc"],
                                   d2["ksl"], d2["kwn"]])))
    put("fab", d2["fa"], FOXH)
    put("conv2", np.concatenate([a["conv_w_2"][0], a["conv_b_2"]], 0).reshape(4, FB, P).transpose(2, 1, 0))
    put("pe", a["cmp_pe_2"][0].reshape(CB // 2, P).T)
    put("w2k", flat(a["cmp_k_w2_2"][0]))
    put("w2v", flat(a["cmp_v_w2_2"][0]))
    put("router", flat(np.concatenate([a["w_group"][0], a["w_router"][0]], 1)))
    rows = np.concatenate([mb[2048:3072], mb[5120:], a["final_norm_g"], a["final_g_2"], a["b_group"][0],
                           a["b_router"][0], d2["va"], d2["vsl"], d2["vwn"], d2["vb"], d2["gc"], d2["gates"]])[None, :]
    assert rows.shape[1] == NROW

    arrays = {"x": np.ascontiguousarray(a["x"]), "consts": constants(), "vecs": vecs,
              "rows": np.ascontiguousarray(rows), "mod": mod, "wa": wa, "experts": experts, "wb": wb, "ffn": ffn}
    nc = bacc.Bacc("TRN2", target_bir_lowering=False, num_devices=1)
    args = [nc.dram_tensor(f"in_{k}_dram", v.shape, F32, kind="ExternalInput").ap() for k, v in arrays.items()]
    out = nc.dram_tensor("out_dram", (1, T, D), F32, kind="ExternalOutput").ap()
    routing = nc.dram_tensor("routing_dram", (NE, T), F32).ap()
    build(nc, routing, *args, out)
    r = run_bass_kernel_spmd(nc, [{f"in_{k}_dram": v for k, v in arrays.items()}], core_ids=[0])
    return r.results[0]["out_dram"]
```
